# Optimizing a Trainium2 kernel written in Bass

```python
import math
import jax, jax.numpy as jnp
from jax import lax
import numpy as np

D_MODEL = 1024
BATCH = 1
SEQ = 1024
DEPTH = 1
DEC_BATCH = 1
DEC_SEQ = 64
PAST_LEN = 256

CHUNK = 64
QBLOCK = 128
ROPE_THETA = 500000.0
MLA_HEADS = 8
MLA_NOPE = 64
MLA_ROPE = 32
MLA_V = 64
MLA_Q_RANK = 256
MLA_KV_RANK = 256
MLA_SCALE = (MLA_NOPE + MLA_ROPE) ** -0.5
DIFF_HEADS = 4
DIFF_D = 64
DIFF_V = 2 * DIFF_D
DIFF_ROT = DIFF_D // 4
DIFF_SCALE = DIFF_D ** -0.5
MIX_WIDTH = MLA_HEADS * MLA_V + DIFF_HEADS * DIFF_V
IN_SPLITS = (MLA_Q_RANK,
             MLA_Q_RANK + MLA_KV_RANK,
             MLA_Q_RANK + MLA_KV_RANK + MLA_ROPE,
             MLA_Q_RANK + MLA_KV_RANK + MLA_ROPE + DIFF_HEADS * 2 * DIFF_D,
             MLA_Q_RANK + MLA_KV_RANK + MLA_ROPE + 2 * DIFF_HEADS * 2 * DIFF_D)
IN_COLS = MLA_Q_RANK + MLA_KV_RANK + MLA_ROPE + 2 * DIFF_HEADS * 2 * DIFF_D + DIFF_HEADS * DIFF_V
N_GROUPS = 4
EXP_PER_GROUP = 8
N_EXPERTS = N_GROUPS * EXP_PER_GROUP
TOP_K = 2
D_EXPERT = 256
ALPHA = (2.0 * DEPTH) ** 0.25
BETA = (8.0 * DEPTH) ** -0.25
EPS_LN = 1e-5
EPS_RMS = 1e-6

kernel_name = 'hymba_mla_diffattn_hmoe_deepnorm_step'

def layer_norm(x, g, b):
    xf = x.astype(jnp.float32)
    mu = jnp.mean(xf, -1, keepdims=True)
    var = jnp.mean(jnp.square(xf - mu), -1, keepdims=True)
    return ((xf - mu) * lax.rsqrt(var + EPS_LN) * g + b).astype(x.dtype)

def rms_norm(x, g):
    xf = x.astype(jnp.float32)
    return (xf * lax.rsqrt(jnp.mean(xf * xf, -1, keepdims=True) + EPS_RMS) * g).astype(x.dtype)

def rope(x, pos):
    r = x.shape[-1]
    inv = ROPE_THETA ** (-jnp.arange(0, r, 2, dtype=jnp.float32) / r)
    ang = pos.astype(jnp.float32)[:, None] * inv
    ang = ang.reshape(ang.shape[0], *([1] * (x.ndim - 3)), r // 2)
    cos, sin = jnp.cos(ang), jnp.sin(ang)
    x1 = x[..., : r // 2].astype(jnp.float32)
    x2 = x[..., r // 2:].astype(jnp.float32)
    return jnp.concatenate([x1 * cos - x2 * sin, x1 * sin + x2 * cos], -1).astype(x.dtype)

def partial_rope(x, pos):
    return jnp.concatenate([rope(x[..., :DIFF_ROT], pos), x[..., DIFF_ROT:]], -1)

def token_projections(x, pos, w_in, q_norm, w_uq, kv_norm):
    B, S, _ = x.shape
    z = jnp.einsum('bsd,dc->bsc', x, w_in)
    c_q, c_kv, k_r, dq, dk, dv = jnp.split(z, IN_SPLITS, axis=-1)
    q = jnp.einsum('bsr,rc->bsc', rms_norm(c_q, q_norm), w_uq).reshape(B, S, MLA_HEADS, MLA_NOPE + MLA_ROPE)
    q_nope = q[..., :MLA_NOPE]
    q_pe = rope(q[..., MLA_NOPE:], pos)
    ckv = rms_norm(c_kv, kv_norm)
    kpe = rope(k_r, pos)
    dq = partial_rope(dq.reshape(B, S, DIFF_HEADS, 2, DIFF_D), pos)
    dk = partial_rope(dk.reshape(B, S, DIFF_HEADS, 2, DIFF_D), pos)
    dv = dv.reshape(B, S, DIFF_HEADS, DIFF_V)
    return q_nope, q_pe, ckv, kpe, dq, dk, dv

def mla_expand(ckv, w_ukv):
    B, K, _ = ckv.shape
    kv = jnp.einsum('bkr,rc->bkc', ckv, w_ukv).reshape(B, K, MLA_HEADS, MLA_NOPE + MLA_V)
    return kv[..., :MLA_NOPE], kv[..., MLA_NOPE:]

def mla_core(q_nope, q_pe, k_nope, k_pe, v, mask):
    s = (jnp.einsum('bqhd,bkhd->bhqk', q_nope, k_nope)
         + jnp.einsum('bqhr,bkr->bhqk', q_pe, k_pe)).astype(jnp.float32) * MLA_SCALE
    if mask is not None:
        s = jnp.where(mask, s, -jnp.inf)
    p = jax.nn.softmax(s, axis=-1).astype(v.dtype)
    return jnp.einsum('bhqk,bkhd->bqhd', p, v)

def diff_core(q, k, v, lam, mask):
    s = jnp.einsum('bqhcd,bkhcd->bchqk', q, k).astype(jnp.float32) * DIFF_SCALE
    if mask is not None:
        s = jnp.where(mask, s, -jnp.inf)
    p = jax.nn.softmax(s, axis=-1)
    a = (p[:, 0] - lam * p[:, 1]).astype(v.dtype)
    return jnp.einsum('bhqk,bkhe->bqhe', a, v)

def diff_lambda(lq1, lk1, lq2, lk2, lam_init):
    f32 = jnp.float32
    return (jnp.exp(jnp.sum(lq1.astype(f32) * lk1.astype(f32)))
            - jnp.exp(jnp.sum(lq2.astype(f32) * lk2.astype(f32))) + lam_init)

def prompt_blocks(core, q_args):
    B, S = q_args[0].shape[:2]
    nblk = S // QBLOCK
    key_chunk = jnp.arange(S) // CHUNK

    def split(a):
        return jnp.moveaxis(a.reshape(B, nblk, QBLOCK, *a.shape[2:]), 1, 0)

    def body(args):
        i, qs = args
        q_chunk = (i * QBLOCK + jnp.arange(QBLOCK)) // CHUNK
        mask = key_chunk[None, :] <= q_chunk[:, None]
        return core(*qs, mask)

    out = lax.map(body, (jnp.arange(nblk), tuple(split(a) for a in q_args)))
    return jnp.moveaxis(out, 0, 1).reshape(B, S, *out.shape[3:])

def hier_moe(h, w_rg, b_rg, w_re, b_re, w_g, w_u, w_d):
    shp = h.shape
    t = h.reshape(-1, shp[-1])
    g_logit = (t @ w_rg + b_rg).astype(jnp.float32)
    g_prob = jax.nn.softmax(g_logit, axis=-1)
    g_idx = jnp.argmax(g_logit, axis=-1)
    g_w = jnp.take_along_axis(g_prob, g_idx[:, None], axis=-1)
    e_logit = (t @ w_re + b_re).astype(jnp.float32).reshape(-1, N_GROUPS, EXP_PER_GROUP)
    e_in = jnp.take_along_axis(e_logit, g_idx[:, None, None], axis=1)[:, 0]
    e_prob = jax.nn.softmax(e_in, axis=-1)
    top_p, top_i = lax.top_k(e_prob, TOP_K)
    top_p = top_p / jnp.sum(top_p, -1, keepdims=True)
    expert_id = g_idx[:, None] * EXP_PER_GROUP + top_i
    gate = jnp.einsum('tk,tke->te', g_w * top_p,
                      jax.nn.one_hot(expert_id, N_EXPERTS, dtype=jnp.float32)).astype(h.dtype)
    hid = jax.nn.silu(jnp.einsum('td,edf->tef', t, w_g)) * jnp.einsum('td,edf->tef', t, w_u)
    y = jnp.einsum('tef,efd->td', hid * gate[..., None], w_d)
    return y.reshape(shp)

def block_output(x, mla_o, diff_o, w_out, ln1_g, ln1_b, ln2_g, ln2_b,
                 w_rg, b_rg, w_re, b_re, w_g, w_u, w_d):
    B, S = x.shape[:2]
    merged = jnp.concatenate([mla_o.reshape(B, S, -1), diff_o.reshape(B, S, -1)], -1)
    a = jnp.einsum('bsm,md->bsd', merged, w_out)
    h = layer_norm(ALPHA * x + a, ln1_g, ln1_b)
    return layer_norm(ALPHA * h + hier_moe(h, w_rg, b_rg, w_re, b_re, w_g, w_u, w_d), ln2_g, ln2_b)

def setup_inputs(seed: int = 0) -> dict:
    key = jax.random.key(seed)
    ks = jax.random.split(key, 32)
    f32 = jnp.float32

    def nrm(k, shape, scale=1.0):
        return jax.random.normal(k, shape, f32) * scale

    in_col_scale = jnp.concatenate([jnp.ones((IN_COLS - DIFF_HEADS * DIFF_V,), f32),
                                    jnp.full((DIFF_HEADS * DIFF_V,), BETA, f32)])
    ukv_col_scale = jnp.tile(jnp.concatenate([jnp.ones((MLA_NOPE,), f32), jnp.full((MLA_V,), BETA, f32)]),
                             MLA_HEADS)
    return {
        'x_prompt': nrm(ks[0], (BATCH, SEQ, D_MODEL)),
        'x_sample': nrm(ks[1], (DEC_BATCH, DEC_SEQ, D_MODEL)),
        'cache_mla_ckv': nrm(ks[2], (DEPTH, DEC_BATCH, PAST_LEN, MLA_KV_RANK)),
        'cache_mla_kpe': nrm(ks[3], (DEPTH, DEC_BATCH, PAST_LEN, MLA_ROPE)),
        'cache_diff_k': nrm(ks[4], (DEPTH, DEC_BATCH, PAST_LEN, DIFF_HEADS, 2 * DIFF_D)),
        'cache_diff_v': nrm(ks[5], (DEPTH, DEC_BATCH, PAST_LEN, DIFF_HEADS, DIFF_V), BETA),
        'w_in': nrm(ks[6], (DEPTH, D_MODEL, IN_COLS), D_MODEL ** -0.5) * in_col_scale,
        'mla_q_norm': 1.0 + nrm(ks[7], (DEPTH, MLA_Q_RANK), 0.02),
        'mla_w_uq': nrm(ks[8], (DEPTH, MLA_Q_RANK, MLA_HEADS * (MLA_NOPE + MLA_ROPE)), MLA_Q_RANK ** -0.5),
        'mla_kv_norm': 1.0 + nrm(ks[9], (DEPTH, MLA_KV_RANK), 0.02),
        'mla_w_ukv': nrm(ks[10], (DEPTH, MLA_KV_RANK, MLA_HEADS * (MLA_NOPE + MLA_V)), MLA_KV_RANK ** -0.5) * ukv_col_scale,
        'diff_lambda_q1': nrm(ks[11], (DEPTH, DIFF_D), 0.1),
        'diff_lambda_k1': nrm(ks[12], (DEPTH, DIFF_D), 0.1),
        'diff_lambda_q2': nrm(ks[13], (DEPTH, DIFF_D), 0.1),
        'diff_lambda_k2': nrm(ks[14], (DEPTH, DIFF_D), 0.1),
        'diff_subln': 1.0 + nrm(ks[15], (DEPTH, DIFF_V), 0.02),
        'w_out': nrm(ks[16], (DEPTH, MIX_WIDTH, D_MODEL), MIX_WIDTH ** -0.5 * BETA),
        'ln1_g': 1.0 + nrm(ks[17], (DEPTH, D_MODEL), 0.02),
        'ln1_b': nrm(ks[18], (DEPTH, D_MODEL), 0.02),
        'ln2_g': 1.0 + nrm(ks[19], (DEPTH, D_MODEL), 0.02),
        'ln2_b': nrm(ks[20], (DEPTH, D_MODEL), 0.02),
        'w_route_group': nrm(ks[21], (DEPTH, D_MODEL, N_GROUPS), D_MODEL ** -0.5),
        'b_route_group': nrm(ks[22], (DEPTH, N_GROUPS), 0.01),
        'w_route_expert': nrm(ks[23], (DEPTH, D_MODEL, N_EXPERTS), D_MODEL ** -0.5),
        'b_route_expert': nrm(ks[24], (DEPTH, N_EXPERTS), 0.01),
        'w_exp_gate': nrm(ks[25], (DEPTH, N_EXPERTS, D_MODEL, D_EXPERT), D_MODEL ** -0.5 * BETA),
        'w_exp_up': nrm(ks[26], (DEPTH, N_EXPERTS, D_MODEL, D_EXPERT), D_MODEL ** -0.5 * BETA),
        'w_exp_down': nrm(ks[27], (DEPTH, N_EXPERTS, D_EXPERT, D_MODEL), D_EXPERT ** -0.5 * BETA),
    }

def reference(x_prompt, x_sample, cache_mla_ckv, cache_mla_kpe, cache_diff_k, cache_diff_v,
              w_in, mla_q_norm, mla_w_uq, mla_kv_norm, mla_w_ukv,
              diff_lambda_q1, diff_lambda_k1, diff_lambda_q2, diff_lambda_k2, diff_subln,
              w_out, ln1_g, ln1_b, ln2_g, ln2_b,
              w_route_group, b_route_group, w_route_expert, b_route_expert,
              w_exp_gate, w_exp_up, w_exp_down):
    pos_p = jnp.arange(SEQ)
    pos_s = PAST_LEN + jnp.arange(x_sample.shape[1])
    hp, hs = x_prompt, x_sample
    ckv_p_l, kpe_p_l, dk_p_l, dv_p_l = [], [], [], []
    ckv_s_l, kpe_s_l, dk_s_l, dv_s_l = [], [], [], []
    for l in range(DEPTH):
        lam_init = 0.8 - 0.6 * math.exp(-0.3 * l)
        lam = diff_lambda(diff_lambda_q1[l], diff_lambda_k1[l], diff_lambda_q2[l], diff_lambda_k2[l], lam_init)
        out_args = (w_out[l], ln1_g[l], ln1_b[l], ln2_g[l], ln2_b[l],
                    w_route_group[l], b_route_group[l], w_route_expert[l], b_route_expert[l],
                    w_exp_gate[l], w_exp_up[l], w_exp_down[l])

        qn, qp, ckv, kpe, dq, dk, dv = token_projections(hp, pos_p, w_in[l], mla_q_norm[l], mla_w_uq[l], mla_kv_norm[l])
        kn, vm = mla_expand(ckv, mla_w_ukv[l])
        mla_o = prompt_blocks(lambda a, b_, m: mla_core(a, b_, kn, kpe, vm, m), (qn, qp))
        diff_o = prompt_blocks(lambda a, m: diff_core(a, dk, dv, lam, m), (dq,))
        diff_o = rms_norm(diff_o, diff_subln[l]) * (1.0 - lam_init)
        ckv_p_l.append(ckv)
        kpe_p_l.append(kpe)
        dk_p_l.append(dk.reshape(*dk.shape[:3], 2 * DIFF_D))
        dv_p_l.append(dv)
        hp = block_output(hp, mla_o, diff_o, *out_args)

        qn_s, qp_s, ckv_s, kpe_s, dq_s, dk_s, dv_s = token_projections(hs, pos_s, w_in[l], mla_q_norm[l], mla_w_uq[l], mla_kv_norm[l])
        ckv_all = jnp.concatenate([cache_mla_ckv[l], ckv_s], axis=1)
        kpe_all = jnp.concatenate([cache_mla_kpe[l], kpe_s], axis=1)
        kn_all, vm_all = mla_expand(ckv_all, mla_w_ukv[l])
        mla_o_s = mla_core(qn_s, qp_s, kn_all, kpe_all, vm_all, None)
        past_k = cache_diff_k[l]
        dk_all = jnp.concatenate([past_k.reshape(*past_k.shape[:3], 2, DIFF_D), dk_s], axis=1)
        dv_all = jnp.concatenate([cache_diff_v[l], dv_s], axis=1)
        diff_o_s = rms_norm(diff_core(dq_s, dk_all, dv_all, lam, None), diff_subln[l]) * (1.0 - lam_init)
        ckv_s_l.append(ckv_s)
        kpe_s_l.append(kpe_s)
        dk_s_l.append(dk_s.reshape(*dk_s.shape[:3], 2 * DIFF_D))
        dv_s_l.append(dv_s)
        hs = block_output(hs, mla_o_s, diff_o_s, *out_args)

    return (hp, hs,
            jnp.stack(ckv_p_l), jnp.stack(kpe_p_l), jnp.stack(dk_p_l), jnp.stack(dv_p_l),
            jnp.stack(ckv_s_l), jnp.stack(kpe_s_l), jnp.stack(dk_s_l), jnp.stack(dv_s_l))


_drawn_inputs = setup_inputs


def setup_inputs(seed=0):
    import zlib

    import numpy as np

    out = dict(_drawn_inputs(seed))
    spreads = {}
    factors = {'cache_mla_ckv': 3.377,
     'cache_mla_kpe': 6.285,
     'mla_q_norm': 8.0,
     'mla_w_uq': 2.899,
     'mla_kv_norm': 2.714,
     'diff_lambda_k1': 3.471,
     'diff_lambda_q2': 3.296,
     'diff_lambda_k2': 4.925,
     'diff_subln': 8.0,
     'ln1_g': 2.767,
     'ln1_b': 2.847,
     'ln2_g': 8.051,
     'ln2_b': 8.373,
     'b_route_group': 8.0,
     'b_route_expert': 25.051}
    for name, (base, spread) in spreads.items():
        noise = np.random.default_rng([zlib.crc32(name.encode()), seed]).standard_normal(out[name].shape)
        drawn = base * np.exp(spread * noise) if base else spread * noise
        out[name] = __import__('jax').numpy.asarray(drawn.astype(out[name].dtype))
    for name, factor in factors.items():
        out[name] = (out[name] * factor).astype(out[name].dtype)
    return out
```

```python
from contextlib import ExitStack

import concourse.bass as bass
import numpy as np
from concourse import mybir

F32 = mybir.dt.float32
U32 = mybir.dt.uint32
I32 = mybir.dt.int32
ALU = mybir.AluOpType
ACT = mybir.ActivationFunctionType
AX = mybir.AxisListType

P = 128
D = 1024
KD = D // P
SEQ, DEC, PAST = 1024, 64, 256
NT = SEQ // P
TOK = SEQ + DEC
KEYS = SEQ + PAST + DEC
QR = KVR = 256
ROPE = 32
NOPE = 64
HM, QD, VM = 8, NOPE + ROPE, 64
HD, DD, VD, ROT = 4, 64, 128, 16
IN_COLS = QR + KVR + ROPE + 3 * HD * 2 * DD
ZC = [(0, 512), (512, 32), (544, 512), (1056, 512), (1568, 512)]
MLA_SCALE = float(QD) ** -0.5
DIFF_SCALE = float(DD) ** -0.5
LAM_INIT = 0.8 - 0.6
ALPHA = 2.0 ** 0.25
EPS_LN, EPS_RMS = 1e-5, 1e-6
NG, EPG = 4, 8
NE = NG * EPG
FE = 256
NEG = -3.0e38
SLOTS = 4
SWEEPS = 9
PAD = 65535

C_ID, C_TRI, C_ONE, C_IOTA, C_DESC, C_TOK, C_HALF, C_THR = 0, 128, 256, 384, 416, 424, 433, 442
C_N = 450
ROPE_N = 2 * (ROPE // 2 + ROT // 2)


class Chain:

    def __init__(self, eng, sem):
        self.eng, self.sem, self.base, self.n = eng, sem, 0, 0

    def inc(self, ins):
        ins.then_inc(self.sem, 1)
        self.n += 1

    def wait(self):
        self.eng.wait_ge(self.sem, self.base + self.n)

    def __call__(self, ins):
        self.inc(ins)
        self.wait()

    def enter(self, i, per):
        self.start, self.per = self.base + self.n, per
        self.base, self.n = self.start + i * per, 0

    def leave(self, trips):
        assert self.n == self.per, self.n
        self.base, self.n = self.start + trips * self.per, 0


def is_tile(t, last):
    return not isinstance(t, int) or 0 <= t <= last


def rows_of(t):
    return DEC if isinstance(t, int) and t == NT else P


def need(eng, sem, value):
    if not isinstance(value, int) or value > 0:
        eng.wait_ge(sem, value)


def build(nc, a, out):
    with ExitStack() as ctx:
        def dram(name, shape, dt=F32):
            return nc.dram_tensor(name, shape, dt, kind="Internal").ap()

        def sem(name):
            return ctx.enter_context(nc.semaphore(name))

        qT_d, kT_d = dram("qT_d", [HM, QD, TOK]), dram("kT_d", [HM, QD, KEYS])
        dqT_d, dkT_d = dram("dqT_d", [HD, P, TOK]), dram("dkT_d", [HD, P, KEYS])
        v_d = dram("v_d", [KEYS, HM * VM])
        h_d, pair_d = dram("h_d", [TOK, D]), dram("pair_d", [2 * TOK, D])
        list_d = dram("list_d", [SWEEPS * P, NE, 4], U32)

        top = [(nc.sbuf_base + 63) // 64 * 64]

        def place(at, name, shape, dt=F32):
            size = int(np.prod(shape[1:])) * 4
            t = nc.alloc_sbuf_tensor_at(name, shape, dt, offset=at[0])
            at[0] += (size + 31) // 32 * 32
            assert at[0] <= nc.sbuf_usable_end, (name, at[0])
            return t

        const = place(top, "const", [P, C_N])
        wgu, wdn = [None] * SLOTS, [None] * SLOTS
        for s in range(2):
            wgu[s] = place(top, f"wgu{s}", [P, KD, 2 * FE])
            wdn[s] = place(top, f"wdn{s}", [P, FE // P, D])
        neglam = place(top, "neglam", [P, 1])
        region = top[0]

        m1 = [region]
        w_in = place(m1, "w_in_sb", [P, KD, IN_COLS])
        w_uq = place(m1, "w_uq_sb", [P, 2, HM * QD])
        w_ukv = place(m1, "w_ukv_sb", [P, 2, 2, HM * NOPE])
        gq, gkv = place(m1, "gq", [P, QR]), place(m1, "gkv", [P, KVR])
        lam4 = place(m1, "lam4", [P, 4, DD])
        lamt = place(m1, "lamt", [P, 2, DD])
        lams = place(m1, "lams", [P, 2])
        lame = place(m1, "lame", [P, 2])
        pad_rows = place(m1, "pad_rows", [P, NE * 4], U32)
        x_in = [place(m1, f"x_in{p}", [P, D]) for p in range(2)]
        rope = [place(m1, f"rope{p}", [P, ROPE_N]) for p in range(2)]
        xT = [place(m1, f"xT{p}", [P, KD, P]) for p in range(2)]
        zqk = [place(m1, f"zqk{p}", [P, 2, 2 * HD, DD]) for p in range(2)]
        zv = [place(m1, f"zv{p}", [P, HD * VD]) for p in range(2)]
        kr = [place(m1, f"kr{p}", [P, ROPE]) for p in range(2)]
        cqn = [place(m1, f"cqn{p}", [P, QR]) for p in range(2)]
        ckvn = [place(m1, f"ckvn{p}", [P, KVR]) for p in range(2)]
        cT = [place(m1, f"cT{p}", [P, 4, P]) for p in range(2)]
        qs = [place(m1, f"qs{p}", [P, HM, QD]) for p in range(2)]
        kpT = [place(m1, f"kpT{p}", [ROPE, P]) for p in range(2)]
        dT = [place(m1, f"dT{p}", [P, 2, HD, P]) for p in range(2)]
        qT = [place(m1, f"qT{p}", [QD, HM, P]) for p in range(2)]
        knT = [place(m1, f"knT{p}", [P, HM // 2, P]) for p in range(2)]
        vs = [place(m1, f"vs{p}", [P, HM * VM]) for p in range(2)]
        junk = place(m1, "junk", [P, 2, QR])
        ss = [place(m1, f"ss{p}", [P, 2]) for p in range(2)]
        ms = [place(m1, f"ms{p}", [P, 2]) for p in range(2)]
        rq = [place(m1, f"rq{p}", [P, 2]) for p in range(2)]
        rt4 = [place(m1, f"rt4{n}", [P, 4, (ROPE // 2, P, P)[n]]) for n in range(3)]

        m2 = [region]
        merged = place(m2, "merged", [P, NT + 1, D])
        m3 = list(m2)
        w_o = place(m3, "w_o_sb", [P, KD, D])
        m4 = list(m3)
        hi = [nc.sbuf_usable_end - (KD * 2 * FE + 2 * D) * 4 - 64]
        hi[0] = hi[0] // 64 * 64
        hi_base = hi[0]
        wgu[2] = place(hi, "wgu2", [P, KD, 2 * FE])
        wdn[2] = place(hi, "wdn2", [P, FE // P, D])
        hq = [place(m3, f"hq{p}", [P, TOK]) for p in range(2)]
        hk = [place(m3, f"hk{p}", [P, KEYS]) for p in range(2)]
        hv = [place(m3, f"hv{p}", [P, 11, VD]) for p in range(2)]
        pr = [[place(m3, f"pr{p}{m}", [P, SEQ]) for m in range(2)] for p in range(2)]
        pT = [place(m3, f"pT{p}", [P, NT, P]) for p in range(2)]
        nmax = [[place(m3, f"nmax{p}{m}", [P, 1]) for m in range(2)] for p in range(2)]
        psums = [[place(m3, f"psums{p}{m}", [P, 1]) for m in range(2)] for p in range(2)]
        rsum = [place(m3, f"rsum{p}", [P, 2]) for p in range(2)]
        mixc = [place(m3, f"mixc{p}", [P, 1]) for p in range(2)]
        assert m3[0] <= hi_base, (m3[0], hi_base)
        xr = [place(m4, f"xr{p}", [P, D]) for p in range(2)]
        mT = [place(m4, f"mT{p}", [P, KD, P]) for p in range(2)]
        r1 = [place(m4, f"r1{p}", [P, D]) for p in range(2)]
        hT = [place(m4, f"hT{p}", [P, KD, P]) for p in range(2)]
        g1b, b1b = place(m4, "g1b", [P, D]), place(m4, "b1b", [P, D])
        subln = place(m4, "subln", [P, VD])
        w_r = place(m4, "w_r_sb", [P, KD, NG + NE])
        b_r = place(m4, "b_r_sb", [P, NG + NE])
        sq = [place(m4, f"sq{p}", [P, HD, VD]) for p in range(2)]
        m4s = [[place(m4, f"{n}{p}", [P, HD]) for n in ("hsq", "hms", "hrs")] for p in range(2)]
        bst = [place(m4, f"bst{p}", [P, 2, 6]) for p in range(2)]
        mv = [place(m4, f"mv{p}", [P, 2]) for p in range(2)]
        ve = [place(m4, f"ve{p}", [P, 1]) for p in range(2)]
        rst = [place(m4, f"rst{p}", [P, 1]) for p in range(2)]
        lg = place(m4, "lg", [P, NG + NE])
        top1 = place(m4, "top1", [P, 8])
        wgt = place(m4, "wgt", [P, 8])
        ohg = place(m4, "ohg", [P, NG])
        ein8 = place(m4, "ein8", [P, 2, EPG])
        emul = place(m4, "emul", [P, NG, EPG])
        ohe = place(m4, "ohe", [P, 2, EPG])
        shifted = [place(m4, f"shifted{p}", [P, 8]) for p in range(2)]
        exped = [place(m4, f"exped{p}", [P, 8]) for p in range(2)]
        oh32 = [place(m4, f"oh32{p}", [P, 2, NE]) for p in range(2)]
        picks = [place(m4, f"picks{p}", [P, NE]) for p in range(2)]
        before = [place(m4, f"before{p}", [P, NE]) for p in range(2)]
        gates = [place(m4, f"gates{p}", [P, 4]) for p in range(2)]
        where = place(m4, "where", [P, NE])
        where2 = place(m4, "where2", [P, 2, NE])
        rowf = place(m4, "rowf", [P, 2])
        row = [place(m4, f"row{p}", [P, 2, 1], U32) for p in range(2)]
        entry = [place(m4, f"entry{p}", [P, 2, 4], U32) for p in range(2)]
        cntm = place(m4, "cntm", [P, 1])
        over = place(m4, "over", [P, 8])
        nover = place(m4, "nover", [P, 1])
        assert m4[0] <= hi_base, (m4[0], hi_base)
        m5 = list(m2)
        wgu[3] = place(m5, "wgu3", [P, KD, 2 * FE])
        wdn[3] = place(m5, "wdn3", [P, FE // P, D])
        m5[0] = max(m5[0], m4[0])
        more = place(m5, "more", [P, 1], I32)
        tab = [place(m5, f"tab{s}", [P, 4], U32) for s in range(SLOTS)]
        m6 = [m2[0] + (KD * 2 * FE + 2 * D) * 4]
        hg = [place(m6, f"hg{p}", [P, D]) for p in range(2)]
        hgT = [place(m6, f"hgT{p}", [P, KD, P]) for p in range(2)]
        sil = [place(m6, f"sil{p}", [P, FE]) for p in range(2)]
        hid = [place(m6, f"hid{p}", [P, FE]) for p in range(2)]
        hidT = [place(m6, f"hidT{p}", [P, 2, P]) for p in range(2)]
        y = [place(m6, f"y{p}", [P, D]) for p in range(2)]
        g2b, b2b = place(m6, "g2b", [P, D]), place(m6, "b2b", [P, D])
        assert m6[0] <= m5[0] or True
        assert m6[0] <= hi_base
        m7 = [nc.sbuf_base // 64 * 64 + 64 + (C_N * 4 + 31) // 32 * 32]
        NF = 3
        y0 = [place(m7, f"y0{p}", [P, D]) for p in range(NF)]
        y1 = [place(m7, f"y1{p}", [P, D]) for p in range(NF)]
        fst = [place(m7, f"fst{p}", [P, 2, 6]) for p in range(NF)]
        fmv = [place(m7, f"fmv{p}", [P, 2]) for p in range(NF)]
        fve = [place(m7, f"fve{p}", [P, 1]) for p in range(NF)]
        frs = [place(m7, f"frs{p}", [P, 1]) for p in range(NF)]
        assert m7[0] <= region

        ps = ctx.enter_context(nc.psum_tensor("ps", [P, 8, 512], F32))
        ident = const[:, C_ID:C_ID + P]

        names = """const_in lam_in lam_prod lam_exp lam_done x_made rope_in wuq_in
            xT_made xT_copied z_made sq_done rms_done norm_done kr_copied dqk_copied dv_copied kr_roped dqk_roped
            cT_made kpT_made dT_made cT_copied kpT_copied dT_copied q_made kn_made v_made q_copied kn_copied
            v_copied q_roped qT_made qT_copied pads_set pads_out
            ch_dve ch_act ch_pool settled
            s_made max_done exp_done mix_done pT_made pT_lo pT_hi o_made o_done
            wo_in ph3_in sub_done sq3_done hsq_done hrs_done md_done mT_made mT_copied op_made res_done ln_stat ln_rstd
            ln_mul h_done hT_made hT_copied lg_made shift_done exp3_done picks_done
            pre_made rows_done cnt_made swp_done before0
            hg_zero hgT_made hgT_copied gu_made silu_done hid_done hidT_made hidT_copied dn_made
            y_lo y_hi add_done fstat frstd fmul fin_done fnorm ln2_in""".split()
        S = {n: sem(n) for n in names}
        x_in_s = [sem(f"x_in_s{p}") for p in range(2)]
        win_s = [sem(f"win_s{c}") for c in range(len(ZC))]
        cache_s = [sem(f"cache_s{p}") for p in range(2)]
        st_s = [sem(f"st_s{p}") for p in range(2)]
        head_s = [sem(f"head_s{p}") for p in range(2)]
        xr_s = [sem(f"xr_s{p}") for p in range(2)]
        h_st = [sem(f"h_st{p}") for p in range(2)]
        ent_s = [sem(f"ent_s{p}") for p in range(2)]
        w_s = [sem(f"w_s{s}") for s in range(SLOTS)]
        tab_s = [sem(f"tab_s{s}") for s in range(SLOTS)]
        hg_s = [sem(f"hg_s{p}") for p in range(2)]
        y_s = [sem(f"y_s{p}") for p in range(2)]
        f_in = [sem(f"f_in{p}") for p in range(NF)]
        f_out = [sem(f"f_out{p}") for p in range(NF)]

        FULL_ST = 16 * 11

        block = ctx.enter_context(nc.Block())

        def settle(eng):
            eng.sem_inc(S["settled"], 1)

        def key_col(t):
            return SEQ + PAST if isinstance(t, int) and t == NT else t * P

        @block.sync
        def _(sp):
            def load_x(t, p):
                need(sp, S["xT_made"], t - 1)
                if not isinstance(t, int) or t >= 2:
                    sp.wait_ge(S["q_roped"], t - 1)
                R = rows_of(t)
                src = a["x_sample"][0] if R == DEC else a["x_prompt"][0, bass.ds(t * P, P), :]
                sp.dma_start(x_in[p][0:R, :], src).then_inc(x_in_s[p], 16)
                sp.dma_start(rope[p][0:R, :], a["rope_table"][bass.ds(t * P, R), :]).then_inc(x_in_s[p], 16)

            def store_early(t, p):
                R, last = rows_of(t), isinstance(t, int) and t == NT

                def row(name):
                    dst = out["new_" + name + ("_s" if last else "_p")][0, 0]
                    return dst if last else dst[bass.ds(t * P, P)]

                sp.wait_ge(S["norm_done"], 1 + t)
                sp.dma_start(row("ckv"), ckvn[p][0:R, :]).then_inc(st_s[p], 16)
                sp.wait_ge(S["kr_roped"], 1 + t)
                sp.dma_start(row("kpe"), kr[p][0:R, :]).then_inc(st_s[p], 16)
                sp.wait_ge(S["dv_copied"], 1 + t)
                sp.dma_start(row("dv").rearrange("t h v -> t (h v)"), zv[p][0:R, :]).then_inc(st_s[p], 16)
                sp.wait_ge(S["dqk_roped"], 1 + t)
                sp.dma_start(row("dk").rearrange("t h v -> t (h v)"),
                             zqk[p][0:R, 1].rearrange("p h d -> p (h d)")).then_inc(st_s[p], 16)

            def store_keys(t, p, R, col):
                sp.wait_ge(S["kpT_copied"], 1 + t)
                src = kpT[p][:, 0:R].unsqueeze(1).broadcast_to([ROPE, HM, R])
                sp.dma_start(kT_d[:, NOPE:QD, bass.ds(col, R)].rearrange("h d k -> d h k"), src).then_inc(st_s[p], 16)
                sp.wait_ge(S["kn_copied"], 1 + t)
                settle(sp)
                for half in range(2):
                    sp.dma_start(kT_d[half::2, 0:NOPE, bass.ds(col, R)].rearrange("h d k -> d h k"),
                                 knT[p][NOPE * half:NOPE * (half + 1), :, 0:R]).then_inc(st_s[p], 16)
                sp.wait_ge(S["v_copied"], 1 + t)
                sp.dma_start(v_d[bass.ds(col, R), :], vs[p][0:R, :]).then_inc(st_s[p], 16)
                sp.wait_ge(S["dT_copied"], 1 + t)
                sp.dma_start(dkT_d[:, :, bass.ds(col, R)].rearrange("h d k -> d h k"),
                             dT[p][:, 1, :, 0:R]).then_inc(st_s[p], 16)

            def store_late(t, p):
                R = rows_of(t)
                store_keys(t, p, R, key_col(t))
                sp.dma_start(dqT_d[:, :, bass.ds(t * P, R)].rearrange("h d k -> d h k"),
                             dT[p][:, 0, :, 0:R]).then_inc(st_s[p], 16)
                sp.wait_ge(S["qT_copied"], 1 + t)
                sp.dma_start(qT_d[:, :, bass.ds(t * P, R)].rearrange("h d k -> d h k"),
                             qT[p][:, :, 0:R]).then_inc(st_s[p], 16)

            def load_expert(s, e):
                sp.dma_start(wgu[s][:, :, 0:FE], a["w_exp_gate"][0, bass.ds(e, 1)].rearrange(
                    "a (k p) f -> p (a k) f", p=P)).then_inc(w_s[s], 16)
                sp.dma_start(wgu[s][:, :, FE:2 * FE], a["w_exp_up"][0, bass.ds(e, 1)].rearrange(
                    "a (k p) f -> p (a k) f", p=P)).then_inc(w_s[s], 16)
                sp.dma_start(wdn[s][:], a["w_exp_down"][0, bass.ds(e, 1)].rearrange(
                    "a (k p) f -> p (a k) f", p=P)).then_inc(w_s[s], 16)

            sp.dma_start(const[:], a["const_table"]).then_inc(S["const_in"], 16)
            load_x(0, 0)
            w3 = a["w_in"][0].rearrange("(k p) c -> p k c", p=P)
            for c, (c0, n) in enumerate(ZC):
                sp.dma_start(w_in[:, :, c0:c0 + n], w3[:, :, c0:c0 + n]).then_inc(win_s[c], 16)
                if c == 0:
                    load_x(1, 1)
                    for dst, name in ((gq, "mla_q_norm"), (gkv, "mla_kv_norm")):
                        sp.dma_start(dst[:], a[name][0].partition_broadcast(P)).then_inc(S["rope_in"], 16)
                if c == 1:
                    sp.dma_start(w_uq[:], a["mla_w_uq"][0].rearrange("(k p) c -> p k c", p=P)).then_inc(S["wuq_in"], 16)
                    for k in range(2):
                        kv = a["mla_w_ukv"][0, k * P:(k + 1) * P].rearrange("p (h x c) -> p x h c", x=2, c=NOPE)
                        for x in range(2):
                            sp.dma_start(w_ukv[:, k, x].rearrange("p (h c) -> p h c", c=NOPE), kv[:, x]).then_inc(S["wuq_in"], 16)
            for n, name in enumerate(("q1", "k1", "q2", "k2")):
                sp.dma_start(lam4[:, n, :], a["diff_lambda_" + name][0].partition_broadcast(P)).then_inc(S["lam_in"], 16)
            sp.wait_ge(S["pads_set"], 1)
            for b in range(SWEEPS):
                sp.dma_start(list_d[b * P:(b + 1) * P].rearrange("p e w -> p (e w)"), pad_rows[:]).then_inc(S["pads_out"], 16)
            for s in range(2):
                load_expert(s, s)

            def body1(t, p):
                if is_tile(t + 1, NT) and not (isinstance(t, int) and t == 0):
                    load_x(t + 1, 1 - p)
                if is_tile(t, NT):
                    store_early(t, p)
                if is_tile(t - 1, NT):
                    store_late(t - 1, 1 - p)

            for t in range(3):
                body1(t, t % 2)
            with sp.Fori(0, 2) as i:
                body1(3 + 2 * i, 1)
                body1(4 + 2 * i, 0)
            body1(7, 1)
            body1(8, 0)
            for c in range(2):
                p, t = 1 - c, NT + 1 + c
                if c == 0:
                    sp.wait_ge(st_s[p], FULL_ST * 4)
                else:
                    store_late(NT, 0)
                    sp.wait_ge(st_s[p], FULL_ST * 5)
                rows = slice(c * P, (c + 1) * P)
                sp.dma_start(ckvn[p][:], a["cache_mla_ckv"][0, 0, rows]).then_inc(cache_s[p], 16)
                sp.dma_start(kr[p][:], a["cache_mla_kpe"][0, 0, rows]).then_inc(cache_s[p], 16)
                sp.dma_start(zqk[p][:, 1].rearrange("p h d -> p (h d)"),
                             a["cache_diff_k"][0, 0, rows].rearrange("t h d -> t (h d)")).then_inc(cache_s[p], 16)
            for c in range(2):
                store_keys(NT + 1 + c, 1 - c, P, SEQ + c * P)

            sp.wait_ge(st_s[1], FULL_ST * 4 + 5 * 16)
            sp.wait_ge(st_s[0], FULL_ST * 5 + 5 * 16)

            def load_mla(h, p):
                need(sp, S["o_made"], 9 * (h - 1))
                sp.dma_start(hq[p][0:QD, :], qT_d[bass.ds(h, 1)].rearrange("a d t -> (a d) t")).then_inc(head_s[p], 16)
                sp.dma_start(hk[p][0:QD, :], kT_d[bass.ds(h, 1)].rearrange("a d t -> (a d) t")).then_inc(head_s[p], 16)
                v = v_d[:, bass.ds(h * VM, VM)]
                sp.dma_start(hv[p][:, 0:10, 0:VM], v[0:10 * P].rearrange("(t p) v -> p t v", p=P)).then_inc(head_s[p], 16)
                sp.dma_start(hv[p][0:DEC, 10, 0:VM], v[10 * P:KEYS]).then_inc(head_s[p], 16)

            def load_diff(h, p):
                sp.wait_ge(S["o_made"], 9 * (HM + h - 1))
                sp.dma_start(hq[p][:], dqT_d[bass.ds(h, 1)].rearrange("a d t -> (a d) t")).then_inc(head_s[p], 16)
                sp.dma_start(hk[p][:], dkT_d[bass.ds(h, 1)].rearrange("a d t -> (a d) t")).then_inc(head_s[p], 16)
                for dst, src in ((hv[p][:, 0:NT, :], out["new_dv_p"]), (hv[p][:, NT:NT + 2, :], a["cache_diff_v"])):
                    sp.dma_start(dst, src[0, 0, :, bass.ds(h, 1), :].rearrange("(t p) a v -> p t (a v)", p=P)).then_inc(head_s[p], 16)
                sp.dma_start(hv[p][0:DEC, 10, :], out["new_dv_s"][0, 0, :, bass.ds(h, 1), :].rearrange("t a v -> t (a v)")).then_inc(head_s[p], 16)

            load_mla(0, 0)
            load_mla(1, 1)
            sp.dma_start(w_o[:], a["w_out"][0].rearrange("(k p) c -> p k c", p=P)).then_inc(S["wo_in"], 16)
            load_expert(2, 2)
            with sp.Fori(1, HM // 2) as i:
                load_mla(2 * i, 0)
                load_mla(2 * i + 1, 1)
            with sp.Fori(0, HD // 2) as i:
                load_diff(2 * i, 0)
                load_diff(2 * i + 1, 1)

            sp.wait_ge(S["o_done"], 9 * (HM + HD))
            sp.dma_start(subln[:], a["diff_subln"][0].partition_broadcast(P)).then_inc(S["ph3_in"], 16)
            for dst, name in ((g1b, "ln1_g"), (b1b, "ln1_b")):
                sp.dma_start(dst[:], a[name][0].partition_broadcast(P)).then_inc(S["ph3_in"], 16)
            sp.dma_start(w_r[:, :, 0:NG], a["w_route_group"][0].rearrange("(k p) c -> p k c", p=P)).then_inc(S["ph3_in"], 16)
            sp.dma_start(w_r[:, :, NG:NG + NE], a["w_route_expert"][0].rearrange("(k p) c -> p k c", p=P)).then_inc(S["ph3_in"], 16)
            sp.dma_start(b_r[:, 0:NG], a["b_route_group"][0].partition_broadcast(P)).then_inc(S["ph3_in"], 16)
            sp.dma_start(b_r[:, NG:NG + NE], a["b_route_expert"][0].partition_broadcast(P)).then_inc(S["ph3_in"], 16)

            def load_xr(t, p):
                need(sp, S["hT_made"], t - 1)
                R = rows_of(t)
                src = a["x_sample"][0] if R == DEC else a["x_prompt"][0, bass.ds(t * P, P), :]
                sp.dma_start(xr[p][0:R, :], src).then_inc(xr_s[p], 16)

            def body3(t, p):
                if is_tile(t + 1, NT):
                    load_xr(t + 1, 1 - p)
                if is_tile(t, NT):
                    R = rows_of(t)
                    sp.wait_ge(S["h_done"], t + 1)
                    sp.dma_start(h_d[bass.ds(t * P, R), :], merged[0:R, bass.ds(t, 1), :].rearrange("p a d -> p (a d)")).then_inc(h_st[p], 16)

            for t in (-1, 0, 1, 2):
                body3(t, t % 2)
            with sp.Fori(0, 2) as i:
                body3(3 + 2 * i, 1)
                body3(4 + 2 * i, 0)
            body3(7, 1)
            body3(8, 0)
            sp.wait_ge(S["op_made"], NT + 1)
            load_expert(3, 3)
            sp.wait_ge(ent_s[0], 32 * 5)
            sp.wait_ge(ent_s[1], 32 * 4)

            def load_list(s, g):
                sweep, e = (0, s) if isinstance(g, int) else (g // (NE // SLOTS), (g % (NE // SLOTS)) * SLOTS + s)
                sp.dma_start(tab[s][:], list_d[bass.ds(sweep * P, P), bass.ds(e, 1), :].rearrange(
                    "p a w -> p (a w)")).then_inc(tab_s[s], 16)

            for s in range(SLOTS):
                load_list(s, 0)
            sp.wait_ge(S["cnt_made"], 1)
            for dst, name in ((g2b, "ln2_g"), (b2b, "ln2_b")):
                sp.wait_ge(S["rows_done"], NT + 1)
                sp.dma_start(dst[:], a[name][0].partition_broadcast(P)).then_inc(S["ln2_in"], 16)
            sp.wait_ge(S["swp_done"], 1)
            n = sp.value_load(more[0:1, 0:1], min_val=0, max_val=SWEEPS - 1) + 1
            with sp.Fori(1, n * (NE // SLOTS)) as g:
                for s in range(SLOTS):
                    e = g * SLOTS + s
                    sp.wait_ge(S["dn_made"], e - SLOTS + 1)
                    load_expert(s, (g % (NE // SLOTS)) * SLOTS + s)
                    sp.wait_ge(y_s[s % 2], (e - SLOTS) // 2 * 16 + 16)
                    load_list(s, g)
            sp.wait_ge(y_s[0], n * (NE // 2) * 16)
            sp.wait_ge(y_s[1], n * (NE // 2) * 16)

            def load_pairs(t, f):
                R = rows_of(t)
                for k, dst in enumerate((y0, y1)):
                    sp.dma_start(dst[f][0:R, :], pair_d[k * TOK + t * P:k * TOK + t * P + R, :]).then_inc(f_in[f], 16)

            for t in range(NF):
                load_pairs(t, t)
            for t in range(NT + 1):
                R = rows_of(t)
                sp.wait_ge(S["fin_done"], t + 1)
                dst = out["y_sample"][0] if t == NT else out["y_prompt"][0, t * P:(t + 1) * P, :]
                sp.dma_start(dst, y0[t % NF][0:R, :]).then_inc(f_out[t % NF], 16)
                if t + NF <= NT:
                    sp.wait_ge(f_out[t % NF], 16 * (t // NF + 1))
                    load_pairs(t + NF, t % NF)
            for f in range(NF):
                sp.wait_ge(f_out[f], 16 * len(range(f, NT + 1, NF)))

        @block.tensor
        def _(pe):
            def turn(bank, col, src, R, n):
                return pe.transpose(ps[0:n, bank, col:col + R], src, const[0:R, C_ID:C_ID + R])

            def xT_of(t, p):
                R = rows_of(t)
                pe.wait_ge(x_in_s[p], (t // 2 + 1) * 32)
                for half in range(2):
                    need(pe, S["kn_copied"] if half == 0 else S["v_copied"], t - 1)
                    for k in range(4):
                        mm = turn(4 + half, k * P, x_in[p][0:R, (4 * half + k) * P:(4 * half + k + 1) * P], R, P)
                mm.then_inc(S["xT_made"], 1)

            def z_of(t, p, c):
                R, (c0, n), bank = rows_of(t), ZC[c], (0, 1, 2, 3, 1)[c]
                if isinstance(t, int) and t == 0:
                    pe.wait_ge(win_s[c], 16)
                if c == 0:
                    pe.wait_ge(S["xT_copied"], t + 1)
                    need(pe, S["norm_done"], t)
                if c == 1:
                    need(pe, S["dv_copied"], t)
                if c == 2 or c == 3:
                    need(pe, S["dqk_copied"], t)
                if c == 4:
                    pe.wait_ge(S["kr_copied"], t + 1)
                for k in range(KD):
                    mm = pe.matmul(ps[0:R, bank, 0:n], xT[p][:, k, 0:R], w_in[:, k, c0:c0 + n],
                                   start=k == 0, stop=k == KD - 1)
                mm.then_inc(S["z_made"], 1)

            def turn_keys(t, p, R, heads):
                pe.wait_ge(S["norm_done"], t + 1) if heads else pe.wait_ge(cache_s[p], 48)
                if isinstance(t, int) and t > NT + 1:
                    pe.wait_ge(S["cT_copied"], t)
                else:
                    need(pe, S["qT_copied"], t)
                for c in range(0 if heads else 2, 4):
                    src = (cqn if c < 2 else ckvn)[p][0:R, (c % 2) * P:(c % 2 + 1) * P]
                    mm = turn(6, c * P, src, R, P)
                mm.then_inc(S["cT_made"], 1)
                if heads:
                    pe.wait_ge(S["kr_roped"], t + 1)
                    need(pe, S["xT_copied"], t + 1)
                    if is_tile(t + 1, NT):
                        pe.wait_ge(S["xT_copied"], t + 2)
                need(pe, S["v_copied"], t)
                turn(5, 0, kr[p][0:R, :], R, ROPE).then_inc(S["kpT_made"], 1)
                if heads:
                    pe.wait_ge(S["dqk_roped"], t + 1)
                need(pe, S["kn_copied"], t)
                for half, bank in ((0, 7), (1, 4)) if heads else ((1, 4),):
                    for h in range(HD):
                        mm = turn(bank, h * P, zqk[p][0:R, half, 2 * h:2 * h + 2, :].rearrange("p a d -> p (a d)"), R, P)
                mm.then_inc(S["dT_made"], 1)

            def expand(t, p, R, heads):
                pe.wait_ge(S["cT_copied"], t + 1)
                if isinstance(t, int) and t == 0:
                    pe.wait_ge(S["wuq_in"], 16 * 5)
                pe.wait_ge(S["dT_copied"], t + 1)
                if heads:
                    for half in range(2):
                        for k in range(2):
                            mm = pe.matmul(ps[0:R, 6 + half, 0:384], cT[p][:, k, 0:R], w_uq[:, k, 384 * half:384 * (half + 1)],
                                           start=k == 0, stop=k == 1)
                    mm.then_inc(S["q_made"], 1)
                for j in range(HM // 2):
                    for k in range(2):
                        mm = pe.matmul(ps[:, 4, j * P:j * P + R], w_ukv[:, k, 0, P * j:P * (j + 1)], cT[p][:, 2 + k, 0:R],
                                       start=k == 0, stop=k == 1)
                mm.then_inc(S["kn_made"], 1)
                pe.wait_ge(S["kpT_copied"], t + 1)
                for k in range(2):
                    mm = pe.matmul(ps[0:R, 5, :], cT[p][:, 2 + k, 0:R], w_ukv[:, k, 1, :],
                                   start=k == 0, stop=k == 1)
                mm.then_inc(S["v_made"], 1)

            def turn_q(t, p):
                R = rows_of(t)
                pe.wait_ge(S["q_roped"], t + 1)
                for h in range(HM):
                    mm = turn(6 + h // 4, (h % 4) * P, qs[p][0:R, h, :], R, QD)
                mm.then_inc(S["qT_made"], 1)

            def body1(t, p):
                cur, prev = is_tile(t, NT), is_tile(t - 1, NT)
                q, R1 = 1 - p, rows_of(t - 1)
                if cur:
                    z_of(t, p, 0)
                    z_of(t, p, 1)
                if prev:
                    turn_keys(t - 1, q, R1, True)
                if cur:
                    z_of(t, p, 2)
                if prev:
                    expand(t - 1, q, R1, True)
                if cur:
                    z_of(t, p, 3)
                    z_of(t, p, 4)
                if prev:
                    turn_q(t - 1, q)
                if is_tile(t + 1, NT):
                    xT_of(t + 1, q)

            pe.wait_ge(S["const_in"], 16)
            xT_of(0, 0)
            for t in range(3):
                body1(t, t % 2)
            with pe.Fori(0, 2) as i:
                body1(3 + 2 * i, 1)
                body1(4 + 2 * i, 0)
            body1(7, 1)
            body1(8, 0)
            body1(9, 1)
            for c in range(2):
                turn_keys(NT + 1 + c, 1 - c, P, False)
                expand(NT + 1 + c, 1 - c, P, False)

            def blocks(i):
                return 3 if i == NT else i + 1

            def scores(h0, i, p, hp, m, maps, s_idx, width):
                R, n0 = rows_of(i), (SEQ if i == NT else 0)
                n = KEYS - SEQ if i == NT else (i + 1) * P
                lo = m * DD
                if i == NT:
                    settle(pe)
                for half in range((n + 511) // 512):
                    c0, c1 = half * 512, min(n, half * 512 + 512)
                    mm = pe.matmul(ps[0:R, 2 * p + half, 0:c1 - c0], hq[hp][lo:lo + width, i * P:i * P + R],
                                   hk[hp][lo:lo + width, n0 + c0:n0 + c1], start=True, stop=True)
                mm.then_inc(S["s_made"], 1)

            def turn_p(c0, u, i, p):
                R, nb = rows_of(i), blocks(i)
                for half in range((nb + 3) // 4):
                    if half == 0:
                        need(pe, S["pT_lo"], u)
                    else:
                        hi_before = max(0, i - 4)
                        need(pe, S["pT_hi"], (u - i) // 9 * 4 + hi_before)
                    if i == NT:
                        settle(pe)
                    for b in range(4 * half, min(nb, 4 * half + 4)):
                        w = DEC if i == NT and b == 2 else P
                        mm = turn(4 + half, (b % 4) * P, pr[p][0][0:R, b * P:b * P + w], R, w)
                    mm.then_inc(S["pT_made"], 1)

            def values(u, free, i, p, hp, V):
                R, nb = rows_of(i), blocks(i)
                need(pe, S["o_done"], free)
                pe.wait_ge(S["pT_lo"], u + 1)
                if nb > 4:
                    pe.wait_ge(S["pT_hi"], (u - i) // 9 * 4 + i - 3)
                for b in range(nb):
                    w = DEC if i == NT and b == 2 else P
                    vb = NT + b if i == NT else b
                    mm = pe.matmul(ps[0:R, 6 + p, 0:V], pT[p][0:w, b, 0:R], hv[hp][0:w, vb, 0:V],
                                   start=b == 0, stop=b == nb - 1)
                mm.then_inc(S["o_made"], 1)

            def chunks(i):
                return i + max(0, i - 4)

            pe.wait_ge(S["qT_copied"], NT + 1)
            pe.wait_ge(S["v_copied"], NT + 3)
            pe.wait_ge(S["kn_copied"], NT + 3)
            with pe.Fori(0, HM // 2) as j:
                def s_unit(x):
                    i, u = x % 9, 18 * j + x
                    if i == 0:
                        pe.wait_ge(head_s[x // 9], 64 * (j + 1))
                    if x >= 2:
                        pe.wait_ge(S["exp_done"], u - 1)
                    scores(0, i, u_par[x], x // 9, 0, 1, u, QD)
                u_par = [x % 2 for x in range(18)]
                s_unit(0)
                for x in range(19):
                    if x + 1 < 18:
                        s_unit(x + 1)
                    if x < 18:
                        pe.wait_ge(S["exp_done"], 18 * j + x + 1)
                        turn_p(0, 18 * j + x, x % 9, x % 2)
                    if x >= 1:
                        values(18 * j + x - 1, 18 * j + max(0, x - 2), (x - 1) % 9, (x - 1) % 2, (x - 1) // 9, VM)
            with pe.Fori(0, HD // 2) as j:
                UB = 9 * HM

                def s_pair(x):
                    i = x % 9
                    if i == 0:
                        pe.wait_ge(head_s[x // 9], 64 * (HM // 2) + 80 * (j + 1))
                    for m in range(2):
                        if x >= 1:
                            pe.wait_ge(S["exp_done"], UB + 2 * (18 * j + x - 1) + m + 1)
                        scores(0, i, m, x // 9, m, 2, 0, DD)
                s_pair(0)
                for x in range(19):
                    if x + 1 < 18:
                        s_pair(x + 1)
                    if x < 18:
                        pe.wait_ge(S["mix_done"], 18 * j + x + 1)
                        turn_p(0, UB + 18 * j + x, x % 9, x % 2)
                    if x >= 1:
                        values(UB + 18 * j + x - 1, UB + 18 * j + max(0, x - 2), (x - 1) % 9, (x - 1) % 2, (x - 1) // 9, VD)

            def mT_of(t, p):
                R = rows_of(t)
                pe.wait_ge(S["md_done"], t + 1)
                need(pe, S["mT_copied"], t)
                for k in range(KD):
                    mm = turn(4 + k // 4, (k % 4) * P, msrc[p][0:R, k * P:(k + 1) * P], R, P)
                mm.then_inc(S["mT_made"], 1)

            msrc = r1

            def project(t, p):
                R = rows_of(t)
                pe.wait_ge(S["mT_copied"], t + 1)
                need(pe, S["res_done"], t - 1)
                for half in range(2):
                    for k in range(KD):
                        mm = pe.matmul(ps[0:R, 2 * p + half, :], mT[p][:, k, 0:R], w_o[:, k, 512 * half:512 * (half + 1)],
                                       start=k == 0, stop=k == KD - 1)
                mm.then_inc(S["op_made"], 1)

            def hT_of(t, p):
                R = rows_of(t)
                pe.wait_ge(S["h_done"], t + 1)
                need(pe, S["shift_done"], t)
                need(pe, S["rows_done"], t - 1)
                for k in range(KD):
                    mm = turn(6 + k // 4, (k % 4) * P, hrow[p][0:R, k * P:(k + 1) * P], R, P)
                mm.then_inc(S["hT_made"], 1)

            hrow = xr

            def route(t, p):
                R = rows_of(t)
                pe.wait_ge(S["hT_copied"], t + 1)
                for k in range(KD):
                    mm = pe.matmul(ps[0:R, 6, 0:NG + NE], hT[p][:, k, 0:R], w_r[:, k, :], start=k == 0, stop=k == KD - 1)
                mm.then_inc(S["lg_made"], 1)

            def positions(t, p):
                R = rows_of(t)
                pe.wait_ge(S["picks_done"], t + 1)
                pe.matmul(ps[0:R, 7, 0:NE], const[0:R, C_TRI:C_TRI + R], picks[p][0:R, :], start=True, stop=False)
                pe.matmul(ps[0:R, 7, 0:NE], const[:, C_ONE:C_ONE + R], before[p][:], start=False, stop=True).then_inc(S["pre_made"], 1)

            def body3(t, p):
                if is_tile(t, NT):
                    project(t, p)
                if is_tile(t - 1, NT):
                    hT_of(t - 1, 1 - p)
                if is_tile(t + 1, NT):
                    mT_of(t + 1, 1 - p)
                if is_tile(t - 1, NT):
                    route(t - 1, 1 - p)
                if is_tile(t - 2, NT):
                    positions(t - 2, p)

            pe.wait_ge(S["o_done"], 9 * (HM + HD))
            pe.wait_ge(S["wo_in"], 16)
            pe.wait_ge(S["ph3_in"], 16 * 7)
            for t in (-1, 0, 1, 2):
                body3(t, t % 2)
            with pe.Fori(0, 2) as i:
                body3(3 + 2 * i, 1)
                body3(4 + 2 * i, 0)
            for t in range(7, NT + 3):
                body3(t, t % 2)
            pe.wait_ge(S["rows_done"], NT + 1)
            pe.matmul(ps[:, 6, 0:NE], const[:, C_ONE:C_ONE + P], before[(NT + 1) % 2][:], start=True, stop=True).then_inc(S["cnt_made"], 1)

            def rows_turned(e, s, loops):
                p = s % 2
                pe.wait_ge(hg_s[p], (e // 2 + 1) * 16)
                need(pe, S["hgT_copied"], 2 * e)
                for k in range(KD):
                    mm = turn(2 + k // 4, (k % 4) * P, hg[p][:, k * P:(k + 1) * P], P, P)
                    if k % 4 == 3:
                        mm.then_inc(S["hgT_made"], 1)

            def gate_up(e, s, lots):
                p = s % 2
                pe.wait_ge(w_s[s], lots * 48)
                pe.wait_ge(S["hgT_copied"], 2 * e + 2)
                need(pe, S["hid_done"], e - 1)
                for k in range(KD):
                    mm = pe.matmul(ps[:, p, :], hgT[p][:, k, :], wgu[s][:, k, :], start=k == 0, stop=k == KD - 1)
                mm.then_inc(S["gu_made"], 1)

            def hidden_turned(e, s):
                p = s % 2
                pe.wait_ge(S["hid_done"], e + 1)
                need(pe, S["hidT_copied"], e)
                for k in range(2):
                    mm = turn(4, k * P, hid[p][:, k * P:(k + 1) * P], P, P)
                mm.then_inc(S["hidT_made"], 1)

            def down(e, s):
                p = s % 2
                pe.wait_ge(S["hidT_copied"], e + 1)
                need(pe, S["y_lo"], e)
                need(pe, S["y_hi"], e)
                for half in range(2):
                    for k in range(2):
                        mm = pe.matmul(ps[:, 5 + half, :], hidT[p][:, k, :], wdn[s][:, k, 512 * half:512 * (half + 1)],
                                       start=k == 0, stop=k == 1)
                mm.then_inc(S["dn_made"], 1)

            def body4(g, first):
                for s in range(SLOTS):
                    e = g * SLOTS + s
                    rows_turned(e, s, g)
                    if not first or s >= 2:
                        down(e - 2, (s - 2) % SLOTS)
                    if not first or s >= 1:
                        hidden_turned(e - 1, (s - 1) % SLOTS)
                    gate_up(e, s, g + 1)

            pe.wait_ge(S["swp_done"], 1)
            n = pe.value_load(more[0:1, 0:1], min_val=0, max_val=SWEEPS - 1) + 1
            body4(0, True)
            with pe.Fori(1, n * (NE // SLOTS)) as g:
                body4(g, False)
            E = n * NE
            down(E - 2, SLOTS - 2)
            hidden_turned(E - 1, SLOTS - 1)
            down(E - 1, SLOTS - 1)

        @block.scalar
        def _(act):
            def copy(dst, src, scale=None):
                return nc.scalar.activation(dst, src, ACT.Copy, scale=1.0 if scale is None else scale)

            def xT_copy(t, p):
                R = rows_of(t)
                act.wait_ge(S["xT_made"], t + 1)
                need(act, S["z_made"], 5 * (t - 1))
                ins = copy(xT[p][:, :, 0:R], ps[:, 4:6, :].rearrange("p b (k r) -> p (b k) r", r=P)[:, :, 0:R])
                ins.then_inc(S["xT_copied"], 1)

            def latents(t, p):
                R = rows_of(t)
                act.wait_ge(S["z_made"], 5 * t + 1)
                need(act, S["rms_done"], t - 1)
                for c in range(2):
                    ins = nc.scalar.activation(junk[0:R, c, :], ps[0:R, 0, 256 * c:256 * (c + 1)], ACT.Square,
                                               accum_out=ss[p][0:R, c:c + 1])
                ins.then_inc(S["sq_done"], 1)

            def keep(t, p, c):
                R = rows_of(t)
                act.wait_ge(S["z_made"], 5 * t + c + 1)
                if c == 1:
                    need(act, st_s[p], FULL_ST * (t // 2))
                    need(act, S["kpT_made"], t - 1)
                    copy(kr[p][0:R, :], ps[0:R, 1, 0:ROPE]).then_inc(S["kr_copied"], 1)
                elif c in (2, 3):
                    if c == 2:
                        need(act, S["dT_made"], t - 1)
                    ins = copy(zqk[p][0:R, c - 2].rearrange("p h d -> p (h d)"), ps[0:R, c, :],
                               DIFF_SCALE if c == 2 else None)
                    if c == 3:
                        ins.then_inc(S["dqk_copied"], 1)
                else:
                    copy(zv[p][0:R, :], ps[0:R, 1, :]).then_inc(S["dv_copied"], 1)

            def cT_copy(t, p, R, c0):
                act.wait_ge(S["cT_made"], t + 1)
                need(act, S["v_made"], t - 1)
                copy(cT[p][:, c0:4, 0:R], ps[:, 6, :].rearrange("p (k r) -> p k r", r=P)[:, c0:4, 0:R]).then_inc(S["cT_copied"], 1)

            def q_copy(t, p):
                R = rows_of(t)
                act.wait_ge(S["q_made"], t + 1)
                need(act, S["qT_made"], t - 1)
                copy(qs[p][0:R].rearrange("p (a h) d -> p a (h d)", a=2), ps[0:R, 6:8, 0:384], MLA_SCALE).then_inc(S["q_copied"], 1)

            def v_copy(t, p, R):
                act.wait_ge(S["v_made"], t + 1)
                if isinstance(t, int) and t > NT:
                    act.wait_ge(st_s[p], FULL_ST * (4 if p else 5))
                copy(vs[p][0:R, :], ps[0:R, 5, :]).then_inc(S["v_copied"], 1)

            def qT_copy(t, p):
                R = rows_of(t)
                act.wait_ge(S["qT_made"], t + 1)
                copy(qT[p][:, :, 0:R], ps[0:QD, 6:8, :].rearrange("p b (k r) -> p (b k) r", r=P)[:, :, 0:R]).then_inc(S["qT_copied"], 1)

            def body1(t, p):
                cur, prev = is_tile(t, NT), is_tile(t - 1, NT)
                q, R1 = 1 - p, rows_of(t - 1)
                if cur:
                    latents(t, p)
                    keep(t, p, 1)
                if prev:
                    cT_copy(t - 1, q, R1, 0)
                if cur:
                    keep(t, p, 2)
                if prev:
                    q_copy(t - 1, q)
                    v_copy(t - 1, q, R1)
                if cur:
                    keep(t, p, 3)
                    keep(t, p, 4)
                if prev:
                    qT_copy(t - 1, q)
                if is_tile(t + 1, NT):
                    xT_copy(t + 1, q)

            ch = Chain(act, S["ch_act"])
            xT_copy(0, 0)
            act.wait_ge(S["lam_prod"], 1)
            nc.scalar.activation(lame[:], lams[:], ACT.Exp).then_inc(S["lam_exp"], 1)
            for t in range(3):
                body1(t, t % 2)
            with act.Fori(0, 2) as i:
                body1(3 + 2 * i, 1)
                body1(4 + 2 * i, 0)
            body1(7, 1)
            body1(8, 0)
            body1(9, 1)
            for c in range(2):
                cT_copy(NT + 1 + c, 1 - c, P, 2)
                v_copy(NT + 1 + c, 1 - c, P)

            def width(i):
                return KEYS - SEQ if i == NT else (i + 1) * P

            def span(p, n, R):
                return ps[0:R, 2 * p:2 * p + 2, :].rearrange("p b c -> p (b c)")[:, 0:n]

            def exp(i, bank, dst, nm, sm):
                R, n = rows_of(i), width(i)
                nc.scalar.activation(dst[0:R, 0:n], span(bank, n, R), ACT.Exp, bias=nm[0:R, :],
                                     accum_out=sm[0:R, :]).then_inc(S["exp_done"], 1)

            def pT_copy(used, made, i, p):
                R, w = rows_of(i), min(4, 3 if i == NT else i + 1)
                act.wait_ge(S["pT_made"], made)
                need(act, S["o_made"], used)
                if i == NT:
                    ch(copy(pT[p][:, 0:2, 0:R], ps[:, 4, :].rearrange("p (k r) -> p k r", r=P)[:, 0:2, 0:R]))
                    copy(pT[p][0:DEC, 2, 0:R], ps[0:DEC, 4, 2 * P:2 * P + R]).then_inc(S["pT_lo"], 1)
                else:
                    copy(pT[p][:, 0:w, :], ps[:, 4, 0:w * P].rearrange("p (k r) -> p k r", r=P)).then_inc(S["pT_lo"], 1)

            def chunks(i):
                return i + max(0, i - 4)

            with act.Fori(0, HM // 2) as j:
                ch.enter(j, 2)

                def exp_unit(x):
                    u = 18 * j + x
                    act.wait_ge(S["max_done"], u + 1)
                    if x >= 2:
                        act.wait_ge(S["pT_made"], 26 * j + 13 * ((x - 2) // 9) + chunks((x - 2) % 9 + 1))
                        act.wait_ge(S["o_done"], u - 1)
                    exp(x % 9, x % 2, pr[x % 2][0], nmax[x % 2][0], psums[x % 2][0])
                exp_unit(0)
                for x in range(18):
                    pT_copy(18 * j + max(0, x - 1), 26 * j + 13 * (x // 9) + chunks(x % 9) + 1, x % 9, x % 2)
                    if x + 1 < 18:
                        exp_unit(x + 1)
            ch.leave(HM // 2)
            with act.Fori(0, HD // 2) as j:
                ch.enter(j, 2)
                UB, CB = 9 * HM, 13 * HM

                def exp_pair(x):
                    for m in range(2):
                        act.wait_ge(S["max_done"], UB + 2 * (18 * j + x) + m + 1)
                        if x >= 2 and m == 0:
                            act.wait_ge(S["pT_made"], CB + 26 * j + 13 * ((x - 2) // 9) + chunks((x - 2) % 9 + 1))
                            act.wait_ge(S["o_done"], UB + 18 * j + x - 1)
                        exp(x % 9, m, pr[x % 2][m], nmax[x % 2][m], psums[x % 2][m])
                exp_pair(0)
                for x in range(18):
                    pT_copy(UB + 18 * j + max(0, x - 1), CB + 26 * j + 13 * (x // 9) + chunks(x % 9) + 1, x % 9, x % 2)
                    if x + 1 < 18:
                        exp_pair(x + 1)
            ch.leave(HD // 2)

            def body3(t, p):
                if is_tile(t - 2, NT):
                    R = rows_of(t - 2)
                    act.wait_ge(S["shift_done"], t - 1)
                    need(act, S["rows_done"], t - 3)
                    nc.scalar.activation(exped[p][0:R, 0:5], shifted[p][0:R, 0:5], ACT.Exp).then_inc(S["exp3_done"], 1)
                if is_tile(t - 1, NT):
                    R = rows_of(t - 1)
                    act.wait_ge(S["hT_made"], t)
                    need(act, S["lg_made"], t - 2)
                    copy(hT[1 - p][:, :, 0:R], ps[:, 6:8, :].rearrange("p b (k r) -> p (b k) r", r=P)[:, :, 0:R]).then_inc(S["hT_copied"], 1)
                if is_tile(t + 1, NT):
                    R = rows_of(t + 1)
                    act.wait_ge(S["mT_made"], t + 2)
                    need(act, S["op_made"], t)
                    copy(mT[1 - p][:, :, 0:R], ps[:, 4:6, :].rearrange("p b (k r) -> p (b k) r", r=P)[:, :, 0:R]).then_inc(S["mT_copied"], 1)

            act.wait_ge(S["o_done"], 9 * (HM + HD))
            for t in (-1, 0, 1, 2):
                body3(t, t % 2)
            with act.Fori(0, 2) as i:
                body3(3 + 2 * i, 1)
                body3(4 + 2 * i, 0)
            for t in range(7, NT + 3):
                body3(t, t % 2)

            def rows_copy(e, s):
                p = s % 2
                act.wait_ge(S["hgT_made"], 2 * e + 1)
                need(act, S["gu_made"], e - 1)
                copy(hgT[p][:, 0:4, :], ps[:, 2, :].rearrange("p (k r) -> p k r", r=P)).then_inc(S["hgT_copied"], 1)

            def silu(e, s):
                p = s % 2
                act.wait_ge(S["gu_made"], e + 1)
                need(act, S["hid_done"], e - 1)
                nc.scalar.activation(sil[p][:], ps[:, p, 0:FE], ACT.Silu).then_inc(S["silu_done"], 1)

            def y_copy(e, s):
                p = s % 2
                act.wait_ge(S["dn_made"], e + 1)
                need(act, y_s[p], (e // 2) * 16)
                copy(y[p][:, 0:512], ps[:, 5, :], tab[s][:, 2:3].bitcast(F32)).then_inc(S["y_lo"], 1)

            def body4(g, first):
                for s in range(SLOTS):
                    e = g * SLOTS + s
                    rows_copy(e, s)
                    if not first or s >= 2:
                        y_copy(e - 2, (s - 2) % SLOTS)
                    silu(e, s)

            act.wait_ge(S["swp_done"], 1)
            n = act.value_load(more[0:1, 0:1], min_val=0, max_val=SWEEPS - 1) + 1
            body4(0, True)
            with act.Fori(1, n * (NE // SLOTS)) as g:
                body4(g, False)
            y_copy(n * NE - 2, SLOTS - 2)
            y_copy(n * NE - 1, SLOTS - 1)
            act.wait_ge(S["ln2_in"], 32)
            for t in range(NT + 1):
                R, f = rows_of(t), t % NF
                act.wait_ge(S["frstd"], 2 * t + 2)
                nc.scalar.activation(y1[f][0:R, :], y0[f][0:R, :], ACT.Identity, bias=fve[f][0:R, :],
                                     scale=frs[f][0:R, :]).then_inc(S["fnorm"], 1)

        @block.vector
        def _(ve_):
            v = nc.vector
            ch = Chain(ve_, S["ch_dve"])

            def rotate(which, x1, x2, cos, sin, shape):
                n = int(np.prod(shape[1:]))
                t = [rt4[which][0:shape[0], k, 0:n] for k in range(4)]
                if len(shape) == 3:
                    t = [b.rearrange("p (a b) -> p a b", b=shape[2]) for b in t]
                ch.inc(v.tensor_tensor(t[0], x1, cos, ALU.mult))
                ch.inc(v.tensor_tensor(t[1], x2, sin, ALU.mult))
                ch.inc(v.tensor_tensor(t[2], x1, sin, ALU.mult))
                ch(v.tensor_tensor(t[3], x2, cos, ALU.mult))
                ch.inc(v.tensor_tensor(x1, t[0], t[1], ALU.subtract))
                return v.tensor_tensor(x2, t[2], t[3], ALU.add)

            def norms(t, p):
                R = rows_of(t)
                ve_.wait_ge(S["rms_done"], t + 1)
                need(ve_, S["cT_made"], t - 1)
                need(ve_, st_s[p], FULL_ST * (t // 2))
                for c, (dst, g) in enumerate(((cqn, gq), (ckvn, gkv))):
                    ins = v.scalar_tensor_tensor(out=dst[p][0:R, :], in0=ps[0:R, 0, 256 * c:256 * (c + 1)],
                                                 scalar=rq[p][0:R, c:c + 1], in1=g[0:R, :], op0=ALU.mult, op1=ALU.mult)
                ins.then_inc(S["norm_done"], 1)

            def table(p, R, a0, n, shape):
                return rope[p][0:R, a0:a0 + n] if shape is None else rope[p][0:R, a0:a0 + n].unsqueeze(1).broadcast_to(shape)

            def kr_rope(t, p):
                R, h = rows_of(t), ROPE // 2
                ve_.wait_ge(S["kr_copied"], t + 1)
                ve_.wait_ge(x_in_s[p], 32 * (t // 2 + 1))
                rotate(0, kr[p][0:R, 0:h], kr[p][0:R, h:2 * h], table(p, R, 0, h, None), table(p, R, h, h, None),
                       (R, h)).then_inc(S["kr_roped"], 1)

            def dqk_rope(t, p):
                R, h = rows_of(t), ROT // 2
                ve_.wait_ge(S["dqk_copied"], t + 1)
                x = zqk[p][0:R].rearrange("p a h d -> p (a h) d")
                shape = [R, 4 * HD, h]
                rotate(2, x[:, :, 0:h], x[:, :, h:2 * h], table(p, R, ROPE, h, shape), table(p, R, ROPE + h, h, shape),
                       shape).then_inc(S["dqk_roped"], 1)

            def kpT_copy(t, p, R):
                ve_.wait_ge(S["kpT_made"], t + 1)
                if isinstance(t, int) and t > NT:
                    ve_.wait_ge(st_s[p], FULL_ST * (4 if p else 5))
                v.tensor_copy(kpT[p][:, 0:R], ps[0:ROPE, 5, 0:R]).then_inc(S["kpT_copied"], 1)

            def dT_copy(t, p, R, first):
                ve_.wait_ge(S["dT_made"], t + 1)
                for half in range(first, 2):
                    ins = v.tensor_copy(dT[p][:, half, :, 0:R],
                                        ps[:, (7, 4)[half], :].rearrange("p (k r) -> p k r", r=P)[:, :, 0:R])
                ins.then_inc(S["dT_copied"], 1)

            def kn_copy(t, p, R):
                ve_.wait_ge(S["kn_made"], t + 1)
                v.tensor_copy(knT[p][:, :, 0:R], ps[:, 4, :].rearrange("p (k r) -> p k r", r=P)[:, :, 0:R]).then_inc(S["kn_copied"], 1)

            def q_rope(t, p):
                R, h = rows_of(t), ROPE // 2
                ve_.wait_ge(S["q_copied"], t + 1)
                shape = [R, HM, h]
                rotate(1, qs[p][0:R, :, NOPE:NOPE + h], qs[p][0:R, :, NOPE + h:QD],
                       table(p, R, 0, h, shape), table(p, R, h, h, shape), shape).then_inc(S["q_roped"], 1)

            def body1(t, p):
                cur, prev = is_tile(t, NT), is_tile(t - 1, NT)
                q, R1 = 1 - p, rows_of(t - 1)
                if cur:
                    norms(t, p)
                    kr_rope(t, p)
                if prev:
                    kpT_copy(t - 1, q, R1)
                    dT_copy(t - 1, q, R1, 0)
                    q_rope(t - 1, q)
                    kn_copy(t - 1, q, R1)
                if cur:
                    dqk_rope(t, p)

            v.memset(pad_rows[:], PAD).then_inc(S["pads_set"], 1)
            ve_.wait_ge(S["lam_in"], 64)
            ch.inc(v.tensor_tensor(lamt[:, 0, :], lam4[:, 0, :], lam4[:, 1, :], ALU.mult))
            ch(v.tensor_tensor(lamt[:, 1, :], lam4[:, 2, :], lam4[:, 3, :], ALU.mult))
            v.tensor_reduce(lams[:], lamt[:], AX.X, ALU.add).then_inc(S["lam_prod"], 1)
            ve_.wait_ge(S["lam_exp"], 1)
            ch(v.tensor_scalar(neglam[:], lame[:, 1:2], -LAM_INIT, None, ALU.add))
            ch(v.tensor_tensor(neglam[:], neglam[:], lame[:, 0:1], ALU.subtract))
            ve_.wait_ge(S["rope_in"], 32)
            for t in range(3):
                body1(t, t % 2)
            with ve_.Fori(0, 2) as i:
                ch.enter(i, 30)
                body1(3 + 2 * i, 1)
                body1(4 + 2 * i, 0)
            ch.leave(2)
            body1(7, 1)
            body1(8, 0)
            body1(9, 1)
            for c in range(2):
                kpT_copy(NT + 1 + c, 1 - c, P)
                dT_copy(NT + 1 + c, 1 - c, P, 1)
                kn_copy(NT + 1 + c, 1 - c, P)

            def chunks(i):
                return i + max(0, i - 4)

            def row_max(i, bank, nm, s_count):
                R, n = rows_of(i), KEYS - SEQ if i == NT else (i + 1) * P
                ve_.wait_ge(S["s_made"], s_count)
                sc = ps[0:R, 2 * bank:2 * bank + 2, :].rearrange("p b c -> p (b c)")
                if i < NT:
                    ch(v.memset(sc[0:64, n - 64:n], NEG))
                v.tensor_reduce(nm[0:R, :], sc[:, 0:n], AX.X, ALU.max, negate=True).then_inc(S["max_done"], 1)

            def pT_copy(used, made, i, p):
                if i == NT or i < 4:
                    return
                w = i - 3
                ve_.wait_ge(S["pT_made"], made)
                need(ve_, S["o_made"], used)
                v.tensor_copy(pT[p][:, 4:4 + w, :], ps[:, 5, 0:w * P].rearrange("p (k r) -> p k r", r=P)).then_inc(S["pT_hi"], 1)

            def o_copy(u, i, p, col, V, m_sum):
                R = rows_of(i)
                ve_.wait_ge(S["exp_done"], m_sum)
                ch(v.reciprocal(rsum[p][0:R, 0:1], psums[p][0][0:R, :]))
                ve_.wait_ge(S["o_made"], u + 1)
                v.tensor_scalar(merged[0:R, i, bass.ds(col, V)], ps[0:R, 6 + p, 0:V], rsum[p][0:R, 0:1], None,
                                ALU.mult).then_inc(S["o_done"], 1)

            ve_.wait_ge(st_s[1], FULL_ST * 4 + 5 * 16)
            ve_.wait_ge(st_s[0], FULL_ST * 5 + 5 * 16)
            with ve_.Fori(0, HM // 2) as j:
                ch.enter(j, 34)

                def mx(x):
                    if x >= 2:
                        ve_.wait_ge(S["exp_done"], 18 * j + x - 1)
                    row_max(x % 9, x % 2, nmax[x % 2][0], 18 * j + x + 1)
                mx(0)
                for x in range(19):
                    if x + 1 < 18:
                        mx(x + 1)
                    if x < 18:
                        pT_copy(18 * j + max(0, x - 1), 26 * j + 13 * (x // 9) + chunks(x % 9) + 2, x % 9, x % 2)
                    if x >= 1:
                        o_copy(18 * j + x - 1, (x - 1) % 9, (x - 1) % 2, (2 * j + (x - 1) // 9) * VM, VM, 18 * j + x)
            ch.leave(HM // 2)
            with ve_.Fori(0, HD // 2) as j:
                ch.enter(j, 16 * 2 + 18 * 3)
                UB, CB = 9 * HM, 13 * HM

                def mx(x):
                    for m in range(2):
                        if x >= 2:
                            ve_.wait_ge(S["exp_done"], UB + 2 * (18 * j + x - 2) + m + 1)
                        row_max(x % 9, m, nmax[x % 2][m], UB + 2 * (18 * j + x) + m + 1)

                def mix(x):
                    i, p = x % 9, x % 2
                    R, n = rows_of(i), KEYS - SEQ if i == NT else (i + 1) * P
                    ve_.wait_ge(S["exp_done"], UB + 2 * (18 * j + x) + 2)
                    ch(v.reciprocal(rsum[p][0:R, 1:2], psums[p][1][0:R, :]))
                    ch(v.scalar_tensor_tensor(out=mixc[p][0:R, :], in0=psums[p][0][0:R, :], scalar=rsum[p][0:R, 1:2],
                                              in1=neglam[0:R, :], op0=ALU.mult, op1=ALU.mult))
                    v.scalar_tensor_tensor(out=pr[p][0][0:R, 0:n], in0=pr[p][1][0:R, 0:n], scalar=mixc[p][0:R, :],
                                           in1=pr[p][0][0:R, 0:n], op0=ALU.mult, op1=ALU.add).then_inc(S["mix_done"], 1)
                mx(0)
                for x in range(19):
                    if x < 18:
                        mix(x)
                    if x + 1 < 18:
                        mx(x + 1)
                    if x < 18:
                        pT_copy(UB + 18 * j + max(0, x - 1), CB + 26 * j + 13 * (x // 9) + chunks(x % 9) + 2, x % 9, x % 2)
                    if x >= 1:
                        o_copy(UB + 18 * j + x - 1, (x - 1) % 9, (x - 1) % 2, HM * VM + (2 * j + (x - 1) // 9) * VD, VD,
                               UB + 2 * (18 * j + x))
            ch.leave(HD // 2)

            def merged_norm(t, p):
                R = rows_of(t)
                ve_.wait_ge(S["sq3_done"], t + 1)
                need(ve_, S["hrs_done"], t - 1)
                v.tensor_reduce(m4s[p][0][0:R, :], sq[p][0:R], AX.X, ALU.add).then_inc(S["hsq_done"], 1)
                need(ve_, S["h_done"], t - 1)
                mr = merged[0:R, bass.ds(t, 1), :].rearrange("p a d -> p (a d)")
                st = r1[p][0:R, :]
                v.tensor_copy(st[:, 0:512], mr[:, 0:512])
                ve_.wait_ge(S["hrs_done"], t + 1)
                d4 = st[:, 512:1024].rearrange("p (h v) -> p h v", v=VD)
                ch(v.tensor_tensor(d4, mr[:, 512:1024].rearrange("p (h v) -> p h v", v=VD),
                                   m4s[p][2][0:R, :].unsqueeze(2).broadcast_to([R, HD, VD]), ALU.mult))
                v.tensor_tensor(d4, d4, subln[0:R, :].unsqueeze(1).broadcast_to([R, HD, VD]), ALU.mult).then_inc(S["md_done"], 1)

            def layer1(t, p):
                R = rows_of(t)
                ve_.wait_ge(S["op_made"], t + 1)
                ve_.wait_ge(xr_s[p], 16 * (t // 2 + 1))
                for half in range(2):
                    c = slice(512 * half, 512 * (half + 1))
                    ins = v.scalar_tensor_tensor(out=r1[p][0:R, c], in0=xr[p][0:R, c], scalar=ALPHA, in1=ps[0:R, 2 * p + half, :],
                                                 op0=ALU.mult, op1=ALU.add)
                ins.then_inc(S["res_done"], 1)
                ve_.wait_ge(S["res_done"], t + 1)
                for half in range(2):
                    ch.inc(v.bn_stats(bst[p][0:R, half, :], r1[p][0:R, 512 * half:512 * (half + 1)]))
                ch.wait()
                settle(ve_)
                v.bn_aggr(mv[p][0:R, :], bst[p][0:R].rearrange("p a b -> p (a b)")).then_inc(S["ln_stat"], 1)
                ve_.wait_ge(S["ln_rstd"], t + 1)
                ch(v.tensor_scalar(r1[p][0:R, :], r1[p][0:R, :], mv[p][0:R, 0:1], rst[p][0:R, :], ALU.subtract, ALU.mult))
                v.tensor_tensor(r1[p][0:R, :], r1[p][0:R, :], g1b[0:R, :], ALU.mult).then_inc(S["ln_mul"], 1)

            def first_of(vals, n, w, m, oh, R):
                ch(v.tensor_reduce(m, vals, AX.X, ALU.max))
                ch(v.scalar_tensor_tensor(out=w, in0=vals, scalar=m, in1=const[0:R, C_DESC:C_DESC + n], op0=ALU.is_ge, op1=ALU.mult))
                ch(v.tensor_reduce(top1[0:R, 7:8], w, AX.X, ALU.max))
                ch(v.tensor_scalar(oh, w, top1[0:R, 7:8], None, ALU.is_equal))

            def choose(t, p):
                R = rows_of(t)
                ve_.wait_ge(S["lg_made"], t + 1)
                ch(v.tensor_tensor(lg[0:R, :], ps[0:R, 6, 0:NG + NE], b_r[0:R, :], ALU.add))
                first_of(lg[0:R, 0:NG], NG, wgt[0:R, 0:NG], top1[0:R, 0:1], ohg[0:R, :], R)
                g3 = ohg[0:R, :].unsqueeze(2).broadcast_to([R, NG, EPG])
                ch(v.tensor_tensor(emul[0:R], lg[0:R, NG:NG + NE].rearrange("p (g j) -> p g j", j=EPG), g3, ALU.mult))
                ch(v.tensor_reduce(ein8[0:R, 0, :], emul[0:R].rearrange("p g j -> p j g"), AX.X, ALU.add))
                first_of(ein8[0:R, 0, :], EPG, wgt[0:R, :], top1[0:R, 1:2], ohe[0:R, 0, :], R)
                ch(v.scalar_tensor_tensor(out=ein8[0:R, 1, :], in0=ohe[0:R, 0, :], scalar=NEG, in1=ein8[0:R, 0, :], op0=ALU.mult, op1=ALU.add))
                first_of(ein8[0:R, 1, :], EPG, wgt[0:R, :], top1[0:R, 2:3], ohe[0:R, 1, :], R)
                need(ve_, S["exp3_done"], t - 1)
                ch.inc(v.tensor_scalar(shifted[p][0:R, 0:NG], lg[0:R, 0:NG], top1[0:R, 0:1], None, ALU.subtract))
                v.tensor_tensor(shifted[p][0:R, 4:5], top1[0:R, 2:3], top1[0:R, 1:2], ALU.subtract).then_inc(S["shift_done"], 1)
                need(ve_, S["pre_made"], t - 1)
                for k in range(2):
                    ch.inc(v.tensor_tensor(oh32[p][0:R, k, :].rearrange("p (g j) -> p g j", j=EPG), g3,
                                           ohe[0:R, k, :].unsqueeze(1).broadcast_to([R, NG, EPG]), ALU.mult))
                ch.wait()
                v.tensor_tensor(picks[p][0:R, :], oh32[p][0:R, 0, :], oh32[p][0:R, 1, :], ALU.add).then_inc(S["picks_done"], 1)

            def list_rows(t, p):
                R = rows_of(t)
                ve_.wait_ge(S["exp3_done"], t + 1)
                ch(v.tensor_reduce(gates[p][0:R, 2:3], exped[p][0:R, 0:NG], AX.X, ALU.add))
                ch(v.scalar_tensor_tensor(out=gates[p][0:R, 3:4], in0=exped[p][0:R, 4:5], scalar=1.0, in1=gates[p][0:R, 2:3],
                                          op0=ALU.add, op1=ALU.mult))
                ch(v.reciprocal(gates[p][0:R, 0:1], gates[p][0:R, 3:4]))
                ch(v.tensor_tensor(gates[p][0:R, 1:2], exped[p][0:R, 4:5], gates[p][0:R, 0:1], ALU.mult))
                if not isinstance(t, int) or t >= 2:
                    ve_.wait_ge(ent_s[p], 32 * (t // 2))
                tok = const[0:R, bass.ds(C_TOK + t, 1)]
                for k in range(2):
                    ch.inc(v.tensor_copy(entry[p][0:R, k, 0:1], tok))
                    ch.inc(v.tensor_scalar(entry[p][0:R, k, 1:2], tok, float(k * TOK), None, ALU.add))
                    ch.inc(v.tensor_copy(entry[p][0:R, k, 2:3].bitcast(F32), gates[p][0:R, k:k + 1]))
                ve_.wait_ge(S["pre_made"], t + 1)
                ch(v.scalar_tensor_tensor(out=where[0:R, :], in0=ps[0:R, 7, 0:NE], scalar=float(NE), in1=const[0:R, C_IOTA:C_IOTA + NE],
                                          op0=ALU.mult, op1=ALU.add))
                ch(v.tensor_tensor(where2[0:R], oh32[p][0:R], where[0:R, :].unsqueeze(1).broadcast_to([R, 2, NE]), ALU.mult))
                ch(v.tensor_reduce(rowf[0:R, :], where2[0:R], AX.X, ALU.add))
                ch(v.tensor_copy(row[p][0:R].rearrange("p a b -> p (a b)"), rowf[0:R, :]))
                if R < P:
                    ch.inc(v.tensor_copy(before[1 - p][R:P, :], before[p][R:P, :]))
                v.tensor_tensor(before[1 - p][0:R, :], before[p][0:R, :], picks[p][0:R, :], ALU.add).then_inc(S["rows_done"], 1)

            def body3(t, p):
                if is_tile(t + 1, NT):
                    merged_norm(t + 1, 1 - p)
                if is_tile(t - 3, NT):
                    list_rows(t - 3, 1 - p)
                if is_tile(t - 2, NT):
                    choose(t - 2, p)
                if is_tile(t, NT):
                    layer1(t, p)

            ve_.wait_ge(S["ph3_in"], 16 * 7)
            ch(v.tensor_scalar(subln[:], subln[:], 1.0 - LAM_INIT, None, ALU.mult))
            for k in range(2):
                ch.inc(v.memset(before[k][:], 0.0))
                ch.inc(v.memset(entry[k][:], 0))
            ch.wait()
            for t in (-1, 0, 1, 2):
                body3(t, t % 2)
            with ve_.Fori(0, 2) as i:
                ch.enter(i, 74)
                body3(3 + 2 * i, 1)
                body3(4 + 2 * i, 0)
            ch.leave(2)
            for t in range(7, NT + 4):
                body3(t, t % 2)
            ve_.wait_ge(S["cnt_made"], 1)
            ch(v.tensor_reduce(cntm[:], ps[:, 6, 0:NE], AX.X, ALU.max))
            ch(v.tensor_scalar(over[:], const[:, C_THR:C_THR + 8], cntm[:], None, ALU.is_lt))
            ch(v.tensor_reduce(nover[:], over[:], AX.X, ALU.add))
            v.tensor_copy(more[:], nover[:]).then_inc(S["swp_done"], 1)

            def rows_copy(e, s):
                p = s % 2
                ve_.wait_ge(S["hgT_made"], 2 * e + 2)
                need(ve_, S["gu_made"], e - 1)
                ve_.wait_ge(S["hgT_copied"], 2 * e + 1)
                v.tensor_copy(hgT[p][:, 4:8, :], ps[:, 3, :].rearrange("p (k r) -> p k r", r=P)).then_inc(S["hgT_copied"], 1)

            def hidden(e, s):
                p = s % 2
                ve_.wait_ge(S["silu_done"], e + 1)
                need(ve_, S["hidT_made"], e - 1)
                v.tensor_tensor(hid[p][:], sil[p][:], ps[:, p, FE:2 * FE], ALU.mult).then_inc(S["hid_done"], 1)

            def hidT_copy(e, s):
                p = s % 2
                ve_.wait_ge(S["hidT_made"], e + 1)
                need(ve_, S["dn_made"], e - 1)
                v.tensor_copy(hidT[p][:].rearrange("p k r -> p (k r)"), ps[:, 4, 0:2 * P]).then_inc(S["hidT_copied"], 1)

            def y_copy(e, s):
                p = s % 2
                ve_.wait_ge(S["dn_made"], e + 1)
                need(ve_, y_s[p], (e // 2) * 16)
                v.tensor_scalar(y[p][:, 512:1024], ps[:, 6, :], tab[s][:, 2:3].bitcast(F32), None, ALU.mult).then_inc(S["y_hi"], 1)

            def body4(g, first):
                for s in range(SLOTS):
                    e = g * SLOTS + s
                    rows_copy(e, s)
                    if not first or s >= 2:
                        y_copy(e - 2, (s - 2) % SLOTS)
                    if not first or s >= 1:
                        hidT_copy(e - 1, (s - 1) % SLOTS)
                    hidden(e, s)

            ve_.wait_ge(S["swp_done"], 1)
            n = ve_.value_load(more[0:1, 0:1], min_val=0, max_val=SWEEPS - 1) + 1
            for k in range(2):
                ins = v.memset(hg[k][:], 0.0)
            ins.then_inc(S["hg_zero"], 1)
            body4(0, True)
            with ve_.Fori(1, n * (NE // SLOTS)) as g:
                body4(g, False)
            E = n * NE
            y_copy(E - 2, SLOTS - 2)
            hidT_copy(E - 1, SLOTS - 1)
            y_copy(E - 1, SLOTS - 1)

            ve_.wait_ge(S["ln2_in"], 32)
            def fin_stats(t):
                R, f = rows_of(t), t % NF
                ve_.wait_ge(f_in[f], 32 * (t // NF + 1))
                ch(v.scalar_tensor_tensor(out=y0[f][0:R, :], in0=merged[0:R, t, :], scalar=ALPHA, in1=y0[f][0:R, :],
                                          op0=ALU.mult, op1=ALU.add))
                ch(v.tensor_tensor(y0[f][0:R, :], y0[f][0:R, :], y1[f][0:R, :], ALU.add))
                for half in range(2):
                    ch.inc(v.bn_stats(fst[f][0:R, half, :], y0[f][0:R, 512 * half:512 * (half + 1)]))
                ch.wait()
                v.bn_aggr(fmv[f][0:R, :], fst[f][0:R].rearrange("p a b -> p (a b)")).then_inc(S["fstat"], 1)

            def fin_mul(t):
                R, f = rows_of(t), t % NF
                ve_.wait_ge(S["fnorm"], t + 1)
                v.tensor_tensor(y1[f][0:R, :], y1[f][0:R, :], g2b[0:R, :], ALU.mult).then_inc(S["fmul"], 1)

            for t in range(NT + 2):
                if t <= NT:
                    fin_stats(t)
                if t >= 1:
                    fin_mul(t - 1)

        @block.gpsimd
        def _(po):
            g = nc.gpsimd
            ch = Chain(po, S["ch_pool"])

            def rsqrt(dst, src, tmp, R, n, inv, eps):
                settle(po)
                ch(g.tensor_scalar(tmp, src, inv, eps, ALU.mult, ALU.add))
                return g.tensor_tensor(dst, tmp, const[0:R, C_HALF:C_HALF + n], ALU.pow)

            def rms(t, p):
                R = rows_of(t)
                po.wait_ge(S["sq_done"], t + 1)
                need(po, S["norm_done"], t - 1)
                rsqrt(rq[p][0:R, :], ss[p][0:R, :], ms[p][0:R, :], R, 2, 1.0 / QR, EPS_RMS).then_inc(S["rms_done"], 1)

            po.wait_ge(S["const_in"], 16)
            for t in range(3):
                rms(t, t % 2)
            with po.Fori(0, 2) as i:
                ch.enter(i, 2)
                rms(3 + 2 * i, 1)
                rms(4 + 2 * i, 0)
            ch.leave(2)
            rms(7, 1)
            rms(8, 0)

            def squares(t, p):
                R = rows_of(t)
                need(po, S["hsq_done"], t - 1)
                d = merged[0:R, bass.ds(t, 1), 512:1024].rearrange("p a (h v) -> p (a h) v", v=VD)
                g.tensor_tensor(sq[p][0:R], d, d, ALU.mult).then_inc(S["sq3_done"], 1)
                po.wait_ge(S["hsq_done"], t + 1)
                need(po, S["md_done"], t - 1)
                rsqrt(m4s[p][2][0:R, :], m4s[p][0][0:R, :], m4s[p][1][0:R, :], R, HD, 1.0 / VD, EPS_RMS).then_inc(S["hrs_done"], 1)

            def layer1(t, p):
                R = rows_of(t)
                po.wait_ge(S["ln_stat"], t + 1)
                rsqrt(rst[p][0:R, :], mv[p][0:R, 1:2], ve[p][0:R, :], R, 1, 1.0, EPS_LN).then_inc(S["ln_rstd"], 1)
                po.wait_ge(S["ln_mul"], t + 1)
                need(po, S["mT_made"], t + 1)
                ch(g.tensor_tensor(xr[p][0:R, :], r1[p][0:R, :], b1b[0:R, :], ALU.add))
                g.tensor_copy(merged[0:R, bass.ds(t, 1), :].rearrange("p a d -> p (a d)"), xr[p][0:R, :]).then_inc(S["h_done"], 1)

            def scatter_rows(t, p):
                R = rows_of(t)
                po.wait_ge(S["rows_done"], t + 1)
                if isinstance(t, int) and t == 0:
                    po.wait_ge(S["pads_out"], 16 * SWEEPS)
                settle(po)
                for k in range(2):
                    g.indirect_dma_start(list_d.rearrange("p e w -> (p e) w"),
                                         bass.IndirectOffsetOnAxis(ap=row[p][0:R, k, 0:1], axis=0),
                                         entry[p][0:R, k, :], None, bounds_check=SWEEPS * P * NE - 1,
                                         oob_is_err=False).then_inc(ent_s[p], 16)

            def body3(t, p):
                if is_tile(t + 1, NT):
                    squares(t + 1, 1 - p)
                if is_tile(t - 3, NT):
                    scatter_rows(t - 3, 1 - p)
                if is_tile(t, NT):
                    layer1(t, p)

            po.wait_ge(S["o_done"], 9 * (HM + HD))
            for t in (-1, 0, 1, 2):
                body3(t, t % 2)
            with po.Fori(0, 2) as i:
                ch.enter(i, 6)
                body3(3 + 2 * i, 1)
                body3(4 + 2 * i, 0)
            ch.leave(2)
            for t in range(7, NT + 4):
                body3(t, t % 2)

            def gather(e, s, lots):
                p = s % 2
                po.wait_ge(tab_s[s], lots * 16)
                need(po, S["hgT_made"], 2 * (e - 1))
                settle(po)
                g.indirect_dma_start(hg[p][:], None, h_d, bass.IndirectOffsetOnAxis(ap=tab[s][:, 0:1], axis=0),
                                     bounds_check=TOK - 1, oob_is_err=False).then_inc(hg_s[p], 16)

            def scatter(e, s):
                p = s % 2
                po.wait_ge(S["y_lo"], e + 1)
                po.wait_ge(S["y_hi"], e + 1)
                settle(po)
                g.indirect_dma_start(pair_d, bass.IndirectOffsetOnAxis(ap=tab[s][:, 1:2], axis=0), y[p][:], None,
                                     bounds_check=2 * TOK - 1, oob_is_err=False).then_inc(y_s[p], 16)

            po.wait_ge(S["hg_zero"], 1)
            po.wait_ge(h_st[0], 16 * 5)
            po.wait_ge(h_st[1], 16 * 4)
            po.wait_ge(S["swp_done"], 1)
            n = po.value_load(more[0:1, 0:1], min_val=0, max_val=SWEEPS - 1) + 1

            def body4(gr, first):
                for s in range(SLOTS):
                    e = gr * SLOTS + s
                    gather(e, s, gr + 1)
                    if not first or s >= 3:
                        scatter(e - 3, (s - 3) % SLOTS)

            body4(0, True)
            with po.Fori(1, n * (NE // SLOTS)) as gr:
                body4(gr, False)
            for k in (3, 2, 1):
                scatter(n * NE - k, SLOTS - k)

            po.wait_ge(S["ln2_in"], 32)
            for t in range(NT + 2):
                if t <= NT:
                    R, f = rows_of(t), t % NF
                    po.wait_ge(S["fstat"], t + 1)
                    g_ = rsqrt(frs[f][0:R, :], fmv[f][0:R, 1:2], fve[f][0:R, :], R, 1, 1.0, EPS_LN)
                    g_.then_inc(S["frstd"], 1)
                    po.wait_ge(S["frstd"], 2 * t + 1)
                    ch(g.tensor_tensor(fve[f][0:R, :], fmv[f][0:R, 0:1], frs[f][0:R, :], ALU.mult))
                    g.tensor_scalar(fve[f][0:R, :], fve[f][0:R, :], -1.0, None, ALU.mult).then_inc(S["frstd"], 1)
                if t >= 1:
                    R, f = rows_of(t - 1), (t - 1) % NF
                    po.wait_ge(S["fmul"], t)
                    g.tensor_tensor(y0[f][0:R, :], y1[f][0:R, :], b2b[0:R, :], ALU.add).then_inc(S["fin_done"], 1)




def const_table():
    c = np.zeros((P, C_N), np.float32)
    c[:, C_ID:C_ID + P] = np.eye(P)
    c[:, C_TRI:C_TRI + P] = np.triu(np.ones((P, P)), 1)
    c[:, C_ONE:C_ONE + P] = 1
    c[:, C_IOTA:C_IOTA + NE] = np.arange(NE)
    c[:, C_DESC:C_DESC + 8] = 8 - np.arange(8)
    c[:, C_TOK:C_TOK + 9] = np.arange(P)[:, None] + P * np.arange(9)
    c[:, C_HALF:C_HALF + 9] = -0.5
    c[:, C_THR:C_THR + 8] = P * (1 + np.arange(8))
    return c


def rope_table():
    pos = np.concatenate([np.arange(SEQ), PAST + np.arange(DEC)]).astype(np.float32)
    cols = []
    for r in (ROPE, ROT):
        inv = np.float32(500000.0) ** (-np.arange(0, r, 2, dtype=np.float32) / np.float32(r))
        ang = pos[:, None] * inv.astype(np.float32)
        cols += [np.cos(ang), np.sin(ang)]
    return np.concatenate(cols, 1).astype(np.float32)


_OUTS = [("y_prompt", (1, SEQ, D)), ("y_sample", (1, DEC, D)),
         ("new_ckv_p", (1, 1, SEQ, KVR)), ("new_kpe_p", (1, 1, SEQ, ROPE)),
         ("new_dk_p", (1, 1, SEQ, HD, 2 * DD)), ("new_dv_p", (1, 1, SEQ, HD, VD)),
         ("new_ckv_s", (1, 1, DEC, KVR)), ("new_kpe_s", (1, 1, DEC, ROPE)),
         ("new_dk_s", (1, 1, DEC, HD, 2 * DD)), ("new_dv_s", (1, 1, DEC, HD, VD))]


def kernel(**inputs):
    import numpy as _np
    import concourse.bacc as _bacc
    from concourse import mybir as _mybir
    from concourse.bass_utils import run_bass_kernel_spmd as _run

    nc = _bacc.Bacc("TRN2", target_bir_lowering=False, num_devices=1)
    arrays, args, outs = {}, {}, {}
    given = dict(inputs)
    given["const_table"] = const_table()
    given["rope_table"] = rope_table()
    for name, value in given.items():
        v = _np.ascontiguousarray(value)
        arrays[f"in_{name}"] = v
        args[name] = nc.dram_tensor(f"in_{name}", v.shape, _mybir.dt.from_np(v.dtype), kind="ExternalInput").ap()
    for name, shape in _OUTS:
        outs[name] = nc.dram_tensor(f"out_{name}", shape, F32, kind="ExternalOutput").ap()
    build(nc, args, outs)
    r = _run(nc, [arrays], core_ids=[0])
    return tuple(r.results[0][f"out_{name}"] for name, _ in _OUTS)
```

```python
from contextlib import ExitStack

import concourse.bass as bass
import numpy as np
from concourse import mybir

F32 = mybir.dt.float32
U32 = mybir.dt.uint32
I32 = mybir.dt.int32
ALU = mybir.AluOpType
ACT = mybir.ActivationFunctionType
AX = mybir.AxisListType

P = 128
D = 1024
KD = D // P
SEQ, DEC, PAST = 1024, 64, 256
NT = SEQ // P
TOK = SEQ + DEC
KEYS = SEQ + PAST + DEC
QR = KVR = 256
ROPE = 32
NOPE = 64
HM, QD, VM = 8, NOPE + ROPE, 64
HD, DD, VD, ROT = 4, 64, 128, 16
IN_COLS = QR + KVR + ROPE + 3 * HD * 2 * DD
ZC = [(0, 512), (512, 32), (544, 512), (1056, 512), (1568, 512)]
MLA_SCALE = float(QD) ** -0.5
DIFF_SCALE = float(DD) ** -0.5
LAM_INIT = 0.8 - 0.6
ALPHA = 2.0 ** 0.25
EPS_LN, EPS_RMS = 1e-5, 1e-6
NG, EPG = 4, 8
NE = NG * EPG
FE = 256
NEG = -3.0e38
SLOTS = 4
TABS = 8
GROUPS = NE // TABS
SWEEPS = 9
PAD = 65535

C_ID, C_TRI, C_ONE, C_IOTA, C_DESC, C_TOK, C_HALF, C_THR = 0, 128, 256, 384, 416, 424, 433, 442
C_N = 450
ROPE_N = 2 * (ROPE // 2 + ROT // 2)


class Chain:

    def __init__(self, eng, sem):
        self.eng, self.sem, self.base, self.n = eng, sem, 0, 0

    def inc(self, ins):
        ins.then_inc(self.sem, 1)
        self.n += 1

    def wait(self):
        self.eng.wait_ge(self.sem, self.base + self.n)

    def __call__(self, ins):
        self.inc(ins)
        self.wait()

    def enter(self, i, per):
        self.start, self.per = self.base + self.n, per
        self.base, self.n = self.start + i * per, 0

    def leave(self, trips):
        assert self.n == self.per, self.n
        self.base, self.n = self.start + trips * self.per, 0


ORDER = [7, 6, 4, 8, 1, 0, 2, 3, 5]
BIG = [i for i in ORDER if 4 <= i < NT]
PAIR = 2 * len(ORDER)
MLA_TILES = HM * len(ORDER)


class Tile:

    def __init__(self, diff, j, k):
        if not diff and isinstance(j, int) and j == HM // 2 - 1 and k >= PAIR:
            diff, j, k = True, 0, k - PAIR
        turn, r = divmod(k, PAIR)
        self.exists = not isinstance(j, int) or (0 <= j + turn and not (diff and j + turn >= HD // 2))
        self.diff, self.j = diff, j + turn
        self.i = ORDER[r % 9]
        self.p, self.p6, self.hp = r % 2, r % 6, r // 9
        self.rows = DEC if self.i == NT else P
        self.keys = KEYS - SEQ if self.i == NT else (self.i + 1) * P
        self.blocks = (self.keys + P - 1) // P
        self.u = PAIR * j + k + (MLA_TILES if diff else 0)
        self.big = self.i in BIG
        bigs = sum(ORDER[x % 9] in BIG for x in range(r))
        self.bigs = 2 * len(BIG) * (j + turn) + bigs + (HM * len(BIG) if diff else 0)
        self.maps = 2 if diff else 1
        self.s = self.u if not diff else MLA_TILES + 2 * (PAIR * j + k)


def is_tile(t, last):
    return not isinstance(t, int) or 0 <= t <= last


def rows_of(t):
    return DEC if isinstance(t, int) and t == NT else P


def need(eng, sem, value):
    if not isinstance(value, int) or value > 0:
        eng.wait_ge(sem, value)


def build(nc, a, out):
    with ExitStack() as ctx:
        def dram(name, shape, dt=F32):
            return nc.dram_tensor(name, shape, dt, kind="Internal").ap()

        def sem(name):
            return ctx.enter_context(nc.semaphore(name))

        qT_d, kT_d = dram("qT_d", [HM, QD, TOK]), dram("kT_d", [HM, QD, KEYS])
        dqT_d, dkT_d = dram("dqT_d", [HD, P, TOK]), dram("dkT_d", [HD, P, KEYS])
        v_d = dram("v_d", [KEYS, HM * VM])
        h_d, pair_d = dram("h_d", [TOK, D]), dram("pair_d", [2 * TOK, D])
        list_d = dram("list_d", [SWEEPS * P, NE, 4], U32)

        top = [(nc.sbuf_base + 63) // 64 * 64]

        def place(at, name, shape, dt=F32):
            size = int(np.prod(shape[1:])) * 4
            t = nc.alloc_sbuf_tensor_at(name, shape, dt, offset=at[0])
            at[0] += (size + 31) // 32 * 32
            assert at[0] <= nc.sbuf_usable_end, (name, at[0])
            return t

        const = place(top, "const", [P, C_N])
        wgu, wdn = [None] * SLOTS, [None] * SLOTS
        ring_base = top[0]
        for s in range(2):
            wgu[s] = place(top, f"wgu{s}", [P, KD, 2 * FE])
            wdn[s] = place(top, f"wdn{s}", [P, FE // P, D])
        neglam = place(top, "neglam", [P, 1])
        region = top[0]

        m1 = [region]
        w_in = place(m1, "w_in_sb", [P, KD, IN_COLS])
        w_uq = place(m1, "w_uq_sb", [P, 2, HM * QD])
        w_ukv = place(m1, "w_ukv_sb", [P, 2, 2, HM * NOPE])
        gq, gkv = place(m1, "gq", [P, QR]), place(m1, "gkv", [P, KVR])
        lam4 = place(m1, "lam4", [P, 4, DD])
        lamt = place(m1, "lamt", [P, 2, DD])
        lams = place(m1, "lams", [P, 2])
        lame = place(m1, "lame", [P, 2])
        pad_rows = place(m1, "pad_rows", [P, NE * 4], U32)
        x_in = [place(m1, f"x_in{p}", [P, D]) for p in range(2)]
        rope = [place(m1, f"rope{p}", [P, ROPE_N]) for p in range(2)]
        xT = [place(m1, f"xT{p}", [P, KD, P]) for p in range(2)]
        zqk = [place(m1, f"zqk{p}", [P, 2, 2 * HD, DD]) for p in range(2)]
        zv = [place(m1, f"zv{p}", [P, HD * VD]) for p in range(2)]
        kr = [place(m1, f"kr{p}", [P, ROPE]) for p in range(2)]
        cqn = [place(m1, f"cqn{p}", [P, QR]) for p in range(2)]
        ckvn = [place(m1, f"ckvn{p}", [P, KVR]) for p in range(2)]
        cT = [place(m1, f"cT{p}", [P, 4, P]) for p in range(2)]
        qs = [place(m1, f"qs{p}", [P, HM, QD]) for p in range(2)]
        kpT = [place(m1, f"kpT{p}", [ROPE, P]) for p in range(2)]
        dT = [place(m1, f"dT{p}", [P, 2, HD, P]) for p in range(2)]
        qT = [place(m1, f"qT{p}", [QD, HM, P]) for p in range(2)]
        knT = [place(m1, f"knT{p}", [P, HM // 2, P]) for p in range(2)]
        vs = [place(m1, f"vs{p}", [P, HM * VM]) for p in range(2)]
        junk = place(m1, "junk", [P, 2, QR])
        ss = [place(m1, f"ss{p}", [P, 2]) for p in range(2)]
        ms = [place(m1, f"ms{p}", [P, 2]) for p in range(2)]
        rq = [place(m1, f"rq{p}", [P, 2]) for p in range(2)]
        rt4 = [place(m1, f"rt4{n}", [P, 4, (ROPE // 2, P, P)[n]]) for n in range(3)]

        m2 = [region]
        merged = place(m2, "merged", [P, NT + 1, D])
        m3 = list(m2)
        w_o = place(m3, "w_o_sb", [P, KD, D])
        m4 = list(m3)
        hi = [nc.sbuf_usable_end - (KD * 2 * FE + 2 * D) * 4 - 64]
        hi[0] = hi[0] // 64 * 64
        hi_base = hi[0]
        wgu[2] = place(hi, "wgu2", [P, KD, 2 * FE])
        wdn[2] = place(hi, "wdn2", [P, FE // P, D])
        hq = [place(m3, f"hq{p}", [P, TOK]) for p in range(2)]
        hk = [place(m3, f"hk{p}", [P, KEYS]) for p in range(2)]
        hv = [place(m3, f"hv{p}", [P, 11, VD]) for p in range(2)]
        pr = [[place(m3, f"pr{p}{m}", [P, SEQ]) for m in range(2)] for p in range(2)]
        pT = [place(m3, f"pT{p}", [P, NT, P]) for p in range(2)]
        nmax = [place(m3, f"nmax{p}", [P, 1]) for p in range(2)]
        rsum = [place(m3, f"rsum{p}", [P, 2]) for p in range(2)]
        psums = [[place(m3, f"psums{p}{m}", [P, 1]) for m in range(2)] for p in range(6)]
        mixc = [place(m3, f"mixc{p}", [P, 1]) for p in range(2)]
        assert m3[0] <= hi_base, (m3[0], hi_base)
        xr = [place(m4, f"xr{p}", [P, D]) for p in range(2)]
        mT = [place(m4, f"mT{p}", [P, KD, P]) for p in range(2)]
        r1 = [place(m4, f"r1{p}", [P, D]) for p in range(2)]
        hT = [place(m4, f"hT{p}", [P, KD, P]) for p in range(2)]
        g1b, b1b = place(m4, "g1b", [P, D]), place(m4, "b1b", [P, D])
        mst = [place(m4, f"mst{p}", [P, D]) for p in range(2)]
        subln = place(m4, "subln", [P, 2])
        w_r = place(m4, "w_r_sb", [P, KD, NG + NE])
        b_r = place(m4, "b_r_sb", [P, NG + NE])
        sqj = [place(m4, f"sqj{p}", [P, HD, VD]) for p in range(2)]
        m4s = [[place(m4, f"{n}{p}", [P, HD]) for n in ("hsq", "hms", "hrs")] for p in range(2)]
        bst = [place(m4, f"bst{p}", [P, 2, 6]) for p in range(2)]
        mv = [place(m4, f"mv{p}", [P, 2]) for p in range(2)]
        ve = [place(m4, f"ve{p}", [P, 1]) for p in range(2)]
        rst = [place(m4, f"rst{p}", [P, 1]) for p in range(2)]
        lg = place(m4, "lg", [P, NG + NE])
        top1 = place(m4, "top1", [P, 8])
        wgt = place(m4, "wgt", [P, 8])
        ohg = place(m4, "ohg", [P, NG])
        ein8 = place(m4, "ein8", [P, 2, EPG])
        emul = place(m4, "emul", [P, NG, EPG])
        ohe = place(m4, "ohe", [P, 2, EPG])
        shifted = [place(m4, f"shifted{p}", [P, 8]) for p in range(2)]
        exped = [place(m4, f"exped{p}", [P, 8]) for p in range(2)]
        oh32 = [place(m4, f"oh32{p}", [P, 2, NE]) for p in range(2)]
        picks = [place(m4, f"picks{p}", [P, NE]) for p in range(2)]
        before = [place(m4, f"before{p}", [P, NE]) for p in range(2)]
        gates = [place(m4, f"gates{p}", [P, 4]) for p in range(2)]
        where = place(m4, "where", [P, NE])
        where2 = place(m4, "where2", [P, 2, NE])
        rowf = place(m4, "rowf", [P, 2])
        row = [place(m4, f"row{p}", [P, 2, 1], U32) for p in range(2)]
        entry = [place(m4, f"entry{p}", [P, 2, 4], U32) for p in range(2)]
        cntm = place(m4, "cntm", [P, 1])
        over = place(m4, "over", [P, 8])
        nover = place(m4, "nover", [P, 1])
        assert m4[0] <= hi_base, (m4[0], hi_base)
        m5 = list(m2)
        wgu[3] = place(m5, "wgu3", [P, KD, 2 * FE])
        wdn[3] = place(m5, "wdn3", [P, FE // P, D])
        m5[0] = max(m5[0], m4[0])
        more = place(m5, "more", [P, 1], I32)
        tab = [place(m5, f"tab{s}", [P, 4], U32) for s in range(TABS)]
        m6 = [m2[0] + (KD * 2 * FE + 2 * D) * 4]
        hg = [place(m6, f"hg{p}", [P, D]) for p in range(2)]
        hgT = [place(m6, f"hgT{p}", [P, KD, P]) for p in range(2)]
        sil = [place(m6, f"sil{p}", [P, FE]) for p in range(2)]
        hid = [place(m6, f"hid{p}", [P, FE]) for p in range(2)]
        hidT = [place(m6, f"hidT{p}", [P, 2, P]) for p in range(2)]
        y = [place(m6, f"y{p}", [P, D]) for p in range(2)]
        g2b, b2b = place(m6, "g2b", [P, D]), place(m6, "b2b", [P, D])
        NF = NT + 1
        fst = [place(m6, f"fst{t}", [P, 2, 6]) for t in range(NF)]
        fmv = [place(m6, f"fmv{t}", [P, 2]) for t in range(NF)]
        fve = [place(m6, f"fve{t}", [P, 1]) for t in range(NF)]
        frs = [place(m6, f"frs{t}", [P, 1]) for t in range(NF)]
        assert m6[0] <= hi_base
        m7, m8 = [ring_base], [hi_base]
        yy = [place(m7 if t < 6 else m8, f"yy{t}", [P, 2, D]) for t in range(NF)]
        assert m7[0] <= region

        ps = ctx.enter_context(nc.psum_tensor("ps", [P, 8, 512], F32))
        ident = const[:, C_ID:C_ID + P]

        names = """const_in lam_in lam_prod lam_exp lam_done x_made rope_in wuq_in
            xT_made xT_copied z_made sq_done rms_done norm_done kr_copied dqk_copied dv_copied kr_roped dqk_roped
            cT_made kpT_made dT_made cT_copied kpT_copied dT_copied q_made kn_made v_made q_copied kn_copied
            v_copied q_roped qT_made qT_copied pads_set pads_out
            ch_dve ch_act ch_pool settled
            s_made max_done exp_done mix_done t_lo t_hi pT_lo pT_hi o_made o_done
            wo_in ph3_in sub_in hsq_done hrs_done md_done mT_made mT_copied op_made res_done ln_stat ln_rstd
            ln_mul h_done hT_made hT_copied lg_made shift_done exp3_done picks_done hm_done ent_free
            pre_made rows_done cnt_made swp_done before0
            hg_zero hgT_made hgT_copied gu_made silu_done hid_done hidT_made hidT_copied dn_made
            y_lo y_hi add_done fstat frstd fmul fin_done f_out fnorm ln2_in""".split()
        S = {n: sem(n) for n in names}
        x_in_s = [sem(f"x_in_s{p}") for p in range(2)]
        win_s = [sem(f"win_s{c}") for c in range(len(ZC))]
        cache_s = [sem(f"cache_s{p}") for p in range(2)]
        st_s = [sem(f"st_s{p}") for p in range(2)]
        head_s = [sem(f"head_s{p}") for p in range(2)]
        xr_s = [sem(f"xr_s{p}") for p in range(2)]
        h_st = [sem(f"h_st{p}") for p in range(2)]
        ent_s = [sem(f"ent_s{p}") for p in range(2)]
        w_s = [sem(f"w_s{s}") for s in range(SLOTS)]
        tab_s = [sem(f"tab_s{s}") for s in range(TABS)]
        hg_s = [sem(f"hg_s{p}") for p in range(2)]
        y_s = [sem(f"y_s{p}") for p in range(2)]
        f_in = [sem(f"f_in{p}") for p in range(NF)]

        FULL_ST = 16 * 11

        block = ctx.enter_context(nc.Block())

        def settle(eng):
            eng.sem_inc(S["settled"], 1)

        def key_col(t):
            return SEQ + PAST if isinstance(t, int) and t == NT else t * P

        @block.sync
        def _(sp):
            def load_x(t, p):
                need(sp, S["xT_made"], t - 1)
                if not isinstance(t, int) or t >= 2:
                    sp.wait_ge(S["q_roped"], t - 1)
                R = rows_of(t)
                src = a["x_sample"][0] if R == DEC else a["x_prompt"][0, bass.ds(t * P, P), :]
                sp.dma_start(x_in[p][0:R, :], src).then_inc(x_in_s[p], 16)
                sp.dma_start(rope[p][0:R, :], a["rope_table"][bass.ds(t * P, R), :]).then_inc(x_in_s[p], 16)

            def store_early(t, p):
                R, last = rows_of(t), isinstance(t, int) and t == NT

                def row(name):
                    dst = out["new_" + name + ("_s" if last else "_p")][0, 0]
                    return dst if last else dst[bass.ds(t * P, P)]

                sp.wait_ge(S["norm_done"], 1 + t)
                sp.dma_start(row("ckv"), ckvn[p][0:R, :]).then_inc(st_s[p], 16)
                sp.wait_ge(S["kr_roped"], 1 + t)
                sp.dma_start(row("kpe"), kr[p][0:R, :]).then_inc(st_s[p], 16)
                sp.wait_ge(S["dv_copied"], 1 + t)
                sp.dma_start(row("dv").rearrange("t h v -> t (h v)"), zv[p][0:R, :]).then_inc(st_s[p], 16)
                sp.wait_ge(S["dqk_roped"], 1 + t)
                sp.dma_start(row("dk").rearrange("t h v -> t (h v)"),
                             zqk[p][0:R, 1].rearrange("p h d -> p (h d)")).then_inc(st_s[p], 16)

            def store_keys(t, p, R, col):
                sp.wait_ge(S["kpT_copied"], 1 + t)
                src = kpT[p][:, 0:R].unsqueeze(1).broadcast_to([ROPE, HM, R])
                sp.dma_start(kT_d[:, NOPE:QD, bass.ds(col, R)].rearrange("h d k -> d h k"), src).then_inc(st_s[p], 16)
                sp.wait_ge(S["kn_copied"], 1 + t)
                settle(sp)
                for half in range(2):
                    sp.dma_start(kT_d[half::2, 0:NOPE, bass.ds(col, R)].rearrange("h d k -> d h k"),
                                 knT[p][NOPE * half:NOPE * (half + 1), :, 0:R]).then_inc(st_s[p], 16)
                sp.wait_ge(S["v_copied"], 1 + t)
                sp.dma_start(v_d[bass.ds(col, R), :], vs[p][0:R, :]).then_inc(st_s[p], 16)
                sp.wait_ge(S["dT_copied"], 1 + t)
                sp.dma_start(dkT_d[:, :, bass.ds(col, R)].rearrange("h d k -> d h k"),
                             dT[p][:, 1, :, 0:R]).then_inc(st_s[p], 16)

            def store_late(t, p):
                R = rows_of(t)
                store_keys(t, p, R, key_col(t))
                sp.dma_start(dqT_d[:, :, bass.ds(t * P, R)].rearrange("h d k -> d h k"),
                             dT[p][:, 0, :, 0:R]).then_inc(st_s[p], 16)
                sp.wait_ge(S["qT_copied"], 1 + t)
                sp.dma_start(qT_d[:, :, bass.ds(t * P, R)].rearrange("h d k -> d h k"),
                             qT[p][:, :, 0:R]).then_inc(st_s[p], 16)

            def load_expert(s, e):
                sp.dma_start(wgu[s][:, :, 0:FE], a["w_exp_gate"][0, bass.ds(e, 1)].rearrange(
                    "a (k p) f -> p (a k) f", p=P)).then_inc(w_s[s], 16)
                sp.dma_start(wgu[s][:, :, FE:2 * FE], a["w_exp_up"][0, bass.ds(e, 1)].rearrange(
                    "a (k p) f -> p (a k) f", p=P)).then_inc(w_s[s], 16)
                sp.dma_start(wdn[s][:], a["w_exp_down"][0, bass.ds(e, 1)].rearrange(
                    "a (k p) f -> p (a k) f", p=P)).then_inc(w_s[s], 16)

            sp.dma_start(const[:], a["const_table"]).then_inc(S["const_in"], 16)
            load_x(0, 0)
            w3 = a["w_in"][0].rearrange("(k p) c -> p k c", p=P)
            for c, (c0, n) in enumerate(ZC):
                sp.dma_start(w_in[:, :, c0:c0 + n], w3[:, :, c0:c0 + n]).then_inc(win_s[c], 16)
                if c == 0:
                    load_x(1, 1)
                    for dst, name in ((gq, "mla_q_norm"), (gkv, "mla_kv_norm")):
                        sp.dma_start(dst[:], a[name][0].partition_broadcast(P)).then_inc(S["rope_in"], 16)
                if c == 2:
                    sp.dma_start(w_uq[:], a["mla_w_uq"][0].rearrange("(k p) c -> p k c", p=P)).then_inc(S["wuq_in"], 16)
                    for k in range(2):
                        kv = a["mla_w_ukv"][0, k * P:(k + 1) * P].rearrange("p (h x c) -> p x h c", x=2, c=NOPE)
                        for x in range(2):
                            sp.dma_start(w_ukv[:, k, x].rearrange("p (h c) -> p h c", c=NOPE), kv[:, x]).then_inc(S["wuq_in"], 16)
            for n, name in enumerate(("q1", "k1", "q2", "k2")):
                sp.dma_start(lam4[:, n, :], a["diff_lambda_" + name][0].partition_broadcast(P)).then_inc(S["lam_in"], 16)
            sp.wait_ge(S["pads_set"], 1)
            for b in range(SWEEPS):
                sp.dma_start(list_d[b * P:(b + 1) * P].rearrange("p e w -> p (e w)"), pad_rows[:]).then_inc(S["pads_out"], 16)
            for s in range(2):
                load_expert(s, s)

            def body1(t, p):
                if is_tile(t + 1, NT) and not (isinstance(t, int) and t == 0):
                    load_x(t + 1, 1 - p)
                if is_tile(t, NT):
                    store_early(t, p)
                if is_tile(t - 1, NT):
                    store_late(t - 1, 1 - p)

            for t in range(3):
                body1(t, t % 2)
            with sp.Fori(0, 2) as i:
                body1(3 + 2 * i, 1)
                body1(4 + 2 * i, 0)
            body1(7, 1)
            body1(8, 0)
            for c in range(2):
                p, t = 1 - c, NT + 1 + c
                if c == 0:
                    sp.wait_ge(st_s[p], FULL_ST * 4)
                else:
                    store_late(NT, 0)
                    sp.wait_ge(st_s[p], FULL_ST * 5)
                rows = slice(c * P, (c + 1) * P)
                sp.dma_start(ckvn[p][:], a["cache_mla_ckv"][0, 0, rows]).then_inc(cache_s[p], 16)
                sp.dma_start(kr[p][:], a["cache_mla_kpe"][0, 0, rows]).then_inc(cache_s[p], 16)
                sp.dma_start(zqk[p][:, 1].rearrange("p h d -> p (h d)"),
                             a["cache_diff_k"][0, 0, rows].rearrange("t h d -> t (h d)")).then_inc(cache_s[p], 16)
            for c in range(2):
                store_keys(NT + 1 + c, 1 - c, P, SEQ + c * P)

            sp.wait_ge(st_s[1], FULL_ST * 4 + 5 * 16)
            sp.wait_ge(st_s[0], FULL_ST * 5 + 5 * 16)

            def load_mla(h, p):
                if not isinstance(h, int):
                    sp.wait_ge(S["o_made"], 2 + 9 * (h - 1))
                sp.dma_start(hq[p][0:QD, :], qT_d[bass.ds(h, 1)].rearrange("a d t -> (a d) t")).then_inc(head_s[p], 16)
                sp.dma_start(hk[p][0:QD, :], kT_d[bass.ds(h, 1)].rearrange("a d t -> (a d) t")).then_inc(head_s[p], 16)
                v = v_d[:, bass.ds(h * VM, VM)]
                sp.dma_start(hv[p][:, 0:10, 0:VM], v[0:10 * P].rearrange("(t p) v -> p t v", p=P)).then_inc(head_s[p], 16)
                sp.dma_start(hv[p][0:DEC, 10, 0:VM], v[10 * P:KEYS]).then_inc(head_s[p], 16)

            def load_diff(h, p):
                sp.wait_ge(S["o_made"], 2 + 9 * (HM + h - 1))
                sp.dma_start(hq[p][:], dqT_d[bass.ds(h, 1)].rearrange("a d t -> (a d) t")).then_inc(head_s[p], 16)
                sp.dma_start(hk[p][:], dkT_d[bass.ds(h, 1)].rearrange("a d t -> (a d) t")).then_inc(head_s[p], 16)
                for dst, src in ((hv[p][:, 0:NT, :], out["new_dv_p"]), (hv[p][:, NT:NT + 2, :], a["cache_diff_v"])):
                    sp.dma_start(dst, src[0, 0, :, bass.ds(h, 1), :].rearrange("(t p) a v -> p t (a v)", p=P)).then_inc(head_s[p], 16)
                sp.dma_start(hv[p][0:DEC, 10, :], out["new_dv_s"][0, 0, :, bass.ds(h, 1), :].rearrange("t a v -> t (a v)")).then_inc(head_s[p], 16)

            load_mla(0, 0)
            load_mla(1, 1)
            sp.dma_start(w_o[:], a["w_out"][0].rearrange("(k p) c -> p k c", p=P)).then_inc(S["wo_in"], 16)
            load_expert(2, 2)
            with sp.Fori(1, HM // 2) as i:
                load_mla(2 * i, 0)
                load_mla(2 * i + 1, 1)
            with sp.Fori(0, HD // 2) as i:
                load_diff(2 * i, 0)
                load_diff(2 * i + 1, 1)

            sp.wait_ge(S["o_done"], 2 + 9 * (HM + HD))
            sp.dma_start(subln[:, 0:1], a["diff_subln"][0].rearrange("(p a) -> p a", a=1)).then_inc(S["sub_in"], 16)
            for dst, name in ((g1b, "ln1_g"), (b1b, "ln1_b")):
                sp.dma_start(dst[:], a[name][0].partition_broadcast(P)).then_inc(S["ph3_in"], 16)
            sp.dma_start(w_r[:, :, 0:NG], a["w_route_group"][0].rearrange("(k p) c -> p k c", p=P)).then_inc(S["ph3_in"], 16)
            sp.dma_start(w_r[:, :, NG:NG + NE], a["w_route_expert"][0].rearrange("(k p) c -> p k c", p=P)).then_inc(S["ph3_in"], 16)
            sp.dma_start(b_r[:, 0:NG], a["b_route_group"][0].partition_broadcast(P)).then_inc(S["ph3_in"], 16)
            sp.dma_start(b_r[:, NG:NG + NE], a["b_route_expert"][0].partition_broadcast(P)).then_inc(S["ph3_in"], 16)

            def load_xr(t, p):
                need(sp, S["hT_made"], t - 1)
                need(sp, S["hm_done"], t - 1)
                R = rows_of(t)
                src = a["x_sample"][0] if R == DEC else a["x_prompt"][0, bass.ds(t * P, P), :]
                sp.dma_start(xr[p][0:R, :], src).then_inc(xr_s[p], 16)

            def body3(t, p):
                if is_tile(t + 1, NT):
                    load_xr(t + 1, 1 - p)
                if is_tile(t, NT):
                    R = rows_of(t)
                    sp.wait_ge(S["hm_done"], t + 1)
                    sp.dma_start(h_d[bass.ds(t * P, R), :], merged[0:R, bass.ds(t, 1), :].rearrange("p a d -> p (a d)")).then_inc(h_st[p], 16)

            for t in (-1, 0, 1):
                body3(t, t % 2)
            with sp.Fori(0, 2) as i:
                body3(2 + 2 * i, 0)
                body3(3 + 2 * i, 1)
            for t in range(6, NT + 1):
                body3(t, t % 2)
            sp.wait_ge(S["op_made"], NT + 1)
            load_expert(3, 3)
            sp.wait_ge(ent_s[0], 32 * 5)
            sp.wait_ge(ent_s[1], 32 * 4)

            def load_list(s, g):
                sweep, e = (0, s) if isinstance(g, int) else (g // GROUPS, (g % GROUPS) * TABS + s)
                sp.dma_start(tab[s][:], list_d[bass.ds(sweep * P, P), bass.ds(e, 1), :].rearrange(
                    "p a w -> p (a w)")).then_inc(tab_s[s], 16)

            for s in range(TABS):
                load_list(s, 0)
            sp.wait_ge(S["cnt_made"], 1)
            for dst, name in ((g2b, "ln2_g"), (b2b, "ln2_b")):
                sp.wait_ge(S["rows_done"], NT + 1)
                sp.dma_start(dst[:], a[name][0].partition_broadcast(P)).then_inc(S["ln2_in"], 16)
            sp.wait_ge(S["swp_done"], 1)
            n = sp.value_load(more[0:1, 0:1], min_val=0, max_val=SWEEPS - 1) + 1
            for s in range(SLOTS, TABS):
                sp.wait_ge(S["dn_made"], s - SLOTS + 1)
                load_expert(s % SLOTS, s)
            with sp.Fori(1, n * GROUPS) as g:
                for s in range(TABS):
                    e = g * TABS + s
                    sp.wait_ge(y_s[s % 2], (e - TABS) // 2 * 16 + 16)
                    load_list(s, g)
                    sp.wait_ge(S["dn_made"], e - SLOTS + 1)
                    load_expert(s % SLOTS, (g % GROUPS) * TABS + s)
            sp.wait_ge(y_s[0], n * (NE // 2) * 16)
            sp.wait_ge(y_s[1], n * (NE // 2) * 16)

            for t in range(NT + 1):
                R = rows_of(t)
                sp.dma_start(yy[t][0:R], pair_d.rearrange("(k n) d -> n k d", k=2)[t * P:t * P + R]).then_inc(f_in[t], 16)
            for t in range(NT + 1):
                R = rows_of(t)
                sp.wait_ge(S["fin_done"], t + 1)
                dst = out["y_sample"][0] if t == NT else out["y_prompt"][0, t * P:(t + 1) * P, :]
                sp.dma_start(dst, yy[t][0:R, 0, :]).then_inc(S["f_out"], 16)
            sp.wait_ge(S["f_out"], 16 * (NT + 1))

        @block.tensor
        def _(pe):
            def turn(bank, col, src, R, n):
                return pe.transpose(ps[0:n, bank, col:col + R], src, const[0:R, C_ID:C_ID + R])

            def xT_of(t, p):
                R = rows_of(t)
                pe.wait_ge(x_in_s[p], (t // 2 + 1) * 32)
                for half in range(2):
                    need(pe, S["kn_copied"] if half == 0 else S["v_copied"], t - 1)
                    for k in range(4):
                        mm = turn(4 + half, k * P, x_in[p][0:R, (4 * half + k) * P:(4 * half + k + 1) * P], R, P)
                mm.then_inc(S["xT_made"], 1)

            def z_of(t, p, c):
                R, (c0, n), bank = rows_of(t), ZC[c], (0, 1, 2, 3, 1)[c]
                if isinstance(t, int) and t == 0:
                    pe.wait_ge(win_s[c], 16)
                if c == 0:
                    pe.wait_ge(S["xT_copied"], t + 1)
                    need(pe, S["norm_done"], t)
                if c == 1:
                    need(pe, S["dv_copied"], t)
                if c == 2 or c == 3:
                    need(pe, S["dqk_copied"], t)
                if c == 4:
                    pe.wait_ge(S["kr_copied"], t + 1)
                for k in range(KD):
                    mm = pe.matmul(ps[0:R, bank, 0:n], xT[p][:, k, 0:R], w_in[:, k, c0:c0 + n],
                                   start=k == 0, stop=k == KD - 1)
                mm.then_inc(S["z_made"], 1)

            def turn_keys(t, p, R, heads):
                pe.wait_ge(S["norm_done"], t + 1) if heads else pe.wait_ge(cache_s[p], 48)
                if isinstance(t, int) and t > NT + 1:
                    pe.wait_ge(S["cT_copied"], t)
                else:
                    need(pe, S["qT_copied"], t)
                for c in range(0 if heads else 2, 4):
                    src = (cqn if c < 2 else ckvn)[p][0:R, (c % 2) * P:(c % 2 + 1) * P]
                    mm = turn(6, c * P, src, R, P)
                mm.then_inc(S["cT_made"], 1)
                if heads:
                    pe.wait_ge(S["kr_roped"], t + 1)
                    need(pe, S["xT_copied"], t + 1)
                    if is_tile(t + 1, NT):
                        pe.wait_ge(S["xT_copied"], t + 2)
                need(pe, S["v_copied"], t)
                turn(5, 0, kr[p][0:R, :], R, ROPE).then_inc(S["kpT_made"], 1)
                if heads:
                    pe.wait_ge(S["dqk_roped"], t + 1)
                need(pe, S["kn_copied"], t)
                for half, bank in ((0, 7), (1, 4)) if heads else ((1, 4),):
                    for h in range(HD):
                        mm = turn(bank, h * P, zqk[p][0:R, half, 2 * h:2 * h + 2, :].rearrange("p a d -> p (a d)"), R, P)
                mm.then_inc(S["dT_made"], 1)

            def expand(t, p, R, heads):
                pe.wait_ge(S["cT_copied"], t + 1)
                if isinstance(t, int) and t == 0:
                    pe.wait_ge(S["wuq_in"], 16 * 5)
                pe.wait_ge(S["dT_copied"], t + 1)
                if heads:
                    for half in range(2):
                        for k in range(2):
                            mm = pe.matmul(ps[0:R, 6 + half, 0:384], cT[p][:, k, 0:R], w_uq[:, k, 384 * half:384 * (half + 1)],
                                           start=k == 0, stop=k == 1)
                    mm.then_inc(S["q_made"], 1)
                for j in range(HM // 2):
                    for k in range(2):
                        mm = pe.matmul(ps[:, 4, j * P:j * P + R], w_ukv[:, k, 0, P * j:P * (j + 1)], cT[p][:, 2 + k, 0:R],
                                       start=k == 0, stop=k == 1)
                mm.then_inc(S["kn_made"], 1)
                pe.wait_ge(S["kpT_copied"], t + 1)
                for k in range(2):
                    mm = pe.matmul(ps[0:R, 5, :], cT[p][:, 2 + k, 0:R], w_ukv[:, k, 1, :],
                                   start=k == 0, stop=k == 1)
                mm.then_inc(S["v_made"], 1)

            def turn_q(t, p):
                R = rows_of(t)
                pe.wait_ge(S["q_roped"], t + 1)
                for h in range(HM):
                    mm = turn(6 + h // 4, (h % 4) * P, qs[p][0:R, h, :], R, QD)
                mm.then_inc(S["qT_made"], 1)

            def body1(t, p):
                cur, prev = is_tile(t, NT), is_tile(t - 1, NT)
                q, R1 = 1 - p, rows_of(t - 1)
                if cur:
                    z_of(t, p, 0)
                    z_of(t, p, 1)
                if prev:
                    turn_keys(t - 1, q, R1, True)
                if cur:
                    z_of(t, p, 2)
                if prev:
                    expand(t - 1, q, R1, True)
                if cur:
                    z_of(t, p, 3)
                if is_tile(t + 1, NT):
                    xT_of(t + 1, q)
                if cur:
                    z_of(t, p, 4)
                if prev:
                    turn_q(t - 1, q)

            pe.wait_ge(S["const_in"], 16)
            xT_of(0, 0)
            for t in range(3):
                body1(t, t % 2)
            with pe.Fori(0, 2) as i:
                body1(3 + 2 * i, 1)
                body1(4 + 2 * i, 0)
            body1(7, 1)
            body1(8, 0)
            body1(9, 1)
            for c in range(2):
                turn_keys(NT + 1 + c, 1 - c, P, False)
                expand(NT + 1 + c, 1 - c, P, False)

            def scores(a, maps):
                R, n0 = a.rows, (SEQ if a.i == NT else 0)
                width = DD if a.diff else QD
                for m in maps:
                    pair = m if a.diff else a.p
                    if m == 0 and a.i == ORDER[0]:
                        pe.wait_ge(head_s[a.hp], 64 * (HM // 2) + 80 * (a.j + 1) if a.diff else 64 * (a.j + 1))
                    need(pe, S["exp_done"], a.s + m - 1)
                    if a.i == NT:
                        settle(pe)
                    for c0 in range(0, a.keys, 512):
                        c1 = min(a.keys, c0 + 512)
                        mm = pe.matmul(ps[0:R, 2 * pair + c0 // 512, 0:c1 - c0], hq[a.hp][m * DD:m * DD + width, a.i * P:a.i * P + R],
                                       hk[a.hp][m * DD:m * DD + width, n0 + c0:n0 + c1], start=True, stop=True)
                    mm.then_inc(S["s_made"], 1)

            def turn_p(a):
                if a.diff:
                    pe.wait_ge(S["mix_done"], a.u - MLA_TILES + 1)
                else:
                    pe.wait_ge(S["exp_done"], a.s + 1)
                for half in range(2 if a.big else 1):
                    if half == 0:
                        need(pe, S["pT_lo"], a.u)
                    else:
                        need(pe, S["pT_hi"], a.bigs)
                    if a.i == NT:
                        settle(pe)
                    for b in range(4 * half, min(a.blocks, 4 * half + 4)):
                        w = min(P, a.keys - b * P)
                        mm = turn(4 + half, (b % 4) * P, pr[a.p][0][0:a.rows, b * P:b * P + w], a.rows, w)
                    mm.then_inc(S["t_hi" if half else "t_lo"], 1)

            def values(a):
                V = VD if a.diff else VM
                pe.wait_ge(S["o_done"], a.u + 1)
                pe.wait_ge(S["pT_lo"], a.u + 1)
                if a.big:
                    pe.wait_ge(S["pT_hi"], a.bigs + 1)
                for b in range(a.blocks):
                    w = min(P, a.keys - b * P)
                    vb = NT + b if a.i == NT else b
                    mm = pe.matmul(ps[0:a.rows, 6 + a.p, 0:V], pT[a.p][0:w, b, 0:a.rows], hv[a.hp][0:w, vb, 0:V],
                                   start=b == 0, stop=b == a.blocks - 1)
                mm.then_inc(S["o_made"], 1)

            def step2(diff, j, k):
                a, b, one, two = (Tile(diff, j, k + n) for n in (0, 2, 4, 3))
                if one.exists and not one.diff:
                    scores(one, (0,))
                if two.exists and two.diff:
                    scores(two, (0,))
                if a.exists:
                    values(a)
                if two.exists and two.diff:
                    scores(two, (1,))
                if b.exists:
                    turn_p(b)

            pe.wait_ge(S["qT_copied"], NT + 1)
            pe.wait_ge(S["v_copied"], NT + 3)
            pe.wait_ge(S["kn_copied"], NT + 3)
            pe.sem_inc(S["o_made"], 2)
            for k in range(-4, 0):
                step2(False, 0, k)
            with pe.Fori(0, HM // 2 - 1) as j:
                for k in range(PAIR):
                    step2(False, j, k)
            for k in range(PAIR):
                step2(False, HM // 2 - 1, k)
            for j in range(HD // 2):
                for k in range(PAIR):
                    step2(True, j, k)

            def mT_of(t, p):
                R = rows_of(t)
                pe.wait_ge(S["md_done"], t + 1)
                need(pe, S["mT_copied"], t)
                for k in range(KD):
                    mm = turn(4 + k // 4, (k % 4) * P, mst[p][0:R, k * P:(k + 1) * P], R, P)
                mm.then_inc(S["mT_made"], 1)

            def project(t, p):
                R = rows_of(t)
                pe.wait_ge(S["mT_copied"], t + 1)
                need(pe, S["res_done"], t - 1)
                for half in range(2):
                    for k in range(KD):
                        mm = pe.matmul(ps[0:R, 2 * p + half, :], mT[p][:, k, 0:R], w_o[:, k, 512 * half:512 * (half + 1)],
                                       start=k == 0, stop=k == KD - 1)
                mm.then_inc(S["op_made"], 1)

            def hT_of(t, p):
                R = rows_of(t)
                pe.wait_ge(S["h_done"], t + 1)
                need(pe, S["shift_done"], t)
                for k in range(KD):
                    mm = turn(6 + k // 4, (k % 4) * P, hrow[p][0:R, k * P:(k + 1) * P], R, P)
                mm.then_inc(S["hT_made"], 1)

            hrow = xr

            def route(t, p):
                R = rows_of(t)
                pe.wait_ge(S["hT_copied"], t + 1)
                if isinstance(t, int) and t == 0:
                    pe.wait_ge(S["ph3_in"], 16 * 6)
                for k in range(KD):
                    mm = pe.matmul(ps[0:R, 6, 0:NG + NE], hT[p][:, k, 0:R], w_r[:, k, :], start=k == 0, stop=k == KD - 1)
                mm.then_inc(S["lg_made"], 1)

            def positions(t, p):
                R = rows_of(t)
                pe.wait_ge(S["picks_done"], t + 1)
                pe.matmul(ps[0:R, 7, 0:NE], const[0:R, C_TRI:C_TRI + R], picks[p][0:R, :], start=True, stop=False)
                pe.matmul(ps[0:R, 7, 0:NE], const[:, C_ONE:C_ONE + R], before[p][:], start=False, stop=True).then_inc(S["pre_made"], 1)

            def body3(t, p):
                if is_tile(t, NT):
                    project(t, p)
                if is_tile(t - 1, NT):
                    hT_of(t - 1, 1 - p)
                if is_tile(t + 1, NT):
                    mT_of(t + 1, 1 - p)
                if is_tile(t - 1, NT):
                    route(t - 1, 1 - p)
                if is_tile(t - 2, NT):
                    positions(t - 2, p)

            pe.wait_ge(S["o_done"], 2 + 9 * (HM + HD))
            pe.wait_ge(S["wo_in"], 16)
            for t in (-2, -1, 0, 1):
                body3(t, t % 2)
            with pe.Fori(0, 2) as i:
                body3(2 + 2 * i, 0)
                body3(3 + 2 * i, 1)
            for t in range(6, NT + 3):
                body3(t, t % 2)
            pe.wait_ge(S["rows_done"], NT + 1)
            pe.matmul(ps[:, 6, 0:NE], const[:, C_ONE:C_ONE + P], before[(NT + 1) % 2][:], start=True, stop=True).then_inc(S["cnt_made"], 1)

            def rows_turned(e, s):
                p = s % 2
                pe.wait_ge(hg_s[p], (e // 2 + 1) * 16)
                need(pe, S["hgT_copied"], 2 * e)
                for k in range(KD):
                    mm = turn(2 + k // 4, (k % 4) * P, hg[p][:, k * P:(k + 1) * P], P, P)
                    if k % 4 == 3:
                        mm.then_inc(S["hgT_made"], 1)

            def gate_up(e, s, g):
                p, w = s % 2, s % SLOTS
                pe.wait_ge(w_s[w], (g * (TABS // SLOTS) + s // SLOTS + 1) * 48)
                pe.wait_ge(S["hgT_copied"], 2 * e + 2)
                need(pe, S["hid_done"], e - 1)
                for k in range(KD):
                    mm = pe.matmul(ps[:, p, :], hgT[p][:, k, :], wgu[w][:, k, :], start=k == 0, stop=k == KD - 1)
                mm.then_inc(S["gu_made"], 1)

            def hidden_turned(e, s):
                p = s % 2
                pe.wait_ge(S["hid_done"], e + 1)
                need(pe, S["hidT_copied"], e)
                for k in range(2):
                    mm = turn(4, k * P, hid[p][:, k * P:(k + 1) * P], P, P)
                mm.then_inc(S["hidT_made"], 1)

            def down(e, s):
                p = s % 2
                pe.wait_ge(S["hidT_copied"], e + 1)
                need(pe, S["y_lo"], e)
                need(pe, S["y_hi"], e)
                for half in range(2):
                    for k in range(2):
                        mm = pe.matmul(ps[:, 5 + half, :], hidT[p][:, k, :], wdn[s % SLOTS][:, k, 512 * half:512 * (half + 1)],
                                       start=k == 0, stop=k == 1)
                mm.then_inc(S["dn_made"], 1)

            def body4(g, first):
                for s in range(TABS):
                    e = g * TABS + s
                    rows_turned(e, s)
                    if not first or s >= 2:
                        down(e - 2, (s - 2) % TABS)
                    if not first or s >= 1:
                        hidden_turned(e - 1, (s - 1) % TABS)
                    gate_up(e, s, g)

            pe.wait_ge(S["swp_done"], 1)
            n = pe.value_load(more[0:1, 0:1], min_val=0, max_val=SWEEPS - 1) + 1
            body4(0, True)
            with pe.Fori(1, n * GROUPS) as g:
                body4(g, False)
            E = n * NE
            down(E - 2, TABS - 2)
            hidden_turned(E - 1, TABS - 1)
            down(E - 1, TABS - 1)

        @block.scalar
        def _(act):
            def copy(dst, src, scale=None):
                return nc.scalar.activation(dst, src, ACT.Copy, scale=1.0 if scale is None else scale)

            def xT_copy(t, p):
                R = rows_of(t)
                act.wait_ge(S["xT_made"], t + 1)
                need(act, S["z_made"], 5 * (t - 1))
                ins = copy(xT[p][:, :, 0:R], ps[:, 4:6, :].rearrange("p b (k r) -> p (b k) r", r=P)[:, :, 0:R])
                ins.then_inc(S["xT_copied"], 1)

            def latents(t, p):
                R = rows_of(t)
                act.wait_ge(S["z_made"], 5 * t + 1)
                need(act, S["rms_done"], t - 1)
                for c in range(2):
                    ins = nc.scalar.activation(junk[0:R, c, :], ps[0:R, 0, 256 * c:256 * (c + 1)], ACT.Square,
                                               accum_out=ss[p][0:R, c:c + 1])
                ins.then_inc(S["sq_done"], 1)

            def keep(t, p, c):
                R = rows_of(t)
                act.wait_ge(S["z_made"], 5 * t + c + 1)
                if c == 1:
                    need(act, st_s[p], FULL_ST * (t // 2))
                    need(act, S["kpT_made"], t - 1)
                    copy(kr[p][0:R, :], ps[0:R, 1, 0:ROPE]).then_inc(S["kr_copied"], 1)
                elif c in (2, 3):
                    if c == 2:
                        need(act, S["dT_made"], t - 1)
                    ins = copy(zqk[p][0:R, c - 2].rearrange("p h d -> p (h d)"), ps[0:R, c, :],
                               DIFF_SCALE if c == 2 else None)
                    if c == 3:
                        ins.then_inc(S["dqk_copied"], 1)
                else:
                    copy(zv[p][0:R, :], ps[0:R, 1, :]).then_inc(S["dv_copied"], 1)

            def cT_copy(t, p, R, c0):
                act.wait_ge(S["cT_made"], t + 1)
                need(act, S["v_made"], t - 1)
                copy(cT[p][:, c0:4, 0:R], ps[:, 6, :].rearrange("p (k r) -> p k r", r=P)[:, c0:4, 0:R]).then_inc(S["cT_copied"], 1)

            def q_copy(t, p):
                R = rows_of(t)
                act.wait_ge(S["q_made"], t + 1)
                need(act, S["qT_made"], t - 1)
                copy(qs[p][0:R].rearrange("p (a h) d -> p a (h d)", a=2), ps[0:R, 6:8, 0:384], MLA_SCALE).then_inc(S["q_copied"], 1)

            def v_copy(t, p, R):
                act.wait_ge(S["v_made"], t + 1)
                if isinstance(t, int) and t > NT:
                    act.wait_ge(st_s[p], FULL_ST * (4 if p else 5))
                copy(vs[p][0:R, :], ps[0:R, 5, :]).then_inc(S["v_copied"], 1)

            def qT_copy(t, p):
                R = rows_of(t)
                act.wait_ge(S["qT_made"], t + 1)
                copy(qT[p][:, :, 0:R], ps[0:QD, 6:8, :].rearrange("p b (k r) -> p (b k) r", r=P)[:, :, 0:R]).then_inc(S["qT_copied"], 1)

            def body1(t, p):
                cur, prev = is_tile(t, NT), is_tile(t - 1, NT)
                q, R1 = 1 - p, rows_of(t - 1)
                if cur:
                    latents(t, p)
                    keep(t, p, 1)
                if prev:
                    cT_copy(t - 1, q, R1, 0)
                if cur:
                    keep(t, p, 2)
                if prev:
                    q_copy(t - 1, q)
                    v_copy(t - 1, q, R1)
                if cur:
                    keep(t, p, 3)
                if is_tile(t + 1, NT):
                    xT_copy(t + 1, q)
                if cur:
                    keep(t, p, 4)
                if prev:
                    qT_copy(t - 1, q)

            ch = Chain(act, S["ch_act"])
            xT_copy(0, 0)
            act.wait_ge(S["lam_prod"], 1)
            nc.scalar.activation(lame[:], lams[:], ACT.Exp).then_inc(S["lam_exp"], 1)
            for t in range(3):
                body1(t, t % 2)
            with act.Fori(0, 2) as i:
                body1(3 + 2 * i, 1)
                body1(4 + 2 * i, 0)
            body1(7, 1)
            body1(8, 0)
            body1(9, 1)
            for c in range(2):
                cT_copy(NT + 1 + c, 1 - c, P, 2)
                v_copy(NT + 1 + c, 1 - c, P)

            def exps(a, last):
                for m in range(a.maps):
                    pair = m if a.diff else a.p
                    act.wait_ge(S["max_done"], a.s + m + 1)
                    if m == 0 and (not isinstance(a.u, int) or a.u >= 2):
                        act.wait_ge(S["t_lo"], last.u + 1)
                        if last.big:
                            act.wait_ge(S["t_hi"], last.bigs + 1)
                        need(act, S["o_done"], a.u - 1)
                    sc = ps[0:a.rows, 2 * pair:2 * pair + 2, :].rearrange("p b c -> p (b c)")[:, 0:a.keys]
                    nc.scalar.activation(pr[a.p][m][0:a.rows, 0:a.keys], sc, ACT.Exp, bias=nmax[pair][0:a.rows, :],
                                         accum_out=psums[a.p6][m][0:a.rows, :]).then_inc(S["exp_done"], 1)

            def pT_copy(a):
                act.wait_ge(S["t_lo"], a.u + 1)
                act.wait_ge(S["o_made"], a.u + 1)
                src = ps[:, 4, :].rearrange("p (k r) -> p k r", r=P)
                if a.i == NT:
                    copy(pT[a.p][:, 0:2, 0:a.rows], src[:, 0:2, 0:a.rows])
                    copy(pT[a.p][0:DEC, 2, 0:a.rows], src[0:DEC, 2, 0:a.rows]).then_inc(S["pT_lo"], 1)
                else:
                    w = min(4, a.blocks)
                    copy(pT[a.p][:, 0:w, :], src[:, 0:w, :]).then_inc(S["pT_lo"], 1)

            def step2(diff, j, k):
                a, b = Tile(diff, j, k + 1), Tile(diff, j, k + 3)
                if a.exists:
                    pT_copy(a)
                if b.exists:
                    exps(b, a)

            for k in (-3, -2, -1):
                step2(False, 0, k)
            with act.Fori(0, HM // 2 - 1) as j:
                for k in range(PAIR):
                    step2(False, j, k)
            for k in range(PAIR):
                step2(False, HM // 2 - 1, k)
            for j in range(HD // 2):
                for k in range(PAIR):
                    step2(True, j, k)

            def head_squares(t, p):
                R = rows_of(t)
                need(act, S["hrs_done"], t - 1)
                for h in range(HD):
                    d = merged[0:R, bass.ds(t, 1), (HM * VM + h * VD):(HM * VM + (h + 1) * VD)].rearrange("p a v -> p (a v)")
                    ins = nc.scalar.activation(sqj[p][0:R, h, :], d, ACT.Square, accum_out=m4s[p][0][0:R, h:h + 1])
                ins.then_inc(S["hsq_done"], 1)

            def hT_copy(t, p):
                R = rows_of(t)
                act.wait_ge(S["hT_made"], t + 1)
                copy(hT[p][:, :, 0:R], ps[:, 6:8, :].rearrange("p b (k r) -> p (b k) r", r=P)[:, :, 0:R]).then_inc(S["hT_copied"], 1)

            def mT_copy(t, p):
                R = rows_of(t)
                act.wait_ge(S["mT_made"], t + 1)
                need(act, S["op_made"], t - 1)
                src = ps[:, 4:6, :].rearrange("p b (k r) -> p b k r", r=P)
                copy(mT[p][:, 0:4, 0:R], src[:, 0, :, 0:R])
                copy(mT[p][:, 4:8, 0:R], src[:, 1, :, 0:R], subln[:, 1:2]).then_inc(S["mT_copied"], 1)

            def h_copy(t, p):
                R = rows_of(t)
                act.wait_ge(S["h_done"], t + 1)
                copy(merged[0:R, bass.ds(t, 1), :].rearrange("p a d -> p (a d)"), xr[p][0:R, :]).then_inc(S["hm_done"], 1)

            def gate_exps(t, p):
                R = rows_of(t)
                act.wait_ge(S["shift_done"], t + 1)
                nc.scalar.activation(exped[p][0:R, 0:5], shifted[p][0:R, 0:5], ACT.Exp).then_inc(S["exp3_done"], 1)

            def body3(t, p):
                if is_tile(t + 2, NT):
                    head_squares(t + 2, p)
                if is_tile(t - 1, NT):
                    hT_copy(t - 1, 1 - p)
                if is_tile(t + 1, NT):
                    mT_copy(t + 1, 1 - p)
                if is_tile(t, NT):
                    h_copy(t, p)
                if is_tile(t - 1, NT):
                    gate_exps(t - 1, 1 - p)

            act.wait_ge(S["o_done"], 2 + 9 * (HM + HD))
            act.wait_ge(S["sub_in"], 16)
            ch(copy(subln[:, 1:2], subln[:, 0:1], 1.0 - LAM_INIT))
            for t in (-2, -1, 0, 1):
                body3(t, t % 2)
            with act.Fori(0, 2) as i:
                body3(2 + 2 * i, 0)
                body3(3 + 2 * i, 1)
            for t in range(6, NT + 3):
                body3(t, t % 2)

            def rows_copy(e, s):
                p = s % 2
                act.wait_ge(S["hgT_made"], 2 * e + 1)
                need(act, S["gu_made"], e - 1)
                copy(hgT[p][:, 0:4, :], ps[:, 2, :].rearrange("p (k r) -> p k r", r=P)).then_inc(S["hgT_copied"], 1)

            def silu(e, s):
                p = s % 2
                act.wait_ge(S["gu_made"], e + 1)
                need(act, S["hid_done"], e - 1)
                nc.scalar.activation(sil[p][:], ps[:, p, 0:FE], ACT.Silu).then_inc(S["silu_done"], 1)

            def y_copy(e, s):
                p = s % 2
                act.wait_ge(S["dn_made"], e + 1)
                need(act, y_s[p], (e // 2) * 16)
                copy(y[p][:, 0:512], ps[:, 5, :], tab[s][:, 2:3].bitcast(F32)).then_inc(S["y_lo"], 1)

            def body4(g, first):
                for s in range(TABS):
                    e = g * TABS + s
                    rows_copy(e, s)
                    if not first or s >= 2:
                        y_copy(e - 2, (s - 2) % TABS)
                    silu(e, s)

            act.wait_ge(S["swp_done"], 1)
            n = act.value_load(more[0:1, 0:1], min_val=0, max_val=SWEEPS - 1) + 1
            body4(0, True)
            with act.Fori(1, n * GROUPS) as g:
                body4(g, False)
            y_copy(n * NE - 2, TABS - 2)
            y_copy(n * NE - 1, TABS - 1)
            act.wait_ge(S["ln2_in"], 32)
            for t in range(NT + 1):
                R = rows_of(t)
                act.wait_ge(S["frstd"], 2 * t + 2)
                nc.scalar.activation(yy[t][0:R, 1, :], yy[t][0:R, 0, :], ACT.Identity, bias=fve[t][0:R, :],
                                     scale=frs[t][0:R, :]).then_inc(S["fnorm"], 1)

        @block.vector
        def _(ve_):
            v = nc.vector
            ch = Chain(ve_, S["ch_dve"])

            def rotate(which, x1, x2, cos, sin, shape):
                n = int(np.prod(shape[1:]))
                t = [rt4[which][0:shape[0], k, 0:n] for k in range(4)]
                if len(shape) == 3:
                    t = [b.rearrange("p (a b) -> p a b", b=shape[2]) for b in t]
                ch.inc(v.tensor_tensor(t[0], x1, cos, ALU.mult))
                ch.inc(v.tensor_tensor(t[1], x2, sin, ALU.mult))
                ch.inc(v.tensor_tensor(t[2], x1, sin, ALU.mult))
                ch(v.tensor_tensor(t[3], x2, cos, ALU.mult))
                ch.inc(v.tensor_tensor(x1, t[0], t[1], ALU.subtract))
                return v.tensor_tensor(x2, t[2], t[3], ALU.add)

            def norms(t, p):
                R = rows_of(t)
                ve_.wait_ge(S["rms_done"], t + 1)
                need(ve_, S["cT_made"], t - 1)
                need(ve_, st_s[p], FULL_ST * (t // 2))
                for c, (dst, g) in enumerate(((cqn, gq), (ckvn, gkv))):
                    ins = v.scalar_tensor_tensor(out=dst[p][0:R, :], in0=ps[0:R, 0, 256 * c:256 * (c + 1)],
                                                 scalar=rq[p][0:R, c:c + 1], in1=g[0:R, :], op0=ALU.mult, op1=ALU.mult)
                ins.then_inc(S["norm_done"], 1)

            def table(p, R, a0, n, shape):
                return rope[p][0:R, a0:a0 + n] if shape is None else rope[p][0:R, a0:a0 + n].unsqueeze(1).broadcast_to(shape)

            def kr_rope(t, p):
                R, h = rows_of(t), ROPE // 2
                ve_.wait_ge(S["kr_copied"], t + 1)
                ve_.wait_ge(x_in_s[p], 32 * (t // 2 + 1))
                rotate(0, kr[p][0:R, 0:h], kr[p][0:R, h:2 * h], table(p, R, 0, h, None), table(p, R, h, h, None),
                       (R, h)).then_inc(S["kr_roped"], 1)

            def dqk_rope(t, p):
                R, h = rows_of(t), ROT // 2
                ve_.wait_ge(S["dqk_copied"], t + 1)
                x = zqk[p][0:R].rearrange("p a h d -> p (a h) d")
                shape = [R, 4 * HD, h]
                rotate(2, x[:, :, 0:h], x[:, :, h:2 * h], table(p, R, ROPE, h, shape), table(p, R, ROPE + h, h, shape),
                       shape).then_inc(S["dqk_roped"], 1)

            def kpT_copy(t, p, R):
                ve_.wait_ge(S["kpT_made"], t + 1)
                if isinstance(t, int) and t > NT:
                    ve_.wait_ge(st_s[p], FULL_ST * (4 if p else 5))
                v.tensor_copy(kpT[p][:, 0:R], ps[0:ROPE, 5, 0:R]).then_inc(S["kpT_copied"], 1)

            def dT_copy(t, p, R, first):
                ve_.wait_ge(S["dT_made"], t + 1)
                for half in range(first, 2):
                    ins = v.tensor_copy(dT[p][:, half, :, 0:R],
                                        ps[:, (7, 4)[half], :].rearrange("p (k r) -> p k r", r=P)[:, :, 0:R])
                ins.then_inc(S["dT_copied"], 1)

            def kn_copy(t, p, R):
                ve_.wait_ge(S["kn_made"], t + 1)
                v.tensor_copy(knT[p][:, :, 0:R], ps[:, 4, :].rearrange("p (k r) -> p k r", r=P)[:, :, 0:R]).then_inc(S["kn_copied"], 1)

            def q_rope(t, p):
                R, h = rows_of(t), ROPE // 2
                ve_.wait_ge(S["q_copied"], t + 1)
                shape = [R, HM, h]
                rotate(1, qs[p][0:R, :, NOPE:NOPE + h], qs[p][0:R, :, NOPE + h:QD],
                       table(p, R, 0, h, shape), table(p, R, h, h, shape), shape).then_inc(S["q_roped"], 1)

            def body1(t, p):
                cur, prev = is_tile(t, NT), is_tile(t - 1, NT)
                q, R1 = 1 - p, rows_of(t - 1)
                if cur:
                    norms(t, p)
                    kr_rope(t, p)
                if prev:
                    kpT_copy(t - 1, q, R1)
                    dT_copy(t - 1, q, R1, 0)
                    q_rope(t - 1, q)
                    kn_copy(t - 1, q, R1)
                if cur:
                    dqk_rope(t, p)

            v.memset(pad_rows[:], PAD).then_inc(S["pads_set"], 1)
            ve_.wait_ge(S["lam_in"], 64)
            ch.inc(v.tensor_tensor(lamt[:, 0, :], lam4[:, 0, :], lam4[:, 1, :], ALU.mult))
            ch(v.tensor_tensor(lamt[:, 1, :], lam4[:, 2, :], lam4[:, 3, :], ALU.mult))
            v.tensor_reduce(lams[:], lamt[:], AX.X, ALU.add).then_inc(S["lam_prod"], 1)
            ve_.wait_ge(S["lam_exp"], 1)
            ch(v.tensor_scalar(neglam[:], lame[:, 1:2], -LAM_INIT, None, ALU.add))
            ch(v.tensor_tensor(neglam[:], neglam[:], lame[:, 0:1], ALU.subtract))
            ve_.wait_ge(S["rope_in"], 32)
            for t in range(3):
                body1(t, t % 2)
            with ve_.Fori(0, 2) as i:
                ch.enter(i, 30)
                body1(3 + 2 * i, 1)
                body1(4 + 2 * i, 0)
            ch.leave(2)
            body1(7, 1)
            body1(8, 0)
            body1(9, 1)
            for c in range(2):
                kpT_copy(NT + 1 + c, 1 - c, P)
                dT_copy(NT + 1 + c, 1 - c, P, 1)
                kn_copy(NT + 1 + c, 1 - c, P)

            def maxima(a, maps):
                for m in maps:
                    pair = m if a.diff else a.p
                    ve_.wait_ge(S["s_made"], a.s + m + 1)
                    sc = ps[0:a.rows, 2 * pair:2 * pair + 2, :].rearrange("p b c -> p (b c)")
                    if a.i < NT:
                        ch(v.memset(sc[0:64, a.keys - 64:a.keys], NEG))
                    v.tensor_reduce(nmax[pair][0:a.rows, :], sc[:, 0:a.keys], AX.X, ALU.max, negate=True).then_inc(S["max_done"], 1)

            def pT_copy(a):
                w = a.blocks - 4
                ve_.wait_ge(S["t_hi"], a.bigs + 1)
                ve_.wait_ge(S["o_made"], a.u + 1)
                v.tensor_copy(pT[a.p][:, 4:4 + w, :], ps[:, 5, 0:w * P].rearrange("p (k r) -> p k r", r=P)).then_inc(S["pT_hi"], 1)

            def mix(a):
                R, n = a.rows, a.keys
                ve_.wait_ge(S["exp_done"], a.s + 2)
                ch(v.reciprocal(rsum[a.p][0:R, 1:2], psums[a.p6][1][0:R, :]))
                ch(v.scalar_tensor_tensor(out=mixc[a.p][0:R, :], in0=psums[a.p6][0][0:R, :], scalar=rsum[a.p][0:R, 1:2],
                                          in1=neglam[0:R, :], op0=ALU.mult, op1=ALU.mult))
                v.scalar_tensor_tensor(out=pr[a.p][0][0:R, 0:n], in0=pr[a.p][1][0:R, 0:n], scalar=mixc[a.p][0:R, :],
                                       in1=pr[a.p][0][0:R, 0:n], op0=ALU.mult, op1=ALU.add).then_inc(S["mix_done"], 1)

            def o_copy(a):
                V = VD if a.diff else VM
                col = HM * VM + (2 * a.j + a.hp) * VD if a.diff else (2 * a.j + a.hp) * VM
                ve_.wait_ge(S["exp_done"], a.s + a.maps)
                ch(v.reciprocal(rsum[a.p][0:a.rows, 0:1], psums[a.p6][0][0:a.rows, :]))
                ve_.wait_ge(S["o_made"], 2 + a.u + 1)
                v.tensor_scalar(merged[0:a.rows, a.i, bass.ds(col, V)], ps[0:a.rows, 6 + a.p, 0:V],
                                rsum[a.p][0:a.rows, 0:1], None, ALU.mult).then_inc(S["o_done"], 1)

            def step2(diff, j, k):
                a, b, c, two, one = (Tile(diff, j, k + n) for n in range(5))
                if b.exists and b.big:
                    pT_copy(b)
                if one.exists and not one.diff:
                    maxima(one, (0,))
                if two.exists and two.diff:
                    maxima(two, (0,))
                if c.exists and c.diff:
                    mix(c)
                if a.exists:
                    o_copy(a)
                if two.exists and two.diff:
                    maxima(two, (1,))

            ve_.wait_ge(st_s[1], FULL_ST * 4 + 5 * 16)
            ve_.wait_ge(st_s[0], FULL_ST * 5 + 5 * 16)
            ve_.sem_inc(S["o_done"], 2)
            for k in range(-4, 0):
                step2(False, 0, k)
            with ve_.Fori(0, HM // 2 - 1) as j:
                ch.enter(j, PAIR - 2 + PAIR)
                for k in range(PAIR):
                    step2(False, j, k)
            ch.leave(HM // 2 - 1)
            for k in range(PAIR):
                step2(False, HM // 2 - 1, k)
            for j in range(HD // 2):
                for k in range(PAIR):
                    step2(True, j, k)

            def stage(t, p):
                R = rows_of(t)
                need(ve_, S["mT_made"], t - 1)
                mr = merged[0:R, bass.ds(t, 1), :].rearrange("p a d -> p (a d)")
                v.tensor_copy(mst[p][0:R, 0:512], mr[:, 0:512])
                ve_.wait_ge(S["hrs_done"], t + 1)
                v.tensor_tensor(mst[p][0:R, 512:1024].rearrange("p (h v) -> p h v", v=VD),
                                mr[:, 512:1024].rearrange("p (h v) -> p h v", v=VD),
                                m4s[p][2][0:R, :].unsqueeze(2).broadcast_to([R, HD, VD]), ALU.mult).then_inc(S["md_done"], 1)

            def layer1(t, p):
                R = rows_of(t)
                ve_.wait_ge(S["op_made"], t + 1)
                ve_.wait_ge(xr_s[p], 16 * (t // 2 + 1))
                need(ve_, S["h_done"], t - 1)
                for half in range(2):
                    c = slice(512 * half, 512 * (half + 1))
                    ins = v.scalar_tensor_tensor(out=r1[p][0:R, c], in0=xr[p][0:R, c], scalar=ALPHA, in1=ps[0:R, 2 * p + half, :],
                                                 op0=ALU.mult, op1=ALU.add)
                ins.then_inc(S["res_done"], 1)
                ve_.wait_ge(S["res_done"], t + 1)
                for half in range(2):
                    ch.inc(v.bn_stats(bst[p][0:R, half, :], r1[p][0:R, 512 * half:512 * (half + 1)]))
                ch.wait()
                settle(ve_)
                v.bn_aggr(mv[p][0:R, :], bst[p][0:R].rearrange("p a b -> p (a b)")).then_inc(S["ln_stat"], 1)
                ve_.wait_ge(S["ln_rstd"], t + 1)
                ch(v.tensor_scalar(r1[p][0:R, :], r1[p][0:R, :], mv[p][0:R, 0:1], rst[p][0:R, :], ALU.subtract, ALU.mult))
                if isinstance(t, int) and t == 0:
                    ve_.wait_ge(S["ph3_in"], 16 * 6)
                v.tensor_tensor(r1[p][0:R, :], r1[p][0:R, :], g1b[0:R, :], ALU.mult).then_inc(S["ln_mul"], 1)

            def first_of(vals, n, w, m, oh, R):
                ch(v.tensor_reduce(m, vals, AX.X, ALU.max))
                ch(v.scalar_tensor_tensor(out=w, in0=vals, scalar=m, in1=const[0:R, C_DESC:C_DESC + n], op0=ALU.is_ge, op1=ALU.mult))
                ch(v.tensor_reduce(top1[0:R, 7:8], w, AX.X, ALU.max))
                ch(v.tensor_scalar(oh, w, top1[0:R, 7:8], None, ALU.is_equal))

            def choose(t, p):
                R = rows_of(t)
                ve_.wait_ge(S["lg_made"], t + 1)
                ch(v.tensor_tensor(lg[0:R, :], ps[0:R, 6, 0:NG + NE], b_r[0:R, :], ALU.add))
                first_of(lg[0:R, 0:NG], NG, wgt[0:R, 0:NG], top1[0:R, 0:1], ohg[0:R, :], R)
                g3 = ohg[0:R, :].unsqueeze(2).broadcast_to([R, NG, EPG])
                ch(v.tensor_tensor(emul[0:R], lg[0:R, NG:NG + NE].rearrange("p (g j) -> p g j", j=EPG), g3, ALU.mult))
                ch(v.tensor_reduce(ein8[0:R, 0, :], emul[0:R].rearrange("p g j -> p j g"), AX.X, ALU.add))
                first_of(ein8[0:R, 0, :], EPG, wgt[0:R, :], top1[0:R, 1:2], ohe[0:R, 0, :], R)
                ch(v.scalar_tensor_tensor(out=ein8[0:R, 1, :], in0=ohe[0:R, 0, :], scalar=NEG, in1=ein8[0:R, 0, :], op0=ALU.mult, op1=ALU.add))
                first_of(ein8[0:R, 1, :], EPG, wgt[0:R, :], top1[0:R, 2:3], ohe[0:R, 1, :], R)
                ch.inc(v.tensor_scalar(shifted[p][0:R, 0:NG], lg[0:R, 0:NG], top1[0:R, 0:1], None, ALU.subtract))
                v.tensor_tensor(shifted[p][0:R, 4:5], top1[0:R, 2:3], top1[0:R, 1:2], ALU.subtract).then_inc(S["shift_done"], 1)
                for k in range(2):
                    ch.inc(v.tensor_tensor(oh32[p][0:R, k, :].rearrange("p (g j) -> p g j", j=EPG), g3,
                                           ohe[0:R, k, :].unsqueeze(1).broadcast_to([R, NG, EPG]), ALU.mult))
                ch.wait()
                v.tensor_tensor(picks[p][0:R, :], oh32[p][0:R, 0, :], oh32[p][0:R, 1, :], ALU.add).then_inc(S["picks_done"], 1)

            def list_rows(t, p):
                R = rows_of(t)
                ve_.wait_ge(S["exp3_done"], t + 1)
                ch(v.tensor_reduce(gates[p][0:R, 2:3], exped[p][0:R, 0:NG], AX.X, ALU.add))
                ch(v.scalar_tensor_tensor(out=gates[p][0:R, 3:4], in0=exped[p][0:R, 4:5], scalar=1.0, in1=gates[p][0:R, 2:3],
                                          op0=ALU.add, op1=ALU.mult))
                ch(v.reciprocal(gates[p][0:R, 0:1], gates[p][0:R, 3:4]))
                ch(v.tensor_tensor(gates[p][0:R, 1:2], exped[p][0:R, 4:5], gates[p][0:R, 0:1], ALU.mult))
                ve_.wait_ge(S["ent_free"], t + 1)
                tok = const[0:R, bass.ds(C_TOK + t, 1)]
                for k in range(2):
                    ch.inc(v.tensor_copy(entry[p][0:R, k, 0:1], tok))
                    ch.inc(v.tensor_scalar(entry[p][0:R, k, 1:2], tok, float(k * TOK), None, ALU.add))
                    ch.inc(v.tensor_copy(entry[p][0:R, k, 2:3].bitcast(F32), gates[p][0:R, k:k + 1]))
                ve_.wait_ge(S["pre_made"], t + 1)
                ch(v.scalar_tensor_tensor(out=where[0:R, :], in0=ps[0:R, 7, 0:NE], scalar=float(NE), in1=const[0:R, C_IOTA:C_IOTA + NE],
                                          op0=ALU.mult, op1=ALU.add))
                ch(v.tensor_tensor(where2[0:R], oh32[p][0:R], where[0:R, :].unsqueeze(1).broadcast_to([R, 2, NE]), ALU.mult))
                ch(v.tensor_reduce(rowf[0:R, :], where2[0:R], AX.X, ALU.add))
                ch(v.tensor_copy(row[p][0:R].rearrange("p a b -> p (a b)"), rowf[0:R, :]))
                if R < P:
                    ch.inc(v.tensor_copy(before[1 - p][R:P, :], before[p][R:P, :]))
                v.tensor_tensor(before[1 - p][0:R, :], before[p][0:R, :], picks[p][0:R, :], ALU.add).then_inc(S["rows_done"], 1)

            def body3(t, p):
                if is_tile(t, NT):
                    layer1(t, p)
                if is_tile(t - 2, NT):
                    list_rows(t - 2, p)
                if is_tile(t - 1, NT):
                    choose(t - 1, 1 - p)
                if is_tile(t + 2, NT):
                    stage(t + 2, p)

            for k in range(2):
                ch.inc(v.memset(before[k][:], 0.0))
                ch.inc(v.memset(entry[k][:], 0))
            ch.wait()
            for t in (-2, -1, 0, 1):
                body3(t, t % 2)
            with ve_.Fori(0, 2) as i:
                ch.enter(i, 72)
                body3(2 + 2 * i, 0)
                body3(3 + 2 * i, 1)
            ch.leave(2)
            for t in range(6, NT + 3):
                body3(t, t % 2)
            ve_.wait_ge(S["cnt_made"], 1)
            ch(v.tensor_reduce(cntm[:], ps[:, 6, 0:NE], AX.X, ALU.max))
            ch(v.tensor_scalar(over[:], const[:, C_THR:C_THR + 8], cntm[:], None, ALU.is_lt))
            ch(v.tensor_reduce(nover[:], over[:], AX.X, ALU.add))
            v.tensor_copy(more[:], nover[:]).then_inc(S["swp_done"], 1)

            def rows_copy(e, s):
                p = s % 2
                ve_.wait_ge(S["hgT_made"], 2 * e + 2)
                need(ve_, S["gu_made"], e - 1)
                ve_.wait_ge(S["hgT_copied"], 2 * e + 1)
                v.tensor_copy(hgT[p][:, 4:8, :], ps[:, 3, :].rearrange("p (k r) -> p k r", r=P)).then_inc(S["hgT_copied"], 1)

            def hidden(e, s):
                p = s % 2
                ve_.wait_ge(S["silu_done"], e + 1)
                need(ve_, S["hidT_made"], e - 1)
                v.tensor_tensor(hid[p][:], sil[p][:], ps[:, p, FE:2 * FE], ALU.mult).then_inc(S["hid_done"], 1)

            def hidT_copy(e, s):
                p = s % 2
                ve_.wait_ge(S["hidT_made"], e + 1)
                need(ve_, S["dn_made"], e - 1)
                v.tensor_copy(hidT[p][:].rearrange("p k r -> p (k r)"), ps[:, 4, 0:2 * P]).then_inc(S["hidT_copied"], 1)

            def y_copy(e, s):
                p = s % 2
                ve_.wait_ge(S["dn_made"], e + 1)
                need(ve_, y_s[p], (e // 2) * 16)
                v.tensor_scalar(y[p][:, 512:1024], ps[:, 6, :], tab[s][:, 2:3].bitcast(F32), None, ALU.mult).then_inc(S["y_hi"], 1)

            def body4(g, first):
                for s in range(TABS):
                    e = g * TABS + s
                    rows_copy(e, s)
                    if not first or s >= 2:
                        y_copy(e - 2, (s - 2) % TABS)
                    if not first or s >= 1:
                        hidT_copy(e - 1, (s - 1) % TABS)
                    hidden(e, s)

            ve_.wait_ge(S["swp_done"], 1)
            n = ve_.value_load(more[0:1, 0:1], min_val=0, max_val=SWEEPS - 1) + 1
            for k in range(2):
                ins = v.memset(hg[k][:], 0.0)
            ins.then_inc(S["hg_zero"], 1)
            body4(0, True)
            with ve_.Fori(1, n * GROUPS) as g:
                body4(g, False)
            E = n * NE
            y_copy(E - 2, TABS - 2)
            hidT_copy(E - 1, TABS - 1)
            y_copy(E - 1, TABS - 1)

            ve_.wait_ge(S["ln2_in"], 32)
            def fin_stats(t):
                R = rows_of(t)
                ve_.wait_ge(f_in[t], 16)
                ch(v.scalar_tensor_tensor(out=yy[t][0:R, 0, :], in0=merged[0:R, t, :], scalar=ALPHA, in1=yy[t][0:R, 0, :],
                                          op0=ALU.mult, op1=ALU.add))
                ch(v.tensor_tensor(yy[t][0:R, 0, :], yy[t][0:R, 0, :], yy[t][0:R, 1, :], ALU.add))
                for half in range(2):
                    ch.inc(v.bn_stats(fst[t][0:R, half, :], yy[t][0:R, 0, 512 * half:512 * (half + 1)]))
                ch.wait()
                v.bn_aggr(fmv[t][0:R, :], fst[t][0:R].rearrange("p a b -> p (a b)")).then_inc(S["fstat"], 1)

            def fin_mul(t):
                R = rows_of(t)
                ve_.wait_ge(S["fnorm"], t + 1)
                v.tensor_tensor(yy[t][0:R, 1, :], yy[t][0:R, 1, :], g2b[0:R, :], ALU.mult).then_inc(S["fmul"], 1)

            for t in range(NT + 2):
                if t <= NT:
                    fin_stats(t)
                if t >= 1:
                    fin_mul(t - 1)

        @block.gpsimd
        def _(po):
            g = nc.gpsimd
            ch = Chain(po, S["ch_pool"])

            def rsqrt(dst, src, tmp, R, n, inv, eps):
                settle(po)
                ch(g.tensor_scalar(tmp, src, inv, eps, ALU.mult, ALU.add))
                return g.tensor_tensor(dst, tmp, const[0:R, C_HALF:C_HALF + n], ALU.pow)

            def rms(t, p):
                R = rows_of(t)
                po.wait_ge(S["sq_done"], t + 1)
                need(po, S["norm_done"], t - 1)
                rsqrt(rq[p][0:R, :], ss[p][0:R, :], ms[p][0:R, :], R, 2, 1.0 / QR, EPS_RMS).then_inc(S["rms_done"], 1)

            po.wait_ge(S["const_in"], 16)
            for t in range(3):
                rms(t, t % 2)
            with po.Fori(0, 2) as i:
                ch.enter(i, 2)
                rms(3 + 2 * i, 1)
                rms(4 + 2 * i, 0)
            ch.leave(2)
            rms(7, 1)
            rms(8, 0)

            def head_rms(t, p):
                R = rows_of(t)
                po.wait_ge(S["hsq_done"], t + 1)
                need(po, S["md_done"], t - 1)
                rsqrt(m4s[p][2][0:R, :], m4s[p][0][0:R, :], m4s[p][1][0:R, :], R, HD, 1.0 / VD, EPS_RMS).then_inc(S["hrs_done"], 1)

            def layer1(t, p):
                R = rows_of(t)
                po.wait_ge(S["ln_stat"], t + 1)
                rsqrt(rst[p][0:R, :], mv[p][0:R, 1:2], ve[p][0:R, :], R, 1, 1.0, EPS_LN).then_inc(S["ln_rstd"], 1)
                po.wait_ge(S["ln_mul"], t + 1)
                g.tensor_tensor(xr[p][0:R, :], r1[p][0:R, :], b1b[0:R, :], ALU.add).then_inc(S["h_done"], 1)

            def scatter_rows(t, p):
                R = rows_of(t)
                po.wait_ge(S["rows_done"], t + 1)
                if isinstance(t, int) and t == 0:
                    po.wait_ge(S["pads_out"], 16 * SWEEPS)
                settle(po)
                for k in range(2):
                    g.indirect_dma_start(list_d.rearrange("p e w -> (p e) w"),
                                         bass.IndirectOffsetOnAxis(ap=row[p][0:R, k, 0:1], axis=0),
                                         entry[p][0:R, k, :], None, bounds_check=SWEEPS * P * NE - 1,
                                         oob_is_err=False).then_inc(ent_s[p], 16)
                po.wait_ge(ent_s[p], 32 * (t // 2 + 1))
                po.sem_inc(S["ent_free"], 1)

            def body3(t, p):
                if is_tile(t + 2, NT):
                    head_rms(t + 2, p)
                if is_tile(t, NT):
                    layer1(t, p)
                if is_tile(t - 2, NT):
                    scatter_rows(t - 2, p)

            po.wait_ge(S["o_done"], 2 + 9 * (HM + HD))
            po.sem_inc(S["ent_free"], 2)
            for t in (-2, -1, 0, 1):
                body3(t, t % 2)
            with po.Fori(0, 2) as i:
                ch.enter(i, 4)
                body3(2 + 2 * i, 0)
                body3(3 + 2 * i, 1)
            ch.leave(2)
            for t in range(6, NT + 3):
                body3(t, t % 2)

            def gather(e, s, lots):
                p = s % 2
                po.wait_ge(tab_s[s], lots * 16)
                need(po, S["hgT_made"], 2 * (e - 1))
                settle(po)
                g.indirect_dma_start(hg[p][:], None, h_d, bass.IndirectOffsetOnAxis(ap=tab[s][:, 0:1], axis=0),
                                     bounds_check=TOK - 1, oob_is_err=False).then_inc(hg_s[p], 16)

            def scatter(e, s):
                p = s % 2
                po.wait_ge(S["y_lo"], e + 1)
                po.wait_ge(S["y_hi"], e + 1)
                settle(po)
                g.indirect_dma_start(pair_d, bass.IndirectOffsetOnAxis(ap=tab[s][:, 1:2], axis=0), y[p][:], None,
                                     bounds_check=2 * TOK - 1, oob_is_err=False).then_inc(y_s[p], 16)

            po.wait_ge(S["hg_zero"], 1)
            po.wait_ge(h_st[0], 16 * 5)
            po.wait_ge(h_st[1], 16 * 4)
            po.wait_ge(S["swp_done"], 1)
            n = po.value_load(more[0:1, 0:1], min_val=0, max_val=SWEEPS - 1) + 1

            def body4(gr, first):
                for s in range(TABS):
                    e = gr * TABS + s
                    gather(e, s, gr + 1)
                    if not first or s >= 3:
                        scatter(e - 3, (s - 3) % TABS)

            body4(0, True)
            with po.Fori(1, n * GROUPS) as gr:
                body4(gr, False)
            for k in (3, 2, 1):
                scatter(n * NE - k, TABS - k)

            po.wait_ge(S["ln2_in"], 32)
            for t in range(NT + 2):
                if t <= NT:
                    R = rows_of(t)
                    po.wait_ge(S["fstat"], t + 1)
                    g_ = rsqrt(frs[t][0:R, :], fmv[t][0:R, 1:2], fve[t][0:R, :], R, 1, 1.0, EPS_LN)
                    g_.then_inc(S["frstd"], 1)
                    po.wait_ge(S["frstd"], 2 * t + 1)
                    ch(g.tensor_tensor(fve[t][0:R, :], fmv[t][0:R, 0:1], frs[t][0:R, :], ALU.mult))
                    g.tensor_scalar(fve[t][0:R, :], fve[t][0:R, :], -1.0, None, ALU.mult).then_inc(S["frstd"], 1)
                if t >= 1:
                    R, u = rows_of(t - 1), t - 1
                    po.wait_ge(S["fmul"], t)
                    g.tensor_tensor(yy[u][0:R, 0, :], yy[u][0:R, 1, :], b2b[0:R, :], ALU.add).then_inc(S["fin_done"], 1)




def const_table():
    c = np.zeros((P, C_N), np.float32)
    c[:, C_ID:C_ID + P] = np.eye(P)
    c[:, C_TRI:C_TRI + P] = np.triu(np.ones((P, P)), 1)
    c[:, C_ONE:C_ONE + P] = 1
    c[:, C_IOTA:C_IOTA + NE] = np.arange(NE)
    c[:, C_DESC:C_DESC + 8] = 8 - np.arange(8)
    c[:, C_TOK:C_TOK + 9] = np.arange(P)[:, None] + P * np.arange(9)
    c[:, C_HALF:C_HALF + 9] = -0.5
    c[:, C_THR:C_THR + 8] = P * (1 + np.arange(8))
    return c


def rope_table():
    pos = np.concatenate([np.arange(SEQ), PAST + np.arange(DEC)]).astype(np.float32)
    cols = []
    for r in (ROPE, ROT):
        inv = np.float32(500000.0) ** (-np.arange(0, r, 2, dtype=np.float32) / np.float32(r))
        ang = pos[:, None] * inv.astype(np.float32)
        cols += [np.cos(ang), np.sin(ang)]
    return np.concatenate(cols, 1).astype(np.float32)


_OUTS = [("y_prompt", (1, SEQ, D)), ("y_sample", (1, DEC, D)),
         ("new_ckv_p", (1, 1, SEQ, KVR)), ("new_kpe_p", (1, 1, SEQ, ROPE)),
         ("new_dk_p", (1, 1, SEQ, HD, 2 * DD)), ("new_dv_p", (1, 1, SEQ, HD, VD)),
         ("new_ckv_s", (1, 1, DEC, KVR)), ("new_kpe_s", (1, 1, DEC, ROPE)),
         ("new_dk_s", (1, 1, DEC, HD, 2 * DD)), ("new_dv_s", (1, 1, DEC, HD, VD))]


def kernel(**inputs):
    import numpy as _np
    import concourse.bacc as _bacc
    from concourse import mybir as _mybir
    from concourse.bass_utils import run_bass_kernel_spmd as _run

    nc = _bacc.Bacc("TRN2", target_bir_lowering=False, num_devices=1)
    arrays, args, outs = {}, {}, {}
    given = dict(inputs)
    given["const_table"] = const_table()
    given["rope_table"] = rope_table()
    for name, value in given.items():
        v = _np.ascontiguousarray(value)
        arrays[f"in_{name}"] = v
        args[name] = nc.dram_tensor(f"in_{name}", v.shape, _mybir.dt.from_np(v.dtype), kind="ExternalInput").ap()
    for name, shape in _OUTS:
        outs[name] = nc.dram_tensor(f"out_{name}", shape, F32, kind="ExternalOutput").ap()
    build(nc, args, outs)
    r = _run(nc, [arrays], core_ids=[0])
    return tuple(r.results[0][f"out_{name}"] for name, _ in _OUTS)
```

```python
from contextlib import ExitStack

import concourse.bass as bass
import numpy as np
from concourse import mybir

F32 = mybir.dt.float32
F32R = mybir.dt.float32r
U32 = mybir.dt.uint32
I32 = mybir.dt.int32
ALU = mybir.AluOpType
ACT = mybir.ActivationFunctionType
AX = mybir.AxisListType

P = 128
D = 1024
KD = D // P
SEQ, DEC, PAST = 1024, 64, 256
NT = SEQ // P
NC = PAST // P
TOK = SEQ + DEC
KEYS = SEQ + PAST + DEC
QR = KVR = 256
ROPE = 32
NOPE = 64
HM, QD, VM = 8, NOPE + ROPE, 64
HD, DD, VD, ROT = 4, 64, 128, 16
IN_COLS = QR + KVR + ROPE + 3 * HD * 2 * DD
ZC = [(0, 512), (512, 288), (800, 512), (1824, 256), (1312, 512)]
Z_BANK = (0, 1, 2, 1, 3)
MLA_SCALE = float(QD) ** -0.5
DIFF_SCALE = float(DD) ** -0.5
LAM_INIT = 0.8 - 0.6
ALPHA = 2.0 ** 0.25
EPS_LN, EPS_RMS = 1e-5, 1e-6
NG, EPG = 4, 8
NE = NG * EPG
FE = 256
NEG = -3.0e38
SLOTS = 4
TABS = 8
GROUPS = NE // TABS
SWEEPS = 9
PAD = 65535

C_ID, C_TRI, C_ONE, C_IOTA, C_DESC, C_TOK, C_HALF, C_THR = 0, 128, 256, 384, 416, 424, 433, 442
C_N = 450
ROPE_N = 2 * (ROPE // 2 + ROT // 2)


class Chain:

    def __init__(self, eng, sem):
        self.eng, self.sem, self.base, self.n = eng, sem, 0, 0

    def inc(self, ins):
        ins.then_inc(self.sem, 1)
        self.n += 1

    def wait(self):
        self.eng.wait_ge(self.sem, self.base + self.n)

    def __call__(self, ins):
        self.inc(ins)
        self.wait()

    def enter(self, i, per):
        self.start, self.per = self.base + self.n, per
        self.base, self.n = self.start + i * per, 0

    def leave(self, trips):
        assert self.n == self.per, self.n
        self.base, self.n = self.start + trips * self.per, 0


ORDER = [7, 6, 4, 8, 0, 2, 1, 3, 5]
BIG = [i for i in ORDER if 4 <= i < NT]
PAIR = 2 * len(ORDER)
MLA_TILES = HM * len(ORDER)


class Tile:

    def __init__(self, diff, j, k):
        if not diff and isinstance(j, int) and j == HM // 2 - 1 and k >= PAIR:
            diff, j, k = True, 0, k - PAIR
        turn, r = divmod(k, PAIR)
        self.exists = not isinstance(j, int) or (0 <= j + turn and not (diff and j + turn >= HD // 2))
        self.diff, self.j = diff, j + turn
        self.i = ORDER[r % 9]
        self.p, self.p6, self.hp = r % 2, r % 6, r // 9
        self.rows = DEC if self.i == NT else P
        self.keys = KEYS - SEQ if self.i == NT else (self.i + 1) * P
        self.blocks = (self.keys + P - 1) // P
        self.u = PAIR * j + k + (MLA_TILES if diff else 0)
        self.big = self.i in BIG
        bigs = sum(ORDER[x % 9] in BIG for x in range(r))
        self.bigs = 2 * len(BIG) * (j + turn) + bigs + (HM * len(BIG) if diff else 0)
        self.maps = 2 if diff else 1
        self.s = self.u if not diff else MLA_TILES + 2 * (PAIR * j + k)


def is_tile(t, last):
    return not isinstance(t, int) or 0 <= t <= last


def rows_of(t):
    return DEC if isinstance(t, int) and t == NT else P


def need(eng, sem, value):
    if not isinstance(value, int) or value > 0:
        eng.wait_ge(sem, value)


def build(nc, a, out):
    with ExitStack() as ctx:
        def dram(name, shape, dt=F32):
            return nc.dram_tensor(name, shape, dt, kind="Internal").ap()

        def sem(name):
            return ctx.enter_context(nc.semaphore(name))

        qT_d, kT_d = dram("qT_d", [HM, QD, TOK]), dram("kT_d", [HM, QD, KEYS])
        dqT_d, dkT_d = dram("dqT_d", [HD, P, TOK]), dram("dkT_d", [HD, P, KEYS])
        v_d = dram("v_d", [KEYS, HM * VM])
        h_d, pair_d = dram("h_d", [TOK, D]), dram("pair_d", [2 * TOK, D])
        list_d = dram("list_d", [SWEEPS * P, NE, 4], U32)

        top = [(nc.sbuf_base + 63) // 64 * 64]

        def place(at, name, shape, dt=F32):
            size = int(np.prod(shape[1:])) * 4
            t = nc.alloc_sbuf_tensor_at(name, shape, dt, offset=at[0])
            at[0] += (size + 31) // 32 * 32
            assert at[0] <= nc.sbuf_usable_end, (name, at[0])
            return t

        const = place(top, "const", [P, C_N])
        wgu, wdn = [None] * SLOTS, [None] * SLOTS
        ring_base = top[0]
        for s in range(2):
            wgu[s] = place(top, f"wgu{s}", [P, KD, 2 * FE])
            wdn[s] = place(top, f"wdn{s}", [P, FE // P, D])
        ring_end = top[0]
        neglam = place(top, "neglam", [P, 1])
        subln = place(top, "subln", [P, 2])
        region = top[0]

        m0 = [ring_base]
        xT = [place(m0, f"xT{p}", [P, KD, P]) for p in range(2)]
        xTl = [place(m0, f"xTl{p}", [P, KD, P]) for p in range(2)]
        zqk = [place(m0, f"zqk{p}", [P, 2, 2 * HD, DD]) for p in range(2)]
        w_uq = place(m0, "w_uq_sb", [P, 2, HM * QD])
        w_ukv = place(m0, "w_ukv_sb", [P, 2, 2, HM * NOPE])
        x_in = place(m0, "x_in", [P, D])
        dT = place(m0, "dT", [P, 2, HD, P])
        zv = place(m0, "zv", [P, HD * VD])
        assert m0[0] <= ring_end
        m1, m1r = [region], [region + KD * IN_COLS * 4]
        w_in = place(m1, "w_in_sb", [P, KD, IN_COLS])
        w_inr = place(m1r, "w_in_raw", [P, KD, IN_COLS])
        w_inl = place(m1, "w_in_rest", [P, KD, IN_COLS])
        gq, gkv = place(m1, "gq", [P, QR]), place(m1, "gkv", [P, KVR])
        lam4 = place(m1, "lam4", [P, 4, DD])
        lams = place(m1, "lams", [P, 2])
        lame = place(m1, "lame", [P, 2])
        pad_rows = place(m1, "pad_rows", [P, NE], U32)
        rope = [place(m1, f"rope{p}", [P, ROPE_N]) for p in range(2)]
        kr = [place(m1, f"kr{p}", [P, ROPE]) for p in range(2)]
        cqn = [place(m1, f"cqn{p}", [P, QR]) for p in range(2)]
        ckvn = [place(m1, f"ckvn{p}", [P, KVR]) for p in range(2)]
        cT = place(m1, "cT", [P, 4, P])
        qs = place(m1, "qs", [P, HM, QD])
        kpT = place(m1, "kpT", [ROPE, P])
        qT = place(m1, "qT", [QD, HM, P])
        knT = place(m1, "knT", [P, HM // 2, P])
        vs = place(m1, "vs", [P, HM * VM])
        junk = place(m1, "junk", [P, 2, QR])
        ss = [place(m1, f"ss{p}", [P, 2]) for p in range(2)]
        ms = [place(m1, f"ms{p}", [P, 2]) for p in range(2)]
        rq = [place(m1, f"rq{p}", [P, 2]) for p in range(2)]
        rt4 = [place(m1, f"rt4{n}", [P, 4, (ROPE // 2, P, P)[n]]) for n in range(3)]

        m2 = [region]
        hq = [place(m2, f"hq{p}", [P, TOK]) for p in range(2)]
        hk = [place(m2, f"hk{p}", [P, KEYS]) for p in range(2)]
        hv = [place(m2, f"hv{p}", [P, 11, VD]) for p in range(2)]
        pr = [[place(m2, f"pr{p}{m}", [P, SEQ]) for m in range(2)] for p in range(2)]
        pT = [place(m2, f"pT{p}", [P, NT, P]) for p in range(2)]
        nmax = [place(m2, f"nmax{p}", [P, 1]) for p in range(2)]
        rsum = [place(m2, f"rsum{p}", [P, 2]) for p in range(2)]
        psums = [[place(m2, f"psums{p}{m}", [P, 1]) for m in range(2)] for p in range(6)]
        mixc = [place(m2, f"mixc{p}", [P, 1]) for p in range(2)]
        assert m2[0] <= region + KD * IN_COLS * 4
        m3 = [region]
        xr = [place(m3, f"xr{p}", [P, D]) for p in range(2)]
        mT = [place(m3, f"mT{p}", [P, KD, P]) for p in range(2)]
        mTl = [place(m3, f"mTl{p}", [P, KD, P]) for p in range(2)]
        r1 = [place(m3, f"r1{p}", [P, D]) for p in range(2)]
        hT = place(m3, "hT", [P, KD, P])
        mst = place(m3, "mst", [P, D])
        sqj = place(m3, "sqj", [P, HD, VD])
        g1b, b1b = place(m3, "g1b", [P, D]), place(m3, "b1b", [P, D])
        w_r = place(m3, "w_r_sb", [P, KD, NG + NE])
        b_r = place(m3, "b_r_sb", [P, NG + NE])
        bst = [place(m3, f"bst{p}", [P, 2, 6]) for p in range(2)]
        mv = [place(m3, f"mv{p}", [P, 2]) for p in range(2)]
        ve = [place(m3, f"ve{p}", [P, 1]) for p in range(2)]
        rst = [place(m3, f"rst{p}", [P, 1]) for p in range(2)]
        lg = place(m3, "lg", [P, NG + NE])
        top1 = place(m3, "top1", [P, 8])
        wgt = place(m3, "wgt", [P, 8])
        ohg = place(m3, "ohg", [P, NG])
        ein8 = place(m3, "ein8", [P, 2, EPG])
        emul = place(m3, "emul", [P, NG, EPG])
        ohe = place(m3, "ohe", [P, 2, EPG])
        shifted = [place(m3, f"shifted{p}", [P, 8]) for p in range(2)]
        exped = [place(m3, f"exped{p}", [P, 8]) for p in range(2)]
        oh32 = [place(m3, f"oh32{p}", [P, 2, NE]) for p in range(2)]
        picks = [place(m3, f"picks{p}", [P, NE]) for p in range(2)]
        before = [place(m3, f"before{p}", [P, NE]) for p in range(2)]
        gates = [place(m3, f"gates{p}", [P, 4]) for p in range(2)]
        where = place(m3, "where", [P, NE])
        where2 = place(m3, "where2", [P, 2, NE])
        rowf = place(m3, "rowf", [P, 2])
        row = [place(m3, f"row{p}", [P, 2, 1], U32) for p in range(2)]
        entry = [place(m3, f"entry{p}", [P, 2, 4], U32) for p in range(2)]
        cntm = place(m3, "cntm", [P, 1])
        over = place(m3, "over", [P, 8])
        nover = place(m3, "nover", [P, 1])
        m4 = [region]
        hgT = [place(m4, f"hgT{p}", [P, KD, P]) for p in range(2)]
        sil = [place(m4, f"sil{p}", [P, FE]) for p in range(2)]
        hid = [place(m4, f"hid{p}", [P, FE]) for p in range(2)]
        hidT = [place(m4, f"hidT{p}", [P, 2, P]) for p in range(2)]
        y = [place(m4, f"y{p}", [P, D]) for p in range(2)]
        g2b, b2b = place(m4, "g2b", [P, D]), place(m4, "b2b", [P, D])
        m5 = [max(m2[0], m3[0], m4[0])]
        merged = place(m5, "merged", [P, NT + 1, D])
        m6 = list(m5)
        w_o = place(m5, "w_o_sb", [P, KD, D])
        wgu[3] = place(m6, "wgu3", [P, KD, 2 * FE])
        wdn[3] = place(m6, "wdn3", [P, FE // P, D])
        hg = [place(m6, f"hg{p}", [P, D]) for p in range(2)]
        assert m6[0] <= m5[0]
        m4s = [[place(m5, f"{n}{p}", [P, HD]) for n in ("hsq", "hms", "hrs")] for p in range(2)]
        more = place(m5, "more", [P, 1], I32)
        tab = [place(m5, f"tab{s}", [P, 4], U32) for s in range(TABS)]
        hi_base = (nc.sbuf_usable_end - KD * D * 4) // 64 * 64
        hi, hi1, hi2 = [hi_base], [hi_base], [hi_base]
        w_raw = place(hi1, "w_raw", [P, KD, D])
        w_ol = place(hi, "w_ol", [P, KD, D])
        wgu[2] = place(hi2, "wgu2", [P, KD, 2 * FE])
        wdn[2] = place(hi2, "wdn2", [P, FE // P, D])
        NF = NT + 1
        fst = [place(m5, f"fst{t}", [P, 2, 6]) for t in range(NF)]
        fmv = [place(m5, f"fmv{t}", [P, 2]) for t in range(NF)]
        fve = [place(m5, f"fve{t}", [P, 1]) for t in range(NF)]
        frs = [place(m5, f"frs{t}", [P, 1]) for t in range(NF)]
        assert m5[0] <= hi_base
        m7, m8 = [ring_base], [hi_base]
        yy = [place(m7 if t < 6 else m8, f"yy{t}", [P, 2, D]) for t in range(NF)]
        assert m7[0] <= region

        ps = ctx.enter_context(nc.psum_tensor("ps", [P, 8, 512], F32))

        names = """const_in lam_in lam_prod lam_exp lam_done x_made rope_in wuq_in wukv_in
            xT_made xT_copied z_made w_hi w_lo xTl_made sq_done rms_done norm_done kr_copied dqk_copied dv_copied kr_roped dqk_roped
            cT_made kpT_made dT_made cT_copied kpT_copied dT_copied q_made kn_made v_made q_copied kn_copied
            v_copied q_roped qT_made qT_copied pads_set pads_out
            ch_dve ch_act ch_pool settled
            s_made max_done exp_done mix_done t_lo t_hi pT_lo pT_hi o_made o_done
            wo_in wo_hi wo_lo mTl_made ph3_in sub_in hsq_done hrs_done md_done mT_made mT_copied op_made res_done ln_stat ln_rstd
            ln_mul h_done hT_made hT_copied lg_made shift_done exp3_done picks_done hm_done ent_free
            pre_made rows_done cnt_made swp_done before0
            hg_zero hgT_made hgT_copied gu_made silu_done hid_done hidT_made hidT_copied dn_made
            y_lo y_hi add_done fstat frstd fmul fin_done f_out sum_made sum_read fnorm ln2_in""".split()
        S = {n: sem(n) for n in names}
        x_in_s = [sem(f"x_in_s{p}") for p in range(2)]
        win_s = [sem(f"win_s{c}") for c in range(len(ZC))]
        cache_s = [sem(f"cache_s{p}") for p in range(2)]
        st_s = [sem(f"st_s{p}") for p in range(2)]
        head_s = [sem(f"head_s{p}") for p in range(2)]
        samp_s = [sem(f"samp_s{p}") for p in range(2)]
        xr_s = [sem(f"xr_s{p}") for p in range(2)]
        h_st = [sem(f"h_st{p}") for p in range(2)]
        ent_s = [sem(f"ent_s{p}") for p in range(2)]
        w_s = [sem(f"w_s{s}") for s in range(SLOTS)]
        tab_s = [sem(f"tab_s{s}") for s in range(TABS)]
        hg_s = [sem(f"hg_s{p}") for p in range(2)]
        y_s = [sem(f"y_s{p}") for p in range(2)]
        f_in = [sem(f"f_in{p}") for p in range(NF)]

        late_s = sem("late_s")
        zv_s = sem("zv_s")
        KEY_ST = 16 * 5
        LATE_ST = KEY_ST + 16 * 2
        EARLY_ST = 16 * 3

        block = ctx.enter_context(nc.Block())

        def settle(eng):
            eng.sem_inc(S["settled"], 1)

        def key_col(t):
            return SEQ + PAST if isinstance(t, int) and t == NT else t * P

        @block.sync
        def _(sp):
            def load_x(t, p):
                need(sp, S["xT_made"], t)
                if not isinstance(t, int):
                    settle(sp)
                if not isinstance(t, int) or t >= 2:
                    sp.wait_ge(S["q_roped"], t - 1)
                R = rows_of(t)
                src = a["x_sample"][0] if R == DEC else a["x_prompt"][0, bass.ds(t * P, P), :]
                sp.dma_start(x_in[0:R, :], src).then_inc(x_in_s[p], 16)
                sp.dma_start(rope[p][0:R, :], a["rope_table"][bass.ds(t * P, R), :]).then_inc(x_in_s[p], 16)

            def store_early(t, p):
                R, last = rows_of(t), isinstance(t, int) and t == NT

                def row(name):
                    dst = out["new_" + name + ("_s" if last else "_p")][0, 0]
                    return dst if last else dst[bass.ds(t * P, P)]

                sp.wait_ge(S["norm_done"], 1 + t)
                sp.dma_start(row("ckv"), ckvn[p][0:R, :]).then_inc(st_s[p], 16)
                sp.wait_ge(S["kr_roped"], 1 + t)
                sp.dma_start(row("kpe"), kr[p][0:R, :]).then_inc(st_s[p], 16)
                sp.wait_ge(S["dv_copied"], 1 + t)
                sp.dma_start(row("dv").rearrange("t h v -> t (h v)"), zv[0:R, :]).then_inc(zv_s, 16)
                sp.wait_ge(S["dqk_roped"], 1 + t)
                sp.dma_start(row("dk").rearrange("t h v -> t (h v)"),
                             zqk[p][0:R, 1].rearrange("p h d -> p (h d)")).then_inc(st_s[p], 16)

            def store_keys(t, p, R, col):
                sp.wait_ge(S["kpT_copied"], NC + 1 + t)
                src = kpT[:, 0:R].unsqueeze(1).broadcast_to([ROPE, HM, R])
                sp.dma_start(kT_d[:, NOPE:QD, bass.ds(col, R)].rearrange("h d k -> d h k"), src).then_inc(late_s, 16)
                sp.wait_ge(S["kn_copied"], NC + 1 + t)
                settle(sp)
                for half in range(2):
                    sp.dma_start(kT_d[half::2, 0:NOPE, bass.ds(col, R)].rearrange("h d k -> d h k"),
                                 knT[NOPE * half:NOPE * (half + 1), :, 0:R]).then_inc(late_s, 16)
                sp.wait_ge(S["v_copied"], NC + 1 + t)
                sp.dma_start(v_d[bass.ds(col, R), :], vs[0:R, :]).then_inc(late_s, 16)
                sp.wait_ge(S["dT_copied"], NC + 1 + t)
                sp.dma_start(dkT_d[:, :, bass.ds(col, R)].rearrange("h d k -> d h k"),
                             dT[:, 1, :, 0:R]).then_inc(late_s, 16)

            def store_late(t, p):
                R = rows_of(t)
                store_keys(t, p, R, key_col(t))
                sp.dma_start(dqT_d[:, :, bass.ds(t * P, R)].rearrange("h d k -> d h k"),
                             dT[:, 0, :, 0:R]).then_inc(late_s, 16)
                sp.wait_ge(S["qT_copied"], 1 + t)
                sp.dma_start(qT_d[:, :, bass.ds(t * P, R)].rearrange("h d k -> d h k"),
                             qT[:, :, 0:R]).then_inc(late_s, 16)

            def load_expert(s, e):
                sp.dma_start(wgu[s][:, :, 0:FE], a["w_exp_gate"][0, bass.ds(e, 1)].rearrange(
                    "a (k p) f -> p (a k) f", p=P)).then_inc(w_s[s], 16)
                sp.dma_start(wgu[s][:, :, FE:2 * FE], a["w_exp_up"][0, bass.ds(e, 1)].rearrange(
                    "a (k p) f -> p (a k) f", p=P)).then_inc(w_s[s], 16)
                sp.dma_start(wdn[s][:], a["w_exp_down"][0, bass.ds(e, 1)].rearrange(
                    "a (k p) f -> p (a k) f", p=P)).then_inc(w_s[s], 16)

            sp.dma_start(const[:], a["const_table"]).then_inc(S["const_in"], 16)
            load_x(0, 0)
            for c in range(NC):
                rows = slice(c * P, (c + 1) * P)
                sp.dma_start(ckvn[c][:], a["cache_mla_ckv"][0, 0, rows]).then_inc(cache_s[c], 16)
                sp.dma_start(kr[c][:], a["cache_mla_kpe"][0, 0, rows]).then_inc(cache_s[c], 16)
                sp.dma_start(zqk[c][:, 1].rearrange("p h d -> p (h d)"),
                             a["cache_diff_k"][0, 0, rows].rearrange("t h d -> t (h d)")).then_inc(cache_s[c], 16)
            for k in range(2):
                kv = a["mla_w_ukv"][0, k * P:(k + 1) * P].rearrange("p (h x c) -> p x h c", x=2, c=NOPE)
                for x in range(2):
                    sp.dma_start(w_ukv[:, k, x].rearrange("p (h c) -> p h c", c=NOPE), kv[:, x]).then_inc(S["wukv_in"], 16)
            w3 = a["w_in"][0].rearrange("(k p) c -> p k c", p=P)
            for c, (c0, n) in enumerate(ZC):
                sp.dma_start(w_inr[:, :, c0:c0 + n], w3[:, :, c0:c0 + n]).then_inc(win_s[c], 16)
                if c in (0, 3):
                    k = (0, 3).index(c)
                    store_keys(k - NC, k, P, SEQ + k * P)
                if c == 1:
                    for dst, name in ((gq, "mla_q_norm"), (gkv, "mla_kv_norm")):
                        sp.dma_start(dst[:], a[name][0].partition_broadcast(P)).then_inc(S["rope_in"], 16)
                if c == 3:
                    load_x(1, 1)
            sp.dma_start(w_uq[:], a["mla_w_uq"][0].rearrange("(k p) c -> p k c", p=P)).then_inc(S["wuq_in"], 16)
            for n, name in enumerate(("q1", "k1", "q2", "k2")):
                sp.dma_start(lam4[:, n, :], a["diff_lambda_" + name][0].partition_broadcast(P)).then_inc(S["lam_in"], 16)
            sp.dma_start(subln[:, 0:1], a["diff_subln"][0].rearrange("(p a) -> p a", a=1)).then_inc(S["sub_in"], 16)
            sp.wait_ge(S["pads_set"], 1)
            for b in range(SWEEPS):
                sp.dma_start(list_d[b * P:(b + 1) * P].rearrange("p (a e) w -> p a (e w)", a=4),
                             pad_rows[:].unsqueeze(1).broadcast_to([P, 4, NE])).then_inc(S["pads_out"], 16)

            def body1(t, p):
                if is_tile(t + 1, NT) and not (isinstance(t, int) and t == 0):
                    load_x(t + 1, 1 - p)
                if is_tile(t, NT):
                    store_early(t, p)
                if is_tile(t - 1, NT):
                    store_late(t - 1, 1 - p)

            for t in range(3):
                body1(t, t % 2)
            with sp.Fori(0, 2) as i:
                body1(3 + 2 * i, 1)
                body1(4 + 2 * i, 0)
            body1(7, 1)
            body1(8, 0)
            def head_parts(q_d, k_d, h, p, part):
                q, k = (slice(0, SEQ), slice(0, SEQ + PAST)) if part == 0 else (slice(SEQ, TOK), slice(SEQ + PAST, KEYS))
                n = QD if q_d is qT_d else P
                return ((hq[p][0:n, q], q_d[bass.ds(h, 1), :, q]), (hk[p][0:n, k], k_d[bass.ds(h, 1), :, k]))

            def load_mla(h, p, parts=(0, 1)):
                if not isinstance(h, int):
                    sp.wait_ge(S["o_made"], 2 + 9 * (h - 1))
                v = v_d[:, bass.ds(h * VM, VM)]
                for part in parts:
                    done = (head_s, samp_s)[part][p]
                    for dst, src in head_parts(qT_d, kT_d, h, p, part):
                        sp.dma_start(dst, src.rearrange("a d t -> (a d) t")).then_inc(done, 16)
                    if part == 0:
                        sp.dma_start(hv[p][:, 0:10, 0:VM], v[0:10 * P].rearrange("(t p) v -> p t v", p=P)).then_inc(done, 16)
                    else:
                        sp.dma_start(hv[p][0:DEC, 10, 0:VM], v[10 * P:KEYS]).then_inc(done, 16)

            def load_diff(h, p):
                sp.wait_ge(S["o_made"], 2 + 9 * (HM + h - 1))
                for part in (0, 1):
                    done = (head_s, samp_s)[part][p]
                    for dst, src in head_parts(dqT_d, dkT_d, h, p, part):
                        sp.dma_start(dst, src.rearrange("a d t -> (a d) t")).then_inc(done, 16)
                    if part == 0:
                        for dst, src in ((hv[p][:, 0:NT, :], out["new_dv_p"]), (hv[p][:, NT:NT + 2, :], a["cache_diff_v"])):
                            sp.dma_start(dst, src[0, 0, :, bass.ds(h, 1), :].rearrange("(t p) a v -> p t (a v)", p=P)).then_inc(done, 16)
                    else:
                        sp.dma_start(hv[p][0:DEC, 10, :], out["new_dv_s"][0, 0, :, bass.ds(h, 1), :].rearrange("t a v -> t (a v)")).then_inc(done, 16)

            sp.wait_ge(late_s, NC * KEY_ST + NT * LATE_ST)
            sp.wait_ge(S["z_made"], 5 * (NT + 1))
            load_mla(0, 0, (0,))
            store_late(NT, 0)
            load_mla(1, 1, (0,))
            for sm, n in ((late_s, NC * KEY_ST + (NT + 1) * LATE_ST), (zv_s, 16 * (NT + 1)), (st_s[1], EARLY_ST * 4),
                          (st_s[0], EARLY_ST * 5)):
                sp.wait_ge(sm, n)
            load_mla(0, 0, (1,))
            load_mla(1, 1, (1,))
            sp.dma_start(w_raw[:], a["w_out"][0].rearrange("(k p) c -> p k c", p=P)).then_inc(S["wo_in"], 16)
            for s in range(2):
                load_expert(s, s)
            with sp.Fori(1, HM // 2) as i:
                load_mla(2 * i, 0)
                load_mla(2 * i + 1, 1)
            with sp.Fori(0, HD // 2) as i:
                load_diff(2 * i, 0)
                load_diff(2 * i + 1, 1)

            sp.wait_ge(S["o_done"], 2 + 9 * (HM + HD))
            for dst, name in ((g1b, "ln1_g"), (b1b, "ln1_b")):
                sp.dma_start(dst[:], a[name][0].partition_broadcast(P)).then_inc(S["ph3_in"], 16)
            sp.dma_start(w_r[:, :, 0:NG], a["w_route_group"][0].rearrange("(k p) c -> p k c", p=P)).then_inc(S["ph3_in"], 16)
            sp.dma_start(w_r[:, :, NG:NG + NE], a["w_route_expert"][0].rearrange("(k p) c -> p k c", p=P)).then_inc(S["ph3_in"], 16)
            sp.dma_start(b_r[:, 0:NG], a["b_route_group"][0].partition_broadcast(P)).then_inc(S["ph3_in"], 16)
            sp.dma_start(b_r[:, NG:NG + NE], a["b_route_expert"][0].partition_broadcast(P)).then_inc(S["ph3_in"], 16)

            def load_xr(t, p):
                need(sp, S["hT_made"], t - 1)
                need(sp, S["hm_done"], t - 1)
                R = rows_of(t)
                src = a["x_sample"][0] if R == DEC else a["x_prompt"][0, bass.ds(t * P, P), :]
                sp.dma_start(xr[p][0:R, :], src).then_inc(xr_s[p], 16)

            def body3(t, p):
                if is_tile(t + 1, NT):
                    load_xr(t + 1, 1 - p)
                if is_tile(t, NT):
                    R = rows_of(t)
                    sp.wait_ge(S["hm_done"], t + 1)
                    sp.dma_start(h_d[bass.ds(t * P, R), :], merged[0:R, bass.ds(t, 1), :].rearrange("p a d -> p (a d)")).then_inc(h_st[p], 16)

            for t in (-1, 0, 1):
                body3(t, t % 2)
            with sp.Fori(0, 2) as i:
                body3(2 + 2 * i, 0)
                body3(3 + 2 * i, 1)
            for t in range(6, NT + 1):
                body3(t, t % 2)
            sp.wait_ge(S["op_made"], NT + 1)
            load_expert(2, 2)
            sp.wait_ge(ent_s[0], 32 * 5)
            sp.wait_ge(ent_s[1], 32 * 4)

            def load_list(s, g):
                sweep, e = (0, s) if isinstance(g, int) else (g // GROUPS, (g % GROUPS) * TABS + s)
                sp.dma_start(tab[s][:], list_d[bass.ds(sweep * P, P), bass.ds(e, 1), :].rearrange(
                    "p a w -> p (a w)")).then_inc(tab_s[s], 16)

            for s in range(TABS):
                load_list(s, 0)
            load_expert(3, 3)
            sp.wait_ge(S["cnt_made"], 1)
            for dst, name in ((g2b, "ln2_g"), (b2b, "ln2_b")):
                sp.wait_ge(S["rows_done"], NT + 1)
                sp.dma_start(dst[:], a[name][0].partition_broadcast(P)).then_inc(S["ln2_in"], 16)
            sp.wait_ge(S["swp_done"], 1)
            n = sp.value_load(more[0:1, 0:1], min_val=0, max_val=SWEEPS - 1) + 1
            for s in range(SLOTS, TABS):
                sp.wait_ge(S["dn_made"], s - SLOTS + 1)
                load_expert(s % SLOTS, s)
            with sp.Fori(1, n * GROUPS) as g:
                for s in range(TABS):
                    e = g * TABS + s
                    sp.wait_ge(y_s[s % 2], (e - TABS) // 2 * 16 + 16)
                    load_list(s, g)
                    sp.wait_ge(S["dn_made"], e - SLOTS + 1)
                    load_expert(s % SLOTS, (g % GROUPS) * TABS + s)
            sp.wait_ge(y_s[0], n * (NE // 2) * 16)
            sp.wait_ge(y_s[1], n * (NE // 2) * 16)

            for t in range(NT + 1):
                R = rows_of(t)
                sp.dma_start(yy[t][0:R], pair_d.rearrange("(k n) d -> n k d", k=2)[t * P:t * P + R]).then_inc(f_in[t], 16)
            for t in range(NT + 1):
                R = rows_of(t)
                sp.wait_ge(S["fin_done"], t + 1)
                dst = out["y_sample"][0] if t == NT else out["y_prompt"][0, t * P:(t + 1) * P, :]
                sp.dma_start(dst, yy[t][0:R, 0, :]).then_inc(S["f_out"], 16)
            sp.wait_ge(S["f_out"], 16 * (NT + 1))

        @block.tensor
        def _(pe):
            def turn(bank, col, src, R, n):
                return pe.transpose(ps[0:n, bank, col:col + R], src, const[0:R, C_ID:C_ID + R])

            def xT_of(t, p):
                R = rows_of(t)
                pe.wait_ge(x_in_s[p], (t // 2 + 1) * 32)
                for half in range(2):
                    if not isinstance(t, int) or t > 0:
                        pe.wait_ge(S["kn_copied"] if half == 0 else S["v_copied"], NC + t - 1)
                    for k in range(4):
                        mm = turn(4 + half, k * P, x_in[0:R, (4 * half + k) * P:(4 * half + k + 1) * P], R, P)
                mm.then_inc(S["xT_made"], 1)

            def z_of(t, p, c):
                (c0, n), bank = ZC[c], Z_BANK[c]
                if isinstance(t, int) and t == 0:
                    pe.wait_ge(S["w_lo"], c + 1)
                if c == 0:
                    pe.wait_ge(S["xTl_made"], t + 1)
                    need(pe, S["norm_done"], t)
                if c == 1:
                    need(pe, S["dv_copied"], t)
                if c == 2 or c == 4:
                    need(pe, S["dqk_copied"], t)
                if c == 3:
                    pe.wait_ge(S["kr_copied"], t + 1)
                for k in range(KD):
                    for i, (x, w) in enumerate(((xT, w_in), (xT, w_inl), (xTl, w_in))):
                        mm = pe.matmul(ps[:, bank, 0:n], x[p][:, k, :].bitcast(F32R), w[:, k, c0:c0 + n].bitcast(F32R),
                                       start=k == 0 and i == 0, stop=k == KD - 1 and i == 2)
                mm.then_inc(S["z_made"], 1)

            def turn_keys(t, p, R, heads):
                pe.wait_ge(S["norm_done"], t + 1) if heads else pe.wait_ge(cache_s[p], 48)
                if isinstance(t, int) and t <= 0:
                    need(pe, S["cT_copied"], NC + t)
                else:
                    pe.wait_ge(S["qT_copied"], t)
                for c in range(0 if heads else 2, 4):
                    src = (cqn if c < 2 else ckvn)[p][0:R, (c % 2) * P:(c % 2 + 1) * P]
                    mm = turn(6, c * P, src, R, P)
                mm.then_inc(S["cT_made"], 1)
                if heads:
                    pe.wait_ge(S["kr_roped"], t + 1)
                    need(pe, S["xTl_made"], t + 1)
                    if is_tile(t + 1, NT):
                        pe.wait_ge(S["xTl_made"], t + 2)
                else:
                    pe.wait_ge(S["xTl_made"], 1)
                need(pe, S["v_copied"], NC + t)
                turn(5, 0, kr[p][0:R, :], R, ROPE).then_inc(S["kpT_made"], 1)
                if heads:
                    pe.wait_ge(S["dqk_roped"], t + 1)
                need(pe, S["kn_copied"], NC + t)
                for half, bank in ((0, 7), (1, 4)) if heads else ((1, 4),):
                    for h in range(HD):
                        mm = turn(bank, h * P, zqk[p][0:R, half, 2 * h:2 * h + 2, :].rearrange("p a d -> p (a d)"), R, P)
                mm.then_inc(S["dT_made"], 1)

            def expand(t, p, R, heads):
                pe.wait_ge(S["cT_copied"], NC + t + 1)
                if isinstance(t, int) and t == -NC:
                    pe.wait_ge(S["wukv_in"], 16 * 4)
                if isinstance(t, int) and t == 0:
                    pe.wait_ge(S["wuq_in"], 16)
                pe.wait_ge(S["dT_copied"], NC + t + 1)
                if heads:
                    for half in range(2):
                        for k in range(2):
                            mm = pe.matmul(ps[0:R, 6 + half, 0:384], cT[:, k, 0:R], w_uq[:, k, 384 * half:384 * (half + 1)],
                                           start=k == 0, stop=k == 1)
                    mm.then_inc(S["q_made"], 1)
                for j in range(HM // 2):
                    for k in range(2):
                        mm = pe.matmul(ps[:, 4, j * P:j * P + R], w_ukv[:, k, 0, P * j:P * (j + 1)], cT[:, 2 + k, 0:R],
                                       start=k == 0, stop=k == 1)
                mm.then_inc(S["kn_made"], 1)
                pe.wait_ge(S["kpT_copied"], NC + t + 1)
                for k in range(2):
                    mm = pe.matmul(ps[0:R, 5, :], cT[:, 2 + k, 0:R], w_ukv[:, k, 1, :],
                                   start=k == 0, stop=k == 1)
                mm.then_inc(S["v_made"], 1)

            def turn_q(t, p):
                R = rows_of(t)
                pe.wait_ge(S["q_roped"], t + 1)
                for h in range(HM):
                    mm = turn(6 + h // 4, (h % 4) * P, qs[0:R, h, :], R, QD)
                mm.then_inc(S["qT_made"], 1)

            def body1(t, p):
                cur, prev = is_tile(t, NT), is_tile(t - 1, NT)
                q, R1 = 1 - p, rows_of(t - 1)
                if cur:
                    z_of(t, p, 0)
                    z_of(t, p, 1)
                if prev:
                    turn_keys(t - 1, q, R1, True)
                if cur:
                    z_of(t, p, 2)
                if prev:
                    expand(t - 1, q, R1, True)
                if cur:
                    z_of(t, p, 3)
                if is_tile(t + 1, NT):
                    xT_of(t + 1, q)
                if cur:
                    z_of(t, p, 4)
                if prev:
                    turn_q(t - 1, q)

            pe.wait_ge(S["const_in"], 16)
            xT_of(0, 0)
            for c in range(NC):
                turn_keys(c - NC, c, P, False)
                expand(c - NC, c, P, False)
            for t in range(3):
                body1(t, t % 2)
            with pe.Fori(0, 2) as i:
                body1(3 + 2 * i, 1)
                body1(4 + 2 * i, 0)
            body1(7, 1)
            body1(8, 0)
            body1(9, 1)

            def scores(a, maps):
                R, n0 = a.rows, (SEQ if a.i == NT else 0)
                width = DD if a.diff else QD
                for m in maps:
                    pair = m if a.diff else a.p
                    if m == 0 and a.i == ORDER[0]:
                        pe.wait_ge(head_s[a.hp], 48 * (HM // 2) + 64 * (a.j + 1) if a.diff else 48 * (a.j + 1))
                    if m == 0 and a.i == NT:
                        pe.wait_ge(samp_s[a.hp], 48 * (HM // 2 + a.j + 1) if a.diff else 48 * (a.j + 1))
                    need(pe, S["exp_done"], a.s + m - 1)
                    if a.i == NT:
                        settle(pe)
                    for c0 in range(0, a.keys, 512):
                        c1 = min(a.keys, c0 + 512)
                        mm = pe.matmul(ps[0:R, 2 * pair + c0 // 512, 0:c1 - c0], hq[a.hp][m * DD:m * DD + width, a.i * P:a.i * P + R],
                                       hk[a.hp][m * DD:m * DD + width, n0 + c0:n0 + c1], start=True, stop=True)
                    mm.then_inc(S["s_made"], 1)

            def turn_p(a):
                if a.diff:
                    pe.wait_ge(S["mix_done"], a.u - MLA_TILES + 1)
                else:
                    pe.wait_ge(S["exp_done"], a.s + 1)
                for half in range(2 if a.big else 1):
                    if half == 0:
                        need(pe, S["pT_lo"], a.u)
                    else:
                        need(pe, S["pT_hi"], a.bigs)
                    if a.i == NT:
                        settle(pe)
                    for b in range(4 * half, min(a.blocks, 4 * half + 4)):
                        w = min(P, a.keys - b * P)
                        mm = turn(4 + half, (b % 4) * P, pr[a.p][0][0:a.rows, b * P:b * P + w], a.rows, w)
                    mm.then_inc(S["t_hi" if half else "t_lo"], 1)

            def values(a):
                V = VD if a.diff else VM
                pe.wait_ge(S["o_done"], a.u + 1)
                pe.wait_ge(S["pT_lo"], a.u + 1)
                if a.big:
                    pe.wait_ge(S["pT_hi"], a.bigs + 1)
                for b in range(a.blocks):
                    w = min(P, a.keys - b * P)
                    vb = NT + b if a.i == NT else b
                    mm = pe.matmul(ps[0:a.rows, 6 + a.p, 0:V], pT[a.p][0:w, b, 0:a.rows], hv[a.hp][0:w, vb, 0:V],
                                   start=b == 0, stop=b == a.blocks - 1)
                mm.then_inc(S["o_made"], 1)

            def step2(diff, j, k):
                a, near, b, two, one = (Tile(diff, j, k + n) for n in range(5))
                if one.exists and not one.diff:
                    scores(one, (0,))
                if two.exists and two.diff:
                    scores(two, (0,))
                if near.exists and near.diff:
                    turn_p(near)
                if a.exists:
                    values(a)
                if two.exists and two.diff:
                    scores(two, (1,))
                if b.exists and not b.diff:
                    turn_p(b)

            pe.wait_ge(S["qT_copied"], NT + 1)
            pe.wait_ge(S["v_copied"], NC + NT + 1)
            pe.wait_ge(S["kn_copied"], NC + NT + 1)
            pe.sem_inc(S["o_made"], 2)
            for k in range(-4, 0):
                step2(False, 0, k)
            with pe.Fori(0, HM // 2 - 1) as j:
                for k in range(PAIR):
                    step2(False, j, k)
            for k in range(PAIR):
                step2(False, HM // 2 - 1, k)
            for j in range(HD // 2):
                for k in range(PAIR):
                    step2(True, j, k)

            def mT_of(t, p):
                pe.wait_ge(S["md_done"], t + 1)
                need(pe, S["mTl_made"], t)
                for k in range(KD):
                    mm = turn(4 + k // 4, (k % 4) * P, mst[:, k * P:(k + 1) * P], P, P)
                mm.then_inc(S["mT_made"], 1)

            def project(t, p):
                pe.wait_ge(S["mTl_made"], t + 1)
                need(pe, S["res_done"], t - 1)
                for half in range(2):
                    for k in range(KD):
                        cols = slice(512 * half, 512 * (half + 1))
                        for n, (m, w) in enumerate(((mT, w_o), (mT, w_ol), (mTl, w_o))):
                            mm = pe.matmul(ps[:, 2 * p + half, :], m[p][:, k, :].bitcast(F32R), w[:, k, cols].bitcast(F32R),
                                           start=k == 0 and n == 0, stop=k == KD - 1 and n == 2)
                mm.then_inc(S["op_made"], 1)

            def hT_of(t, p):
                R = rows_of(t)
                pe.wait_ge(S["h_done"], t + 1)
                need(pe, S["shift_done"], t)
                for k in range(KD):
                    mm = turn(6 + k // 4, (k % 4) * P, hrow[p][0:R, k * P:(k + 1) * P], R, P)
                mm.then_inc(S["hT_made"], 1)

            hrow = xr

            def route(t, p):
                R = rows_of(t)
                pe.wait_ge(S["hT_copied"], t + 1)
                if isinstance(t, int) and t == 0:
                    pe.wait_ge(S["ph3_in"], 16 * 6)
                for k in range(KD):
                    mm = pe.matmul(ps[0:R, 6, 0:NG + NE], hT[:, k, 0:R], w_r[:, k, :], start=k == 0, stop=k == KD - 1)
                mm.then_inc(S["lg_made"], 1)

            def positions(t, p):
                R = rows_of(t)
                pe.wait_ge(S["picks_done"], t + 1)
                pe.matmul(ps[0:R, 7, 0:NE], const[0:R, C_TRI:C_TRI + R], picks[p][0:R, :], start=True, stop=False)
                pe.matmul(ps[0:R, 7, 0:NE], const[:, C_ONE:C_ONE + R], before[p][:], start=False, stop=True).then_inc(S["pre_made"], 1)

            def body3(t, p):
                if is_tile(t, NT):
                    project(t, p)
                if is_tile(t - 1, NT):
                    hT_of(t - 1, 1 - p)
                if is_tile(t + 2, NT):
                    mT_of(t + 2, p)
                if is_tile(t - 1, NT):
                    route(t - 1, 1 - p)
                if is_tile(t - 2, NT):
                    positions(t - 2, p)

            pe.wait_ge(S["o_done"], 2 + 9 * (HM + HD))
            pe.wait_ge(S["wo_lo"], KD)
            for t in range(-3, 2):
                body3(t, t % 2)
            with pe.Fori(0, 2) as i:
                body3(2 + 2 * i, 0)
                body3(3 + 2 * i, 1)
            for t in range(6, NT + 3):
                body3(t, t % 2)
            pe.wait_ge(S["rows_done"], NT + 1)
            pe.matmul(ps[:, 6, 0:NE], const[:, C_ONE:C_ONE + P], before[(NT + 1) % 2][:], start=True, stop=True).then_inc(S["cnt_made"], 1)

            def rows_turned(e, s):
                p = s % 2
                pe.wait_ge(hg_s[p], (e // 2 + 1) * 16)
                need(pe, S["hgT_copied"], 2 * e)
                for k in range(KD):
                    mm = turn(2 + k // 4, (k % 4) * P, hg[p][:, k * P:(k + 1) * P], P, P)
                    if k % 4 == 3:
                        mm.then_inc(S["hgT_made"], 1)

            def gate_up(e, s, g):
                p, w = s % 2, s % SLOTS
                pe.wait_ge(w_s[w], (g * (TABS // SLOTS) + s // SLOTS + 1) * 48)
                pe.wait_ge(S["hgT_copied"], 2 * e + 2)
                need(pe, S["hid_done"], e - 1)
                for k in range(KD):
                    mm = pe.matmul(ps[:, p, :], hgT[p][:, k, :], wgu[w][:, k, :], start=k == 0, stop=k == KD - 1)
                mm.then_inc(S["gu_made"], 1)

            def hidden_turned(e, s):
                p = s % 2
                pe.wait_ge(S["hid_done"], e + 1)
                need(pe, S["hidT_copied"], e)
                for k in range(2):
                    mm = turn(4, k * P, hid[p][:, k * P:(k + 1) * P], P, P)
                mm.then_inc(S["hidT_made"], 1)

            def down(e, s):
                p = s % 2
                pe.wait_ge(S["hidT_copied"], e + 1)
                need(pe, S["y_lo"], e)
                need(pe, S["y_hi"], e)
                for half in range(2):
                    for k in range(2):
                        mm = pe.matmul(ps[:, 5 + half, :], hidT[p][:, k, :], wdn[s % SLOTS][:, k, 512 * half:512 * (half + 1)],
                                       start=k == 0, stop=k == 1)
                mm.then_inc(S["dn_made"], 1)

            def body4(g, first):
                for s in range(TABS):
                    e = g * TABS + s
                    rows_turned(e, s)
                    if not first or s >= 2:
                        down(e - 2, (s - 2) % TABS)
                    if not first or s >= 1:
                        hidden_turned(e - 1, (s - 1) % TABS)
                    gate_up(e, s, g)

            pe.wait_ge(S["swp_done"], 1)
            n = pe.value_load(more[0:1, 0:1], min_val=0, max_val=SWEEPS - 1) + 1
            body4(0, True)
            with pe.Fori(1, n * GROUPS) as g:
                body4(g, False)
            E = n * NE
            down(E - 2, TABS - 2)
            hidden_turned(E - 1, TABS - 1)
            down(E - 1, TABS - 1)
            for t in range(NT + 1):
                R, b = rows_of(t), 2 * (t % 4)
                pe.wait_ge(f_in[t], 16)
                need(pe, S["sum_read"], t - 3)
                for half in range(2):
                    for k in range(2):
                        mm = pe.matmul(ps[0:R, b + half, :], const[0:R, C_ID:C_ID + R], yy[t][0:R, k, 512 * half:512 * (half + 1)],
                                       start=k == 0, stop=k == 1)
                mm.then_inc(S["sum_made"], 1)

        @block.scalar
        def _(act):
            def copy(dst, src, scale=None):
                return nc.scalar.activation(dst, src, ACT.Copy, scale=1.0 if scale is None else scale)

            def xT_copy(t, p):
                R = rows_of(t)
                act.wait_ge(S["xT_made"], t + 1)
                need(act, S["z_made"], 5 * (t - 1))
                ins = copy(xT[p][:, :, 0:R].bitcast(F32R), ps[:, 4:6, :].rearrange("p b (k r) -> p (b k) r", r=P)[:, :, 0:R])
                ins.then_inc(S["xT_copied"], 1)

            def latents(t, p):
                R = rows_of(t)
                act.wait_ge(S["z_made"], 5 * t + 1)
                need(act, S["rms_done"], t - 1)
                for c in range(2):
                    ins = nc.scalar.activation(junk[0:R, c, :], ps[0:R, 0, 256 * c:256 * (c + 1)], ACT.Square,
                                               accum_out=ss[p][0:R, c:c + 1])
                ins.then_inc(S["sq_done"], 1)

            def keep(t, p, c):
                R = rows_of(t)
                act.wait_ge(S["z_made"], 5 * t + c + 1)
                qk = zqk[p][0:R].rearrange("p a h d -> p (a h d)")
                if c == 1:
                    need(act, st_s[p], EARLY_ST * (t // 2))
                    act.wait_ge(S["dT_made"], NC + t - 1)
                    copy(qk[:, 0:256], ps[0:R, 1, ROPE:ROPE + 256], DIFF_SCALE)
                    copy(kr[p][0:R, :], ps[0:R, 1, 0:ROPE]).then_inc(S["kr_copied"], 1)
                elif c == 2:
                    copy(qk[:, 256:512], ps[0:R, 2, 0:256], DIFF_SCALE)
                    copy(qk[:, 512:768], ps[0:R, 2, 256:512])
                elif c == 3:
                    need(act, zv_s, 16 * t)
                    copy(zv[0:R, 256:512], ps[0:R, 1, 0:256])
                else:
                    copy(zv[0:R, 0:256], ps[0:R, 3, 256:512]).then_inc(S["dv_copied"], 1)
                    copy(qk[:, 768:1024], ps[0:R, 3, 0:256]).then_inc(S["dqk_copied"], 1)

            def round_w(c):
                c0, n = ZC[c]
                act.wait_ge(win_s[c], 16)
                copy(w_in[:, :, c0:c0 + n].bitcast(F32R), w_inr[:, :, c0:c0 + n]).then_inc(S["w_hi"], 1)

            def cT_copy(t, p, R, c0):
                act.wait_ge(S["cT_made"], NC + t + 1)
                need(act, S["v_made"], NC + t)
                copy(cT[:, c0:4, 0:R], ps[:, 6, :].rearrange("p (k r) -> p k r", r=P)[:, c0:4, 0:R]).then_inc(S["cT_copied"], 1)

            def q_copy(t, p):
                R = rows_of(t)
                act.wait_ge(S["q_made"], t + 1)
                need(act, S["qT_made"], t)
                copy(qs[0:R].rearrange("p (a h) d -> p a (h d)", a=2), ps[0:R, 6:8, 0:384], MLA_SCALE).then_inc(S["q_copied"], 1)

            def v_copy(t, p, R):
                act.wait_ge(S["v_made"], NC + t + 1)
                copy(vs[0:R, :], ps[0:R, 5, :]).then_inc(S["v_copied"], 1)

            def qT_copy(t, p):
                R = rows_of(t)
                act.wait_ge(S["qT_made"], t + 1)
                copy(qT[:, :, 0:R], ps[0:QD, 6:8, :].rearrange("p b (k r) -> p (b k) r", r=P)[:, :, 0:R]).then_inc(S["qT_copied"], 1)

            def body1(t, p):
                cur, prev = is_tile(t, NT), is_tile(t - 1, NT)
                q, R1 = 1 - p, rows_of(t - 1)
                first = isinstance(t, int) and t == 0
                if cur:
                    latents(t, p)
                    if first:
                        round_w(3)
                    keep(t, p, 1)
                if prev:
                    cT_copy(t - 1, q, R1, 0)
                if cur:
                    keep(t, p, 2)
                    if first:
                        round_w(4)
                if prev:
                    q_copy(t - 1, q)
                    v_copy(t - 1, q, R1)
                if cur:
                    keep(t, p, 3)
                if is_tile(t + 1, NT):
                    xT_copy(t + 1, q)
                if cur:
                    keep(t, p, 4)
                if prev:
                    qT_copy(t - 1, q)

            ch = Chain(act, S["ch_act"])
            xT_copy(0, 0)
            for c in range(NC):
                cT_copy(c - NC, c, P, 2)
                if c > 0:
                    round_w(0)
                v_copy(c - NC, c, P)
            round_w(1)
            round_w(2)
            for t in range(3):
                body1(t, t % 2)
                if t == 1:
                    act.wait_ge(S["lam_prod"], 1)
                    nc.scalar.activation(lame[:], lams[:], ACT.Exp).then_inc(S["lam_exp"], 1)
            with act.Fori(0, 2) as i:
                body1(3 + 2 * i, 1)
                body1(4 + 2 * i, 0)
            body1(7, 1)
            body1(8, 0)
            body1(9, 1)

            def exps(a, last):
                for m in range(a.maps):
                    pair = m if a.diff else a.p
                    act.wait_ge(S["max_done"], a.s + m + 1)
                    if m == 0 and (not isinstance(a.u, int) or a.u >= 2):
                        act.wait_ge(S["t_lo"], last.u + 1)
                        if last.big:
                            act.wait_ge(S["t_hi"], last.bigs + 1)
                        need(act, S["o_done"], a.u - 1)
                    sc = ps[0:a.rows, 2 * pair:2 * pair + 2, :].rearrange("p b c -> p (b c)")[:, 0:a.keys]
                    nc.scalar.activation(pr[a.p][m][0:a.rows, 0:a.keys], sc, ACT.Exp, bias=nmax[pair][0:a.rows, :],
                                         accum_out=psums[a.p6][m][0:a.rows, :]).then_inc(S["exp_done"], 1)

            def pT_copy(a):
                act.wait_ge(S["t_lo"], a.u + 1)
                act.wait_ge(S["o_made"], a.u + 1)
                src = ps[:, 4, :].rearrange("p (k r) -> p k r", r=P)
                if a.i == NT:
                    copy(pT[a.p][:, 0:2, 0:a.rows], src[:, 0:2, 0:a.rows])
                    copy(pT[a.p][0:DEC, 2, 0:a.rows], src[0:DEC, 2, 0:a.rows]).then_inc(S["pT_lo"], 1)
                else:
                    w = min(4, a.blocks)
                    copy(pT[a.p][:, 0:w, :], src[:, 0:w, :]).then_inc(S["pT_lo"], 1)

            def step2(diff, j, k):
                a, b = Tile(diff, j, k + 1), Tile(diff, j, k + 3)
                if a.exists:
                    pT_copy(a)
                if b.exists:
                    exps(b, a)

            for k in (-3, -2, -1):
                step2(False, 0, k)
            with act.Fori(0, HM // 2 - 1) as j:
                for k in range(PAIR):
                    step2(False, j, k)
            for k in range(PAIR):
                step2(False, HM // 2 - 1, k)
            for j in range(HD // 2):
                for k in range(PAIR):
                    step2(True, j, k)

            def head_squares(t, p):
                need(act, S["hrs_done"], t)
                for h in range(HD):
                    d = merged[0:P, bass.ds(t, 1), (HM * VM + h * VD):(HM * VM + (h + 1) * VD)].rearrange("p a v -> p (a v)")
                    ins = nc.scalar.activation(sqj[0:P, h, :], d, ACT.Square, accum_out=m4s[p][0][0:P, h:h + 1])
                ins.then_inc(S["hsq_done"], 1)

            def hT_copy(t, p):
                R = rows_of(t)
                act.wait_ge(S["hT_made"], t + 1)
                copy(hT[:, :, 0:R], ps[:, 6:8, :].rearrange("p b (k r) -> p (b k) r", r=P)[:, :, 0:R]).then_inc(S["hT_copied"], 1)

            def mT_copy(t, p):
                act.wait_ge(S["mT_made"], t + 1)
                need(act, S["op_made"], t - 1)
                src = ps[:, 4:6, :].rearrange("p b (k r) -> p b k r", r=P)
                copy(mT[p][:, 0:4, 0:P].bitcast(F32R), src[:, 0, :, 0:P])
                copy(mT[p][:, 4:8, 0:P].bitcast(F32R), src[:, 1, :, 0:P], subln[:, 1:2]).then_inc(S["mT_copied"], 1)

            def h_copy(t, p):
                R = rows_of(t)
                act.wait_ge(S["h_done"], t + 1)
                copy(merged[0:R, bass.ds(t, 1), :].rearrange("p a d -> p (a d)"), xr[p][0:R, :]).then_inc(S["hm_done"], 1)

            def gate_exps(t, p):
                R = rows_of(t)
                act.wait_ge(S["shift_done"], t + 1)
                nc.scalar.activation(exped[p][0:R, 0:5], shifted[p][0:R, 0:5], ACT.Exp).then_inc(S["exp3_done"], 1)

            def body3(t, p):
                if is_tile(t + 3, NT):
                    head_squares(t + 3, 1 - p)
                if is_tile(t - 1, NT):
                    hT_copy(t - 1, 1 - p)
                if is_tile(t + 2, NT):
                    mT_copy(t + 2, p)
                if is_tile(t, NT):
                    h_copy(t, p)
                if is_tile(t - 1, NT):
                    gate_exps(t - 1, 1 - p)

            act.wait_ge(S["o_done"], 2 + 9 * (HM + HD))
            act.wait_ge(S["sub_in"], 16)
            ch(copy(subln[:, 1:2], subln[:, 0:1], 1.0 - LAM_INIT))
            for t in range(-3, 2):
                body3(t, t % 2)
            with act.Fori(0, 2) as i:
                body3(2 + 2 * i, 0)
                body3(3 + 2 * i, 1)
            for t in range(6, NT + 3):
                body3(t, t % 2)

            def rows_copy(e, s):
                p = s % 2
                act.wait_ge(S["hgT_made"], 2 * e + 1)
                need(act, S["gu_made"], e - 1)
                copy(hgT[p][:, 0:4, :], ps[:, 2, :].rearrange("p (k r) -> p k r", r=P)).then_inc(S["hgT_copied"], 1)

            def silu(e, s):
                p = s % 2
                act.wait_ge(S["gu_made"], e + 1)
                need(act, S["hid_done"], e - 1)
                nc.scalar.activation(sil[p][:], ps[:, p, 0:FE], ACT.Silu).then_inc(S["silu_done"], 1)

            def y_copy(e, s):
                p = s % 2
                act.wait_ge(S["dn_made"], e + 1)
                need(act, y_s[p], (e // 2) * 16)
                copy(y[p][:, 0:512], ps[:, 5, :], tab[s][:, 2:3].bitcast(F32)).then_inc(S["y_lo"], 1)

            def body4(g, first):
                for s in range(TABS):
                    e = g * TABS + s
                    rows_copy(e, s)
                    if not first or s >= 2:
                        y_copy(e - 2, (s - 2) % TABS)
                    silu(e, s)

            act.wait_ge(S["swp_done"], 1)
            n = act.value_load(more[0:1, 0:1], min_val=0, max_val=SWEEPS - 1) + 1
            body4(0, True)
            with act.Fori(1, n * GROUPS) as g:
                body4(g, False)
            y_copy(n * NE - 2, TABS - 2)
            y_copy(n * NE - 1, TABS - 1)
            act.wait_ge(S["ln2_in"], 32)
            for t in range(NT + 1):
                R = rows_of(t)
                act.wait_ge(S["frstd"], 2 * t + 2)
                nc.scalar.activation(yy[t][0:R, 1, :], yy[t][0:R, 0, :], ACT.Identity, bias=fve[t][0:R, :],
                                     scale=frs[t][0:R, :]).then_inc(S["fnorm"], 1)

        @block.vector
        def _(ve_):
            v = nc.vector
            ch = Chain(ve_, S["ch_dve"])

            def rotate(which, x1, x2, cos, sin, shape):
                n = int(np.prod(shape[1:]))
                t = [rt4[which][0:shape[0], k, 0:n] for k in range(4)]
                if len(shape) == 3:
                    t = [b.rearrange("p (a b) -> p a b", b=shape[2]) for b in t]
                ch.inc(v.tensor_tensor(t[0], x1, cos, ALU.mult))
                ch.inc(v.tensor_tensor(t[1], x2, sin, ALU.mult))
                ch.inc(v.tensor_tensor(t[2], x1, sin, ALU.mult))
                ch(v.tensor_tensor(t[3], x2, cos, ALU.mult))
                ch.inc(v.tensor_tensor(x1, t[0], t[1], ALU.subtract))
                return v.tensor_tensor(x2, t[2], t[3], ALU.add)

            def norms(t, p):
                R = rows_of(t)
                ve_.wait_ge(S["rms_done"], t + 1)
                ve_.wait_ge(S["cT_made"], NC + t - 1)
                need(ve_, st_s[p], EARLY_ST * (t // 2))
                for c, (dst, g) in enumerate(((cqn, gq), (ckvn, gkv))):
                    ins = v.scalar_tensor_tensor(out=dst[p][0:R, :], in0=ps[0:R, 0, 256 * c:256 * (c + 1)],
                                                 scalar=rq[p][0:R, c:c + 1], in1=g[0:R, :], op0=ALU.mult, op1=ALU.mult)
                ins.then_inc(S["norm_done"], 1)

            def table(p, R, a0, n, shape):
                return rope[p][0:R, a0:a0 + n] if shape is None else rope[p][0:R, a0:a0 + n].unsqueeze(1).broadcast_to(shape)

            def kr_rope(t, p):
                R, h = rows_of(t), ROPE // 2
                ve_.wait_ge(S["kr_copied"], t + 1)
                ve_.wait_ge(x_in_s[p], 32 * (t // 2 + 1))
                rotate(0, kr[p][0:R, 0:h], kr[p][0:R, h:2 * h], table(p, R, 0, h, None), table(p, R, h, h, None),
                       (R, h)).then_inc(S["kr_roped"], 1)

            def dqk_rope(t, p):
                R, h = rows_of(t), ROT // 2
                ve_.wait_ge(S["dqk_copied"], t + 1)
                x = zqk[p][0:R].rearrange("p a h d -> p (a h) d")
                shape = [R, 4 * HD, h]
                rotate(2, x[:, :, 0:h], x[:, :, h:2 * h], table(p, R, ROPE, h, shape), table(p, R, ROPE + h, h, shape),
                       shape).then_inc(S["dqk_roped"], 1)

            def kpT_copy(t, p, R):
                ve_.wait_ge(S["kpT_made"], NC + t + 1)
                need(ve_, late_s, max(0, NC + t) * KEY_ST if isinstance(t, int) and t < 0 else NC * KEY_ST + t * LATE_ST)
                v.tensor_copy(kpT[:, 0:R], ps[0:ROPE, 5, 0:R]).then_inc(S["kpT_copied"], 1)

            def dT_copy(t, p, R, first):
                ve_.wait_ge(S["dT_made"], NC + t + 1)
                for half in range(first, 2):
                    ins = v.tensor_copy(dT[:, half, :, 0:R],
                                        ps[:, (7, 4)[half], :].rearrange("p (k r) -> p k r", r=P)[:, :, 0:R])
                ins.then_inc(S["dT_copied"], 1)

            def kn_copy(t, p, R):
                ve_.wait_ge(S["kn_made"], NC + t + 1)
                v.tensor_copy(knT[:, :, 0:R], ps[:, 4, :].rearrange("p (k r) -> p k r", r=P)[:, :, 0:R]).then_inc(S["kn_copied"], 1)

            def q_rope(t, p):
                R, h = rows_of(t), ROPE // 2
                ve_.wait_ge(S["q_copied"], t + 1)
                shape = [R, HM, h]
                rotate(1, qs[0:R, :, NOPE:NOPE + h], qs[0:R, :, NOPE + h:QD],
                       table(p, R, 0, h, shape), table(p, R, h, h, shape), shape).then_inc(S["q_roped"], 1)

            def rest_of_w(c):
                c0, n = ZC[c]
                ve_.wait_ge(S["w_hi"], c + 1)
                v.tensor_tensor(w_inl[:, :, c0:c0 + n].bitcast(F32R), w_inr[:, :, c0:c0 + n], w_in[:, :, c0:c0 + n],
                                ALU.subtract).then_inc(S["w_lo"], 1)

            def rest_of_x(t, p):
                R = rows_of(t)
                ve_.wait_ge(S["xT_copied"], t + 1)
                v.tensor_tensor(xTl[p][:, :, 0:R].bitcast(F32R), ps[:, 4:6, :].rearrange("p b (k r) -> p (b k) r", r=P)[:, :, 0:R],
                                xT[p][:, :, 0:R], ALU.subtract).then_inc(S["xTl_made"], 1)

            def body1(t, p):
                cur, prev = is_tile(t, NT), is_tile(t - 1, NT)
                q, R1 = 1 - p, rows_of(t - 1)
                if cur:
                    norms(t, p)
                    if isinstance(t, int) and t == 0:
                        rest_of_w(3)
                    kr_rope(t, p)
                    if isinstance(t, int) and t == 0:
                        rest_of_w(4)
                if prev:
                    kpT_copy(t - 1, q, R1)
                    dT_copy(t - 1, q, R1, 0)
                    q_rope(t - 1, q)
                    kn_copy(t - 1, q, R1)
                if is_tile(t + 1, NT):
                    rest_of_x(t + 1, q)
                if cur:
                    dqk_rope(t, p)

            v.memset(pad_rows[:], PAD).then_inc(S["pads_set"], 1)
            rest_of_x(0, 0)
            for c in range(NC):
                kpT_copy(c - NC, c, P)
                dT_copy(c - NC, c, P, 1)
                if c > 0:
                    rest_of_w(0)
                kn_copy(c - NC, c, P)
            rest_of_w(1)
            rest_of_w(2)
            ve_.wait_ge(S["rope_in"], 32)
            for t in range(3):
                body1(t, t % 2)
                if t == 0:
                    ve_.wait_ge(S["lam_in"], 64)
                    ch.inc(v.tensor_tensor(lam4[:, 0, :], lam4[:, 0, :], lam4[:, 1, :], ALU.mult))
                    ch(v.tensor_tensor(lam4[:, 2, :], lam4[:, 2, :], lam4[:, 3, :], ALU.mult))
                    v.tensor_reduce(lams[:], lam4[:, 0::2, :], AX.X, ALU.add).then_inc(S["lam_prod"], 1)
                if t == 2:
                    ve_.wait_ge(S["lam_exp"], 1)
                    ch(v.tensor_scalar(neglam[:], lame[:, 1:2], -LAM_INIT, None, ALU.add))
                    ch(v.tensor_tensor(neglam[:], neglam[:], lame[:, 0:1], ALU.subtract))
            with ve_.Fori(0, 2) as i:
                ch.enter(i, 30)
                body1(3 + 2 * i, 1)
                body1(4 + 2 * i, 0)
            ch.leave(2)
            body1(7, 1)
            body1(8, 0)
            body1(9, 1)

            def maxima(a, maps):
                for m in maps:
                    pair = m if a.diff else a.p
                    ve_.wait_ge(S["s_made"], a.s + m + 1)
                    sc = ps[0:a.rows, 2 * pair:2 * pair + 2, :].rearrange("p b c -> p (b c)")
                    if a.i < NT:
                        ch(v.memset(sc[0:64, a.keys - 64:a.keys], NEG))
                    v.tensor_reduce(nmax[pair][0:a.rows, :], sc[:, 0:a.keys], AX.X, ALU.max, negate=True).then_inc(S["max_done"], 1)

            def pT_copy(a):
                w = a.blocks - 4
                ve_.wait_ge(S["t_hi"], a.bigs + 1)
                ve_.wait_ge(S["o_made"], a.u + 1)
                v.tensor_copy(pT[a.p][:, 4:4 + w, :], ps[:, 5, 0:w * P].rearrange("p (k r) -> p k r", r=P)).then_inc(S["pT_hi"], 1)

            def mix(a):
                R, n = a.rows, a.keys
                ve_.wait_ge(S["exp_done"], a.s + 2)
                ch(v.reciprocal(rsum[a.p][0:R, 1:2], psums[a.p6][1][0:R, :]))
                ch(v.scalar_tensor_tensor(out=mixc[a.p][0:R, :], in0=psums[a.p6][0][0:R, :], scalar=rsum[a.p][0:R, 1:2],
                                          in1=neglam[0:R, :], op0=ALU.mult, op1=ALU.mult))
                v.scalar_tensor_tensor(out=pr[a.p][0][0:R, 0:n], in0=pr[a.p][1][0:R, 0:n], scalar=mixc[a.p][0:R, :],
                                       in1=pr[a.p][0][0:R, 0:n], op0=ALU.mult, op1=ALU.add).then_inc(S["mix_done"], 1)

            def o_copy(a):
                V = VD if a.diff else VM
                col = HM * VM + (2 * a.j + a.hp) * VD if a.diff else (2 * a.j + a.hp) * VM
                ve_.wait_ge(S["exp_done"], a.s + a.maps)
                ch(v.reciprocal(rsum[a.p][0:a.rows, 0:1], psums[a.p6][0][0:a.rows, :]))
                ve_.wait_ge(S["o_made"], 2 + a.u + 1)
                v.tensor_scalar(merged[0:a.rows, a.i, bass.ds(col, V)], ps[0:a.rows, 6 + a.p, 0:V],
                                rsum[a.p][0:a.rows, 0:1], None, ALU.mult).then_inc(S["o_done"], 1)

            def step2(diff, j, k):
                a, b, c, two, one = (Tile(diff, j, k + n) for n in range(5))
                if b.exists and b.big and not b.diff:
                    pT_copy(b)
                if one.exists and not one.diff:
                    maxima(one, (0,))
                if two.exists and two.diff:
                    maxima(two, (0,))
                if b.exists and b.big and b.diff:
                    pT_copy(b)
                if c.exists and c.diff:
                    mix(c)
                if a.exists:
                    o_copy(a)
                if two.exists and two.diff:
                    maxima(two, (1,))

            ve_.sem_inc(S["o_done"], 2)
            for k in range(-4, 0):
                step2(False, 0, k)
            for sm, n in ((late_s, NC * KEY_ST + (NT + 1) * LATE_ST), (zv_s, 16 * (NT + 1)), (st_s[1], EARLY_ST * 4),
                          (st_s[0], EARLY_ST * 5)):
                ve_.wait_ge(sm, n)
            v.memset(merged[DEC:P, NT, :], 0.0)
            with ve_.Fori(0, HM // 2 - 1) as j:
                ch.enter(j, PAIR - 2 + PAIR)
                for k in range(PAIR):
                    step2(False, j, k)
            ch.leave(HM // 2 - 1)
            for k in range(PAIR):
                step2(False, HM // 2 - 1, k)
            for j in range(HD // 2):
                for k in range(PAIR):
                    step2(True, j, k)

            def rest_of_mT(t, p):
                ve_.wait_ge(S["mT_copied"], t + 1)
                src = ps[:, 4:6, :].rearrange("p b (k r) -> p b k r", r=P)
                v.tensor_tensor(mTl[p][:, 0:4, 0:P].bitcast(F32R), src[:, 0, :, 0:P], mT[p][:, 0:4, 0:P], ALU.subtract)
                v.scalar_tensor_tensor(out=mTl[p][:, 4:8, 0:P].bitcast(F32R), in0=src[:, 1, :, 0:P], scalar=subln[:, 1:2],
                                       in1=mT[p][:, 4:8, 0:P], op0=ALU.mult, op1=ALU.subtract).then_inc(S["mTl_made"], 1)

            def stage(t, p):
                need(ve_, S["mT_made"], t)
                mr = merged[0:P, bass.ds(t, 1), :].rearrange("p a d -> p (a d)")
                v.tensor_copy(mst[0:P, 0:512], mr[:, 0:512])
                ve_.wait_ge(S["hrs_done"], t + 1)
                v.tensor_tensor(mst[0:P, 512:1024].rearrange("p (h v) -> p h v", v=VD),
                                mr[:, 512:1024].rearrange("p (h v) -> p h v", v=VD),
                                m4s[p][2][0:P, :].unsqueeze(2).broadcast_to([P, HD, VD]), ALU.mult).then_inc(S["md_done"], 1)

            def layer1(t, p):
                R = rows_of(t)
                ve_.wait_ge(S["op_made"], t + 1)
                ve_.wait_ge(xr_s[p], 16 * (t // 2 + 1))
                need(ve_, S["h_done"], t - 1)
                for half in range(2):
                    c = slice(512 * half, 512 * (half + 1))
                    ins = v.scalar_tensor_tensor(out=r1[p][0:R, c], in0=xr[p][0:R, c], scalar=ALPHA, in1=ps[0:R, 2 * p + half, :],
                                                 op0=ALU.mult, op1=ALU.add)
                ins.then_inc(S["res_done"], 1)
                ve_.wait_ge(S["res_done"], t + 1)
                for half in range(2):
                    ch.inc(v.bn_stats(bst[p][0:R, half, :], r1[p][0:R, 512 * half:512 * (half + 1)]))
                ch.wait()
                settle(ve_)
                v.bn_aggr(mv[p][0:R, :], bst[p][0:R].rearrange("p a b -> p (a b)")).then_inc(S["ln_stat"], 1)
                ve_.wait_ge(S["ln_rstd"], t + 1)
                ch(v.tensor_scalar(r1[p][0:R, :], r1[p][0:R, :], mv[p][0:R, 0:1], rst[p][0:R, :], ALU.subtract, ALU.mult))
                if isinstance(t, int) and t == 0:
                    ve_.wait_ge(S["ph3_in"], 16 * 6)
                v.tensor_tensor(r1[p][0:R, :], r1[p][0:R, :], g1b[0:R, :], ALU.mult).then_inc(S["ln_mul"], 1)

            def first_of(vals, n, w, m, oh, R):
                ch(v.tensor_reduce(m, vals, AX.X, ALU.max))
                ch(v.scalar_tensor_tensor(out=w, in0=vals, scalar=m, in1=const[0:R, C_DESC:C_DESC + n], op0=ALU.is_ge, op1=ALU.mult))
                ch(v.tensor_reduce(top1[0:R, 7:8], w, AX.X, ALU.max))
                ch(v.tensor_scalar(oh, w, top1[0:R, 7:8], None, ALU.is_equal))

            def choose(t, p):
                R = rows_of(t)
                ve_.wait_ge(S["lg_made"], t + 1)
                ch(v.tensor_tensor(lg[0:R, :], ps[0:R, 6, 0:NG + NE], b_r[0:R, :], ALU.add))
                first_of(lg[0:R, 0:NG], NG, wgt[0:R, 0:NG], top1[0:R, 0:1], ohg[0:R, :], R)
                g3 = ohg[0:R, :].unsqueeze(2).broadcast_to([R, NG, EPG])
                ch(v.tensor_tensor(emul[0:R], lg[0:R, NG:NG + NE].rearrange("p (g j) -> p g j", j=EPG), g3, ALU.mult))
                ch(v.tensor_reduce(ein8[0:R, 0, :], emul[0:R].rearrange("p g j -> p j g"), AX.X, ALU.add))
                first_of(ein8[0:R, 0, :], EPG, wgt[0:R, :], top1[0:R, 1:2], ohe[0:R, 0, :], R)
                ch(v.scalar_tensor_tensor(out=ein8[0:R, 1, :], in0=ohe[0:R, 0, :], scalar=NEG, in1=ein8[0:R, 0, :], op0=ALU.mult, op1=ALU.add))
                first_of(ein8[0:R, 1, :], EPG, wgt[0:R, :], top1[0:R, 2:3], ohe[0:R, 1, :], R)
                ch.inc(v.tensor_scalar(shifted[p][0:R, 0:NG], lg[0:R, 0:NG], top1[0:R, 0:1], None, ALU.subtract))
                v.tensor_tensor(shifted[p][0:R, 4:5], top1[0:R, 2:3], top1[0:R, 1:2], ALU.subtract).then_inc(S["shift_done"], 1)
                for k in range(2):
                    ch.inc(v.tensor_tensor(oh32[p][0:R, k, :].rearrange("p (g j) -> p g j", j=EPG), g3,
                                           ohe[0:R, k, :].unsqueeze(1).broadcast_to([R, NG, EPG]), ALU.mult))
                ch.wait()
                v.tensor_tensor(picks[p][0:R, :], oh32[p][0:R, 0, :], oh32[p][0:R, 1, :], ALU.add).then_inc(S["picks_done"], 1)

            def list_rows(t, p):
                R = rows_of(t)
                ve_.wait_ge(S["exp3_done"], t + 1)
                ch(v.tensor_reduce(gates[p][0:R, 2:3], exped[p][0:R, 0:NG], AX.X, ALU.add))
                ch(v.scalar_tensor_tensor(out=gates[p][0:R, 3:4], in0=exped[p][0:R, 4:5], scalar=1.0, in1=gates[p][0:R, 2:3],
                                          op0=ALU.add, op1=ALU.mult))
                ch(v.reciprocal(gates[p][0:R, 0:1], gates[p][0:R, 3:4]))
                ch(v.tensor_tensor(gates[p][0:R, 1:2], exped[p][0:R, 4:5], gates[p][0:R, 0:1], ALU.mult))
                ve_.wait_ge(S["ent_free"], t + 1)
                tok = const[0:R, bass.ds(C_TOK + t, 1)]
                for k in range(2):
                    ch.inc(v.tensor_copy(entry[p][0:R, k, 0:1], tok))
                    ch.inc(v.tensor_scalar(entry[p][0:R, k, 1:2], tok, float(k * TOK), None, ALU.add))
                    ch.inc(v.tensor_copy(entry[p][0:R, k, 2:3].bitcast(F32), gates[p][0:R, k:k + 1]))
                ve_.wait_ge(S["pre_made"], t + 1)
                ch(v.scalar_tensor_tensor(out=where[0:R, :], in0=ps[0:R, 7, 0:NE], scalar=float(NE), in1=const[0:R, C_IOTA:C_IOTA + NE],
                                          op0=ALU.mult, op1=ALU.add))
                ch(v.tensor_tensor(where2[0:R], oh32[p][0:R], where[0:R, :].unsqueeze(1).broadcast_to([R, 2, NE]), ALU.mult))
                ch(v.tensor_reduce(rowf[0:R, :], where2[0:R], AX.X, ALU.add))
                ch(v.tensor_copy(row[p][0:R].rearrange("p a b -> p (a b)"), rowf[0:R, :]))
                if R < P:
                    ch.inc(v.tensor_copy(before[1 - p][R:P, :], before[p][R:P, :]))
                v.tensor_tensor(before[1 - p][0:R, :], before[p][0:R, :], picks[p][0:R, :], ALU.add).then_inc(S["rows_done"], 1)

            def body3(t, p):
                if is_tile(t, NT):
                    layer1(t, p)
                if is_tile(t + 2, NT):
                    rest_of_mT(t + 2, p)
                if is_tile(t - 2, NT):
                    list_rows(t - 2, p)
                if is_tile(t - 1, NT):
                    choose(t - 1, 1 - p)
                if is_tile(t + 3, NT):
                    stage(t + 3, 1 - p)

            for k in range(2):
                ch.inc(v.memset(before[k][:], 0.0))
                ch.inc(v.memset(entry[k][:], 0))
            ch.wait()
            for t in range(-3, 2):
                body3(t, t % 2)
            with ve_.Fori(0, 2) as i:
                ch.enter(i, 72)
                body3(2 + 2 * i, 0)
                body3(3 + 2 * i, 1)
            ch.leave(2)
            for t in range(6, NT + 3):
                body3(t, t % 2)
            ve_.wait_ge(S["cnt_made"], 1)
            ch(v.tensor_reduce(cntm[:], ps[:, 6, 0:NE], AX.X, ALU.max))
            ch(v.tensor_scalar(over[:], const[:, C_THR:C_THR + 8], cntm[:], None, ALU.is_lt))
            ch(v.tensor_reduce(nover[:], over[:], AX.X, ALU.add))
            v.tensor_copy(more[:], nover[:]).then_inc(S["swp_done"], 1)

            def rows_copy(e, s):
                p = s % 2
                ve_.wait_ge(S["hgT_made"], 2 * e + 2)
                need(ve_, S["gu_made"], e - 1)
                ve_.wait_ge(S["hgT_copied"], 2 * e + 1)
                v.tensor_copy(hgT[p][:, 4:8, :], ps[:, 3, :].rearrange("p (k r) -> p k r", r=P)).then_inc(S["hgT_copied"], 1)

            def hidden(e, s):
                p = s % 2
                ve_.wait_ge(S["silu_done"], e + 1)
                need(ve_, S["hidT_made"], e - 1)
                v.tensor_tensor(hid[p][:], sil[p][:], ps[:, p, FE:2 * FE], ALU.mult).then_inc(S["hid_done"], 1)

            def hidT_copy(e, s):
                p = s % 2
                ve_.wait_ge(S["hidT_made"], e + 1)
                need(ve_, S["dn_made"], e - 1)
                v.tensor_copy(hidT[p][:].rearrange("p k r -> p (k r)"), ps[:, 4, 0:2 * P]).then_inc(S["hidT_copied"], 1)

            def y_copy(e, s):
                p = s % 2
                ve_.wait_ge(S["dn_made"], e + 1)
                need(ve_, y_s[p], (e // 2) * 16)
                v.tensor_scalar(y[p][:, 512:1024], ps[:, 6, :], tab[s][:, 2:3].bitcast(F32), None, ALU.mult).then_inc(S["y_hi"], 1)

            def body4(g, first):
                for s in range(TABS):
                    e = g * TABS + s
                    rows_copy(e, s)
                    if not first or s >= 2:
                        y_copy(e - 2, (s - 2) % TABS)
                    if not first or s >= 1:
                        hidT_copy(e - 1, (s - 1) % TABS)
                    hidden(e, s)

            ve_.wait_ge(S["swp_done"], 1)
            n = ve_.value_load(more[0:1, 0:1], min_val=0, max_val=SWEEPS - 1) + 1
            for k in range(2):
                ins = v.memset(hg[k][:], 0.0)
            ins.then_inc(S["hg_zero"], 1)
            body4(0, True)
            with ve_.Fori(1, n * GROUPS) as g:
                body4(g, False)
            E = n * NE
            y_copy(E - 2, TABS - 2)
            hidT_copy(E - 1, TABS - 1)
            y_copy(E - 1, TABS - 1)

            ve_.wait_ge(S["ln2_in"], 32)
            def fin_stats(t):
                R = rows_of(t)
                ve_.wait_ge(S["sum_made"], t + 1)
                b = 2 * (t % 4)
                v.scalar_tensor_tensor(out=yy[t][0:R, 0, :], in0=merged[0:R, t, :], scalar=ALPHA,
                                       in1=ps[0:R, b:b + 2, :].rearrange("p b c -> p (b c)"),
                                       op0=ALU.mult, op1=ALU.add).then_inc(S["sum_read"], 1)
                ve_.wait_ge(S["sum_read"], t + 1)
                for half in range(2):
                    ch.inc(v.bn_stats(fst[t][0:R, half, :], yy[t][0:R, 0, 512 * half:512 * (half + 1)]))
                ch.wait()
                v.bn_aggr(fmv[t][0:R, :], fst[t][0:R].rearrange("p a b -> p (a b)")).then_inc(S["fstat"], 1)

            def fin_mul(t):
                R = rows_of(t)
                ve_.wait_ge(S["fnorm"], t + 1)
                v.tensor_tensor(yy[t][0:R, 1, :], yy[t][0:R, 1, :], g2b[0:R, :], ALU.mult).then_inc(S["fmul"], 1)

            for t in range(NT + 2):
                if t <= NT:
                    fin_stats(t)
                if t >= 1:
                    fin_mul(t - 1)

        @block.gpsimd
        def _(po):
            g = nc.gpsimd
            ch = Chain(po, S["ch_pool"])

            def rsqrt(dst, src, tmp, R, n, inv, eps):
                settle(po)
                ch(g.tensor_scalar(tmp, src, inv, eps, ALU.mult, ALU.add))
                return g.tensor_tensor(dst, tmp, const[0:R, C_HALF:C_HALF + n], ALU.pow)

            def rms(t, p):
                R = rows_of(t)
                po.wait_ge(S["sq_done"], t + 1)
                need(po, S["norm_done"], t - 1)
                rsqrt(rq[p][0:R, :], ss[p][0:R, :], ms[p][0:R, :], R, 2, 1.0 / QR, EPS_RMS).then_inc(S["rms_done"], 1)

            po.wait_ge(S["const_in"], 16)
            for t in range(3):
                rms(t, t % 2)
            with po.Fori(0, 2) as i:
                ch.enter(i, 2)
                rms(3 + 2 * i, 1)
                rms(4 + 2 * i, 0)
            ch.leave(2)
            rms(7, 1)
            rms(8, 0)

            def head_rms(t, p):
                po.wait_ge(S["hsq_done"], t + 1)
                need(po, S["md_done"], t - 1)
                rsqrt(m4s[p][2][0:P, :], m4s[p][0][0:P, :], m4s[p][1][0:P, :], P, HD, 1.0 / VD, EPS_RMS).then_inc(S["hrs_done"], 1)

            def layer1(t, p):
                R = rows_of(t)
                po.wait_ge(S["ln_stat"], t + 1)
                rsqrt(rst[p][0:R, :], mv[p][0:R, 1:2], ve[p][0:R, :], R, 1, 1.0, EPS_LN).then_inc(S["ln_rstd"], 1)
                po.wait_ge(S["ln_mul"], t + 1)
                g.tensor_tensor(xr[p][0:R, :], r1[p][0:R, :], b1b[0:R, :], ALU.add).then_inc(S["h_done"], 1)

            def scatter_rows(t, p):
                R = rows_of(t)
                po.wait_ge(S["rows_done"], t + 1)
                if isinstance(t, int) and t == 0:
                    po.wait_ge(S["pads_out"], 16 * SWEEPS)
                settle(po)
                for k in range(2):
                    g.indirect_dma_start(list_d.rearrange("p e w -> (p e) w"),
                                         bass.IndirectOffsetOnAxis(ap=row[p][0:R, k, 0:1], axis=0),
                                         entry[p][0:R, k, :], None, bounds_check=SWEEPS * P * NE - 1,
                                         oob_is_err=False).then_inc(ent_s[p], 16)
                po.wait_ge(ent_s[p], 32 * (t // 2 + 1))
                po.sem_inc(S["ent_free"], 1)

            def body3(t, p):
                if is_tile(t + 3, NT):
                    head_rms(t + 3, 1 - p)
                if is_tile(t, NT):
                    layer1(t, p)
                if is_tile(t - 2, NT):
                    scatter_rows(t - 2, p)

            po.wait_ge(S["wo_in"], 16)
            for k in range(KD):
                g.tensor_copy(w_o[:, k, :].bitcast(F32R), w_raw[:, k, :]).then_inc(S["wo_hi"], 1)
                po.wait_ge(S["wo_hi"], k + 1)
                g.tensor_tensor(w_ol[:, k, :].bitcast(F32R), w_raw[:, k, :], w_o[:, k, :], ALU.subtract).then_inc(S["wo_lo"], 1)

            po.wait_ge(S["o_done"], 2 + 9 * (HM + HD))
            po.sem_inc(S["ent_free"], 2)
            for t in range(-3, 2):
                body3(t, t % 2)
            with po.Fori(0, 2) as i:
                ch.enter(i, 4)
                body3(2 + 2 * i, 0)
                body3(3 + 2 * i, 1)
            ch.leave(2)
            for t in range(6, NT + 3):
                body3(t, t % 2)

            def gather(e, s, lots):
                p = s % 2
                po.wait_ge(tab_s[s], lots * 16)
                need(po, S["hgT_made"], 2 * (e - 1))
                settle(po)
                g.indirect_dma_start(hg[p][:], None, h_d, bass.IndirectOffsetOnAxis(ap=tab[s][:, 0:1], axis=0),
                                     bounds_check=TOK - 1, oob_is_err=False).then_inc(hg_s[p], 16)

            def scatter(e, s):
                p = s % 2
                po.wait_ge(S["y_lo"], e + 1)
                po.wait_ge(S["y_hi"], e + 1)
                settle(po)
                g.indirect_dma_start(pair_d, bass.IndirectOffsetOnAxis(ap=tab[s][:, 1:2], axis=0), y[p][:], None,
                                     bounds_check=2 * TOK - 1, oob_is_err=False).then_inc(y_s[p], 16)

            po.wait_ge(S["hg_zero"], 1)
            po.wait_ge(h_st[0], 16 * 5)
            po.wait_ge(h_st[1], 16 * 4)
            po.wait_ge(S["swp_done"], 1)
            n = po.value_load(more[0:1, 0:1], min_val=0, max_val=SWEEPS - 1) + 1

            def body4(gr, first):
                for s in range(TABS):
                    e = gr * TABS + s
                    gather(e, s, gr + 1)
                    if not first or s >= 3:
                        scatter(e - 3, (s - 3) % TABS)

            body4(0, True)
            with po.Fori(1, n * GROUPS) as gr:
                body4(gr, False)
            for k in (3, 2, 1):
                scatter(n * NE - k, TABS - k)

            po.wait_ge(S["ln2_in"], 32)
            for t in range(NT + 2):
                if t <= NT:
                    R = rows_of(t)
                    po.wait_ge(S["fstat"], t + 1)
                    g_ = rsqrt(frs[t][0:R, :], fmv[t][0:R, 1:2], fve[t][0:R, :], R, 1, 1.0, EPS_LN)
                    g_.then_inc(S["frstd"], 1)
                    po.wait_ge(S["frstd"], 2 * t + 1)
                    ch(g.tensor_tensor(fve[t][0:R, :], fmv[t][0:R, 0:1], frs[t][0:R, :], ALU.mult))
                    g.tensor_scalar(fve[t][0:R, :], fve[t][0:R, :], -1.0, None, ALU.mult).then_inc(S["frstd"], 1)
                if t >= 1:
                    R, u = rows_of(t - 1), t - 1
                    po.wait_ge(S["fmul"], t)
                    g.tensor_tensor(yy[u][0:R, 0, :], yy[u][0:R, 1, :], b2b[0:R, :], ALU.add).then_inc(S["fin_done"], 1)




def const_table():
    c = np.zeros((P, C_N), np.float32)
    c[:, C_ID:C_ID + P] = np.eye(P)
    c[:, C_TRI:C_TRI + P] = np.triu(np.ones((P, P)), 1)
    c[:, C_ONE:C_ONE + P] = 1
    c[:, C_IOTA:C_IOTA + NE] = np.arange(NE)
    c[:, C_DESC:C_DESC + 8] = 8 - np.arange(8)
    c[:, C_TOK:C_TOK + 9] = np.arange(P)[:, None] + P * np.arange(9)
    c[:, C_HALF:C_HALF + 9] = -0.5
    c[:, C_THR:C_THR + 8] = P * (1 + np.arange(8))
    return c


def rope_table():
    pos = np.concatenate([np.arange(SEQ), PAST + np.arange(DEC)]).astype(np.float32)
    cols = []
    for r in (ROPE, ROT):
        inv = np.float32(500000.0) ** (-np.arange(0, r, 2, dtype=np.float32) / np.float32(r))
        ang = pos[:, None] * inv.astype(np.float32)
        cols += [np.cos(ang), np.sin(ang)]
    return np.concatenate(cols, 1).astype(np.float32)


_OUTS = [("y_prompt", (1, SEQ, D)), ("y_sample", (1, DEC, D)),
         ("new_ckv_p", (1, 1, SEQ, KVR)), ("new_kpe_p", (1, 1, SEQ, ROPE)),
         ("new_dk_p", (1, 1, SEQ, HD, 2 * DD)), ("new_dv_p", (1, 1, SEQ, HD, VD)),
         ("new_ckv_s", (1, 1, DEC, KVR)), ("new_kpe_s", (1, 1, DEC, ROPE)),
         ("new_dk_s", (1, 1, DEC, HD, 2 * DD)), ("new_dv_s", (1, 1, DEC, HD, VD))]


def kernel(**inputs):
    import numpy as _np
    import concourse.bacc as _bacc
    from concourse import mybir as _mybir
    from concourse.bass_utils import run_bass_kernel_spmd as _run

    nc = _bacc.Bacc("TRN2", target_bir_lowering=False, num_devices=1)
    arrays, args, outs = {}, {}, {}
    given = dict(inputs)
    given["const_table"] = const_table()
    given["rope_table"] = rope_table()
    for name, value in given.items():
        v = _np.ascontiguousarray(value)
        arrays[f"in_{name}"] = v
        args[name] = nc.dram_tensor(f"in_{name}", v.shape, _mybir.dt.from_np(v.dtype), kind="ExternalInput").ap()
    for name, shape in _OUTS:
        outs[name] = nc.dram_tensor(f"out_{name}", shape, F32, kind="ExternalOutput").ap()
    build(nc, args, outs)
    r = _run(nc, [arrays], core_ids=[0])
    return tuple(r.results[0][f"out_{name}"] for name, _ in _OUTS)
```
